# Optimizing a Trainium2 kernel written in Bass

```python
import jax, jax.numpy as jnp
from jax import lax
import numpy as np

D_MODEL = 1024
BATCH = 1
SEQ = 512
DEPTH = 2

MEM_LEN = 256
EPS = 1e-6
BLOCK = 128
CONV_CH = D_MODEL // 2
CONV_WIDTH = 31
SB_HEADS = 8
SB_HEAD_DIM = (D_MODEL // 2) // SB_HEADS
SB_DIM = SB_HEADS * SB_HEAD_DIM
AB_IN = 2 * CONV_CH + 3 * SB_DIM
GM_DIM = D_MODEL
GM_GROUPS = 8
GM_GROUP_DIM = GM_DIM // GM_GROUPS
GM_CHUNK = 128
XA_HEADS = 4
XA_HEAD_DIM = D_MODEL // XA_HEADS
N_GROUPS = 4
EXPERTS_PER_GROUP = 4
N_EXPERTS = N_GROUPS * EXPERTS_PER_GROUP
TOP_K_IN_GROUP = 2
D_EXPERT = D_MODEL // 4
N_EVEN = (DEPTH + 1) // 2
N_ODD = DEPTH // 2

kernel_name = 'hybrid_conv_stickbreak_gmlp_hmoe'

def rmsnorm(x, g):
    xf = x.astype(jnp.float32)
    y = xf * lax.rsqrt(jnp.mean(xf * xf, axis=-1, keepdims=True) + EPS)
    return (y * g.astype(jnp.float32)).astype(x.dtype)

def layernorm(x, g, b):
    xf = x.astype(jnp.float32)
    mu = jnp.mean(xf, axis=-1, keepdims=True)
    var = jnp.mean(jnp.square(xf - mu), axis=-1, keepdims=True)
    y = (xf - mu) * lax.rsqrt(var + EPS) * g.astype(jnp.float32) + b.astype(jnp.float32)
    return y.astype(x.dtype)

def conformer_conv(a, gate, conv_w, conv_b, ln_g, ln_b):
    h = a * jax.nn.sigmoid(gate)
    h = lax.conv_general_dilated(h, conv_w[:, None, :].astype(h.dtype), window_strides=(1,),
                                 padding=[(CONV_WIDTH - 1, 0)],
                                 dimension_numbers=('NWC', 'WIO', 'NWC'),
                                 feature_group_count=CONV_CH) + conv_b
    h = layernorm(h, ln_g, ln_b)
    return jax.nn.silu(h)

def stick_breaking_attention(q, k, v):
    bsz, s_len, n_h, dh = q.shape
    nb = s_len // BLOCK
    scale = dh ** -0.5
    qb = q.reshape(bsz, nb, BLOCK, n_h, dh).transpose(1, 0, 3, 2, 4)
    kt = k.transpose(0, 2, 1, 3)
    vt = v.transpose(0, 2, 1, 3)
    kpos = jnp.arange(s_len)

    def one_block(args):
        q_blk, start = args
        z = jnp.einsum('bhqd,bhkd->bhqk', q_blk, kt, preferred_element_type=jnp.float32) * scale
        qpos = start + jnp.arange(BLOCK)
        mask = kpos[None, :] < qpos[:, None]
        log_stay = jnp.where(mask, jax.nn.log_sigmoid(-z), 0.0)
        after = lax.cumsum(log_stay, axis=3, reverse=True) - log_stay
        log_w = jnp.where(mask, jax.nn.log_sigmoid(z) + after, -jnp.inf)
        w = jnp.exp(log_w)
        return jnp.einsum('bhqk,bhkd->bhqd', w.astype(vt.dtype), vt)

    starts = jnp.arange(nb, dtype=jnp.int32) * BLOCK
    o = lax.map(one_block, (qb, starts))
    return o.transpose(1, 0, 3, 2, 4).reshape(bsz, s_len, n_h * dh)

def mixer_ab(xn, w_in, conv_w, conv_b, ln_g, ln_b, w_out):
    bsz, s_len, _ = xn.shape
    p = xn @ w_in
    a, g, q, k, v = jnp.split(p, [CONV_CH, 2 * CONV_CH, 2 * CONV_CH + SB_DIM,
                                  2 * CONV_CH + 2 * SB_DIM], axis=-1)
    conv_out = conformer_conv(a, g, conv_w, conv_b, ln_g, ln_b)
    heads = lambda t: t.reshape(bsz, s_len, SB_HEADS, SB_HEAD_DIM)
    sb_out = stick_breaking_attention(heads(q), heads(k), heads(v))
    return jnp.concatenate([conv_out, sb_out.astype(conv_out.dtype)], axis=-1) @ w_out

def mixer_c(xn, w_in, v_g, v_b, ws, bs, w_out):
    bsz, s_len, _ = xn.shape
    p = jax.nn.gelu(xn @ w_in, approximate=False)
    u, v = jnp.split(p, 2, axis=-1)
    v = layernorm(v, v_g, v_b)
    nc = s_len // GM_CHUNK
    v = v.reshape(bsz, nc, GM_CHUNK, GM_GROUPS, GM_GROUP_DIM)
    causal = jnp.tril(jnp.ones((GM_CHUNK, GM_CHUNK), dtype=ws.dtype))
    mixed = jnp.einsum('gts,bcsgd->bctgd', ws * causal[None], v) + bs.T[:, :, None]
    out = u * mixed.reshape(bsz, s_len, GM_DIM)
    return out @ w_out

def cross_attn(xn, memn, wq, wk, wv, wo):
    bsz, s_len, d = xn.shape
    m_len = memn.shape[1]
    q = (xn @ wq).reshape(bsz, s_len, XA_HEADS, XA_HEAD_DIM)
    k = (memn @ wk).reshape(bsz, m_len, XA_HEADS, XA_HEAD_DIM)
    v = (memn @ wv).reshape(bsz, m_len, XA_HEADS, XA_HEAD_DIM)
    s = jnp.einsum('bqhd,bkhd->bhqk', q, k, preferred_element_type=jnp.float32) * (XA_HEAD_DIM ** -0.5)
    pr = jax.nn.softmax(s, axis=-1).astype(v.dtype)
    o = jnp.einsum('bhqk,bkhd->bqhd', pr, v).reshape(bsz, s_len, d)
    return o @ wo

def hier_moe(xn, wg, bg, we, be, w_gate, w_up, w_down):
    bsz, s_len, d = xn.shape
    t = xn.reshape(bsz * s_len, d)
    n_tok = t.shape[0]
    lg = (t @ wg).astype(jnp.float32) + bg.astype(jnp.float32)
    pg = jax.nn.softmax(lg, axis=-1)
    pg_top, g_idx = lax.top_k(pg, 1)
    le = ((t @ we).astype(jnp.float32) + be.astype(jnp.float32)).reshape(n_tok, N_GROUPS, EXPERTS_PER_GROUP)
    idx = jnp.broadcast_to(g_idx[:, :, None], (n_tok, 1, EXPERTS_PER_GROUP))
    le_sel = jnp.take_along_axis(le, idx, axis=1)[:, 0]
    pe = jax.nn.softmax(le_sel, axis=-1)
    w2, i2 = lax.top_k(pe, TOP_K_IN_GROUP)
    w2 = w2 / jnp.sum(w2, axis=-1, keepdims=True) * pg_top
    ids = g_idx * EXPERTS_PER_GROUP + i2
    gates = jnp.sum(jax.nn.one_hot(ids, N_EXPERTS, dtype=jnp.float32) * w2[..., None], axis=1)
    h = jax.nn.silu(jnp.einsum('td,edf->tef', t, w_gate)) * jnp.einsum('td,edf->tef', t, w_up)
    y = jnp.einsum('tef,efd->td', h * gates[:, :, None].astype(h.dtype), w_down)
    return y.reshape(bsz, s_len, d)

def setup_inputs(seed: int = 0) -> dict:
    key = jax.random.key(seed)
    ks = iter(jax.random.split(key, 40))
    nrm = lambda shape, scale: jax.random.normal(next(ks), shape, jnp.float32) * scale
    gain = lambda shape: 1.0 + nrm(shape, 0.02)
    d = D_MODEL
    return {
        'x': nrm((BATCH, SEQ, d), 1.0),
        'mem': nrm((BATCH, MEM_LEN, d), 1.0),
        'mem_norm_g': gain((d,)),
        'norm_mix': gain((DEPTH, d)),
        'norm_xa': gain((DEPTH, d)),
        'norm_ffn': gain((DEPTH, d)),
        'final_norm_g': gain((d,)),
        'ab_w_in': nrm((N_EVEN, d, AB_IN), d ** -0.5),
        'ab_conv_w': nrm((N_EVEN, CONV_WIDTH, CONV_CH), CONV_WIDTH ** -0.5),
        'ab_conv_b': nrm((N_EVEN, CONV_CH), 0.02),
        'ab_cnorm_g': gain((N_EVEN, CONV_CH)),
        'ab_cnorm_b': nrm((N_EVEN, CONV_CH), 0.02),
        'ab_w_out': nrm((N_EVEN, CONV_CH + SB_DIM, d), (CONV_CH + SB_DIM) ** -0.5),
        'c_w_in': nrm((N_ODD, d, 2 * GM_DIM), d ** -0.5),
        'c_vnorm_g': gain((N_ODD, GM_DIM)),
        'c_vnorm_b': nrm((N_ODD, GM_DIM), 0.02),
        'c_ws': nrm((N_ODD, GM_GROUPS, GM_CHUNK, GM_CHUNK), GM_CHUNK ** -0.5),
        'c_bs': 1.0 + nrm((N_ODD, GM_GROUPS, GM_CHUNK), 0.1),
        'c_w_out': nrm((N_ODD, GM_DIM, d), GM_DIM ** -0.5),
        'xa_wq': nrm((DEPTH, d, d), d ** -0.5),
        'xa_wk': nrm((DEPTH, d, d), d ** -0.5),
        'xa_wv': nrm((DEPTH, d, d), d ** -0.5),
        'xa_wo': nrm((DEPTH, d, d), d ** -0.5),
        'rt_wg': nrm((DEPTH, d, N_GROUPS), d ** -0.5),
        'rt_bg': nrm((DEPTH, N_GROUPS), 0.01),
        'rt_we': nrm((DEPTH, d, N_EXPERTS), d ** -0.5),
        'rt_be': nrm((DEPTH, N_EXPERTS), 0.01),
        'ex_w_gate': nrm((DEPTH, N_EXPERTS, d, D_EXPERT), d ** -0.5),
        'ex_w_up': nrm((DEPTH, N_EXPERTS, d, D_EXPERT), d ** -0.5),
        'ex_w_down': nrm((DEPTH, N_EXPERTS, D_EXPERT, d), D_EXPERT ** -0.5),
    }

def reference(x, mem, mem_norm_g, norm_mix, norm_xa, norm_ffn, final_norm_g,
              ab_w_in, ab_conv_w, ab_conv_b, ab_cnorm_g, ab_cnorm_b, ab_w_out,
              c_w_in, c_vnorm_g, c_vnorm_b, c_ws, c_bs, c_w_out,
              xa_wq, xa_wk, xa_wv, xa_wo,
              rt_wg, rt_bg, rt_we, rt_be,
              ex_w_gate, ex_w_up, ex_w_down):
    memn = rmsnorm(mem, mem_norm_g)
    h = x
    for i in range(DEPTH):
        j = i // 2
        xn = rmsnorm(h, norm_mix[i])
        if i % 2 == 0:
            h = h + mixer_ab(xn, ab_w_in[j], ab_conv_w[j], ab_conv_b[j],
                             ab_cnorm_g[j], ab_cnorm_b[j], ab_w_out[j])
        else:
            h = h + mixer_c(xn, c_w_in[j], c_vnorm_g[j], c_vnorm_b[j],
                            c_ws[j], c_bs[j], c_w_out[j])
        h = h + cross_attn(rmsnorm(h, norm_xa[i]), memn, xa_wq[i], xa_wk[i], xa_wv[i], xa_wo[i])
        h = h + hier_moe(rmsnorm(h, norm_ffn[i]), rt_wg[i], rt_bg[i], rt_we[i], rt_be[i],
                         ex_w_gate[i], ex_w_up[i], ex_w_down[i])
    return rmsnorm(h, final_norm_g)


_drawn_inputs = setup_inputs


def setup_inputs(seed=0):
    import zlib

    import numpy as np

    out = dict(_drawn_inputs(seed))
    spreads = {}
    factors = {'mem_norm_g': 3.699,
     'norm_xa': 6.179,
     'final_norm_g': 7.505,
     'c_vnorm_g': 5.269,
     'c_vnorm_b': 4.728,
     'rt_be': 2.944,
     'rt_bg': 6.589}
    for name, (base, spread) in spreads.items():
        noise = np.random.default_rng([zlib.crc32(name.encode()), seed]).standard_normal(out[name].shape)
        drawn = base * np.exp(spread * noise) if base else spread * noise
        out[name] = __import__('jax').numpy.asarray(drawn.astype(out[name].dtype))
    for name, factor in factors.items():
        out[name] = (out[name] * factor).astype(out[name].dtype)
    return out
```

```python
import concourse.bass as bass
from concourse import mybir
from contextlib import ExitStack


def trunk_program(nc, x, mem, mem_norm_g, norm_mix, norm_xa, norm_ffn, final_norm_g,
                  ab_w_in, ab_conv_w, ab_conv_b, ab_cnorm_g, ab_cnorm_b, ab_w_out,
                  c_w_in, c_vnorm_g, c_vnorm_b, c_ws, c_bs, c_w_out,
                  xa_wq, xa_wk, xa_wv, xa_wo, rt_wg, rt_bg, rt_we, rt_be,
                  ex_w_gate, ex_w_up, ex_w_down, out):
    fp32, fp32r, i32 = mybir.dt.float32, mybir.dt.float32r, mybir.dt.int32
    ALU, ACT, AX = mybir.AluOpType, mybir.ActivationFunctionType, mybir.AxisListType

    P = 128
    _, T, D = x.shape
    M = mem.shape[1]
    EPS = 1e-6
    TT, KD, MT = T // P, D // P, M // P
    BANK = 512
    NL = norm_mix.shape[0]
    TAPS, CH = ab_conv_w.shape[1], ab_conv_w.shape[2]
    CC = CH // P
    PAD = TAPS - 1
    SB_HEADS, SB_DH = 8, 64
    XH = 4
    XD = D // XH
    NG, EPG = rt_wg.shape[2], rt_we.shape[2] // rt_wg.shape[2]
    NE = NG * EPG
    FE = ex_w_gate.shape[3]
    OVERFLOW = (2 * T) // (P + 1)
    NB = NE + OVERFLOW + 1
    GC = 4
    RING, SPLIT = 6, 2
    GM = c_ws.shape[1]
    FAR = 1000.0

    ctx = ExitStack()
    sems, place = {}, {}

    def family(shared, members):
        base = 0
        for name, n in members:
            place[name] = (shared, base)
            base += n

    def sem(name):
        shared = place.get(name, (name, 0))[0]
        if shared not in sems:
            sems[shared] = ctx.enter_context(nc.semaphore(shared))
        return sems[shared]

    def have(name, n):
        return sem(name), n + place.get(name, (name, 0))[1]

    for name, n in (("a_full", KD), ("assigned", 1), ("combined", 2 * TT), ("expert_w_used", 3 * NE),
                    ("hidden", NE), ("hidden_t", NE), ("hidden_t_in_psum", NE), ("hots", 2), ("logits", 1),
                    ("overflow_known", 1), ("r_exp", 2), ("r_args", 2), ("ranks", 1),
                    ("router_consts", 3), ("router_loaded", 64), ("silu", NE), ("table", 1), ("table_ready", 1),
                    ("x_exp", TT * XH), ("x_heads_hi", KD), ("x_heads_in_psum", XH), ("x_heads_lo", KD),
                    ("x_max", XH), ("x_probs", XH), ("x_probs_t", XH), ("x_probs_t_in_psum", XH), ("x_scores", XH),
                    ("xq_ready", 2), ("xs_cleared", 1), ("xs_t_in_psum", NE), ("xs_t_ready", NE), ("y_left", NE),
                    ("y_right", NE), ("kx_ready", 2), ("vx_ready", 2), ("mem_t_in_psum", MT),
                    ("mem_split_hi", KD), ("mem_split_lo", KD), ("h_xa", TT), ("h_ffn", TT), ("h_part_xa", TT),
                    ("h_part_ffn", TT)):
        family(name, [(f"{name}{l}", n) for l in range(NL)])
    for name, slots_of, n in (("gathered", 2, 8 * NE), ("xn_stored", 2, 8 * TT), ("y_stored", 2, 8 * NE),
                              ("y_gathered", 4, 8 * TT)):
        for s in range(slots_of):
            family(f"{name}_{s}", [(f"{name}{l}_{s}", n) for l in range(NL)])
    NORMS = [("mix0", TT), ("mem0", MT), ("xa0", TT), ("ffn0", TT), ("mem1", MT), ("mix1", TT), ("v", 0),
             ("xa1", TT), ("ffn1", TT), ("fin1", TT)]
    family("squares_act", [(f"squares_act_{tag}", n // 2) for tag, n in NORMS])
    family("norm_var", [(f"norm_var_{tag}", 1) for tag, n in NORMS])
    family("norm_root", [(f"norm_root_{tag}", 1) for tag, n in NORMS])
    family("xn", [(f"xn_{tag}", n) for tag, n in NORMS])
    family("xn_t_in_psum", [(f"xn_t_in_psum_{tag}", n) for tag, n in NORMS if tag[:3] != "mem"])
    for part in ("split_hi", "split_lo"):
        family(part, [(f"{part}_{tag}", KD) for tag in ("mix0", "xa0", "mix1", "xa1")])

    BASE = 16512
    K = 1024

    def at(name, shape, dt, offset):
        return nc.alloc_sbuf_tensor_at(name, shape, dt, offset=BASE + int(offset))

    raw = at("raw", [P, RING, GC * BANK], fp32, 0)
    w_hi = at("w_hi", [P, SPLIT, GC, BANK], fp32r, 48 * K)
    w_lo = at("w_lo", [P, SPLIT, GC, BANK], fp32r, 64 * K)
    h = at("h", [P, TT, D], fp32, 80 * K)
    a_hi = at("a_hi", [P, KD, T], fp32r, 96 * K)
    a_lo = at("a_lo", [P, KD, T], fp32r, 112 * K)
    mem_hi = at("mem_hi", [P, KD, M], fp32r, 128 * K)
    mem_lo = at("mem_lo", [P, KD, M], fp32r, 136 * K)
    xn = at("xn", [P, 2, D], fp32, 148 * K)
    mem_tok = at("mem_tok", [P, MT, D], fp32, 180 * K)
    q_t = at("q_t", [P, CC, T], fp32, 148 * K)
    k_t = at("k_t", [P, CC, T], fp32, 156 * K)
    v_s = at("v_s", [P, TT, CH], fp32, 164 * K)
    ZW = 1280
    zbuf = at("zbuf", [P, 2, ZW], fp32, 128 * K)
    sbuf = at("sbuf", [P, 2, ZW], fp32, 138 * K)
    CIN_W = T + PAD
    conv_in = at("conv_in", [P, CC, CIN_W], fp32, 188 * K)
    conv_sq = at("conv_sq", [P, CC, T], fp32, 188 * K)
    conv_acc = at("conv_acc", [P, CC, T], fp32, 196.5 * K)
    conv_rs = at("conv_rs", [P, 2, T], fp32, 148 * K)
    kx = at("kx", [P, KD, M], fp32, 172 * K)
    vx = at("vx", [P, MT, D], fp32, 180 * K)
    xq = at("xq", [P, KD, T], fp32, 148 * K)
    xp = at("xp", [P, 2, TT, M], fp32, 188 * K)
    xpt = at("xpt", [P, 2, MT, T], fp32, 164 * K)
    v_c = at("v_c", [P, TT, D], fp32, 148 * K)
    u_c = at("u_c", [P, KD, T], fp32, 188 * K)
    vg_b = at("vg_b", [P, D], fp32, 164 * K)
    vb_b = at("vb_b", [P, D], fp32, 168 * K)
    ws_in = at("ws_in", [P, GM, P], fp32, 160 * K)
    ws_t = at("ws_t", [P, GM, P], fp32, 144 * K)
    bs_b = at("bs_b", [P, GM, P], fp32, 128 * K)
    a_full = at("a_full", [P, KD, T], fp32, 96 * K)
    xs = at("xs", [P, 2, D], fp32, 112 * K)
    xs_t = at("xs_t", [P, 2, KD, P], fp32, 164 * K)
    y_sb = at("y_sb", [P, 2, D], fp32, 188 * K)
    silu_g = at("silu_g", [P, 2, FE], fp32, 196 * K)
    hid = at("hid", [P, 2, FE], fp32, 198 * K)
    hid_t = at("hid_t", [P, 2, 2, P], fp32, 200 * K)
    y_back = at("y_back", [P, 4, D], fp32, 96 * K)
    over_w = [at(f"over_w{i}", [P, GC * BANK], fp32, o * K) for i, o in enumerate((96, 104, 148))]
    slot_hot = at("slot_hot", [P, 2 * TT, P], fp32, 188 * K)
    before = at("before", [P, P], fp32, 202 * K)
    iota_p = at("iota_p", [P, P], fp32, 202.5 * K)
    rt_w = at("rt_w", [P, KD, NG + NE], fp32, 203 * K)
    rt_b = at("rt_b", [P, NG + NE], fp32, 203 * K + 640)
    rt_off = [144 * K]

    def small(name, shape, dt=fp32):
        n = 1
        for s in shape:
            n *= s
        if rt_off[0] < 148 * K < rt_off[0] + 4 * n:
            rt_off[0] = 156 * K
        assert rt_off[0] + 4 * n <= 160 * K
        t = at(name, [P] + shape, dt, rt_off[0])
        rt_off[0] += (4 * n + 31) // 32 * 32
        return t

    lg = small("lg", [TT, NG + NE])
    r4a, r4b, r4c = (small(f"r4_{c}", [TT, NG]) for c in "abc")
    oh_g, oh_1, oh_2 = (small(n, [TT, NG]) for n in ("oh_g", "oh_1", "oh_2"))
    le = small("le", [TT, EPG])
    r1a, r1b, p_top, gate1, gate2 = (small(n, [TT]) for n in ("r1a", "r1b", "p_top", "gate1", "gate2"))
    e_1, e_2, e_sum, rank, slots = (small(n, [TT, NE]) for n in ("e_1", "e_2", "e_sum", "rank", "slots"))
    e_tmp = small("e_tmp", [TT, NG, EPG])
    count, over, b_hi = (small(n, [NE]) for n in ("count", "over", "b_hi"))
    scan = small("scan", [2, 2 * NE])
    slot_f = small("slot_f", [2 * TT])
    slot_i = small("slot_i", [2 * TT], i32)
    row_i, blk_i = small("row_i", [2 * TT], i32), small("blk_i", [2 * TT], i32)
    row_f, blk_f = small("row_f", [2 * TT]), small("blk_f", [2 * TT])
    blk_hot = small("blk_hot", [2 * TT, NB])
    tok_f, tok_e = small("tok_f", [NB]), small("tok_e", [NB])
    tok_i = small("tok_i", [NB], i32)
    own_cmp = small("own_cmp", [OVERFLOW, NE])
    own_f = small("own_f", [OVERFLOW])
    own_i = small("own_i", [OVERFLOW], i32)
    nov_i = small("nov_i", [1], i32)
    idx_c = small("idx_c", [1], i32)

    c_pool = at("constants", [P, (229344 - BASE - 209408) // 4], fp32, 204.5 * K)
    c_off = [0]

    def const(name, shape):
        n = 1
        for s in shape:
            n *= s
        t = c_pool[:, c_off[0]:c_off[0] + n]
        c_off[0] += n
        assert c_off[0] <= c_pool.shape[1], c_off
        return t if len(shape) == 1 else t.rearrange("p (a b) -> p a b", a=shape[0])

    ident, ones, tri, causal = (const(n, [P]) for n in ("ident", "ones", "tri", "causal"))
    NV = (1 + 3 * NL) * KD + 3 * CC
    vecs = const("vecs", [NV])
    taps = const("taps", [CC, TAPS])
    iota4, iota_b, slot_lo, tok_no = (const(n, s) for n, s in (
        ("iota4", [NG]), ("iota_b", [NB]), ("slot_lo", [NE]), ("tok_no", [TT])))
    n_ss, n_var, n_y, n_t = (const(n, [4]) for n in ("n_ss", "n_var", "n_y", "n_t"))
    x_max, x_sum, x_rec = (const(n, [TT]) for n in ("x_max", "x_sum", "x_rec"))
    v_st, v_mv = at("v_st", [P, TT, 2, 6], fp32, 132 * K), at("v_mv", [P, TT, 2], fp32, 132 * K + 256)
    vec_in = at("vec_in", [P, P], fp32, 188 * K)
    tap_in = at("tap_in", [P, CH], fp32, 189 * K)
    fg_b = at("fg_b", [P, D], fp32, 164 * K)

    MEM_G, MIX_G, XA_G, FFN_G = 0, KD, (1 + NL) * KD, (1 + 2 * NL) * KD
    CONV_B, CN_G, CN_B = (1 + 3 * NL) * KD, (1 + 3 * NL) * KD + CC, (1 + 3 * NL) * KD + 2 * CC

    ps = ctx.enter_context(nc.psum_tensor("ps", [P, 8, BANK], fp32))

    xn_dram = [nc.dram_tensor(f"xn_dram{l}", [T, D], fp32, kind="Internal").ap() for l in range(NL)]
    ys_dram = [nc.dram_tensor(f"ys_dram{l}", [(NB - 1) * P, D], fp32, kind="Internal").ap() for l in range(NL)]

    def slabs(w, cols):
        return [w[:, c:c + BANK] for c in cols]

    dense, first = [], {}

    def plan(name, sl):
        first[name] = len(dense)
        for s in sl:
            for half in range(2):
                dense.append(s[half * GC * P:(half + 1) * GC * P, :].rearrange("(k p) n -> p k n", p=P))

    cols = lambda lo, n: range(lo, lo + n * BANK, BANK)
    plan("sb_gate", slabs(ab_w_in[0], [BANK]))
    plan("sb_a", slabs(ab_w_in[0], [0]))
    plan("sb_q", slabs(ab_w_in[0], [2 * BANK]))
    plan("sb_k", slabs(ab_w_in[0], [3 * BANK]))
    plan("sb_v", slabs(ab_w_in[0], [4 * BANK]))
    plan("kx0", slabs(xa_wk[0], cols(0, 2)))
    plan("vx0", slabs(xa_wv[0], cols(0, 2)))
    plan("mix_out0", slabs(ab_w_out[0], cols(0, 2)))
    plan("xq0", slabs(xa_wq[0], cols(0, 2)))
    plan("xo0", slabs(xa_wo[0], cols(0, 2)))
    plan("kx1", slabs(xa_wk[1], cols(0, 2)))
    moe_at = {0: len(dense)}
    plan("vx1", slabs(xa_wv[1], cols(0, 2)))
    plan("c_v", slabs(c_w_in[0], cols(D, 2)))
    plan("c_u", slabs(c_w_in[0], cols(0, 2)))
    plan("mix_out1", slabs(c_w_out[0], cols(0, 2)))
    plan("xq1", slabs(xa_wq[1], cols(0, 2)))
    plan("xo1", slabs(xa_wo[1], cols(0, 2)))
    moe_at[1] = len(dense)
    ND = len(dense)

    stream, ring_pos, ring_count = [], {}, {}
    slot_total = [0] * RING

    def push(key, inc):
        s = len(stream) % RING
        slot_total[s] += inc
        ring_pos[key], ring_count[key] = s, slot_total[s]
        stream.append(key)

    for d in range(ND + 1):
        for l in range(NL):
            if moe_at[l] == d:
                for e in range(NE):
                    for part in range(3):
                        push(("moe", l, e, part), 32 if part < 2 else 16)
        if d < ND:
            push(("dense", d), 16)

    def ring_free(eng, n):
        if n >= RING:
            key = stream[n - RING]
            if key[0] == "dense":
                eng.wait_ge(*have("w_lo_ready", key[1] + 1))
            else:
                eng.wait_ge(*have(f"expert_w_used{key[1]}", 3 * key[2] + key[3] + 1))

    def expert_views(l, e, part):
        pick = (lambda w: w[l, bass.ds(e, 1)]) if not isinstance(e, int) else (lambda w: w[l, e:e + 1])
        if part < 2:
            rows = slice(part * GC * P, (part + 1) * GC * P)
            return [pick(w)[:, rows, :].rearrange("o (k p) n -> p (o k) n", p=P) for w in (ex_w_gate, ex_w_up)]
        return [pick(ex_w_down).rearrange("o (k p) n -> p (o k) n", p=P)]

    def load_expert(eng, l, e, part, dst, done):
        views = expert_views(l, e, part)
        if part < 2:
            d4 = dst.rearrange("p (k n) -> p k n", k=GC)
            eng.dma_start(d4[:, :, 0:FE], views[0]).then_inc(done, 16)
            eng.dma_start(d4[:, :, FE:2 * FE], views[1]).then_inc(done, 16)
        else:
            eng.dma_start(dst.rearrange("p (k n) -> p k n", k=2), views[0]).then_inc(done, 16)

    def norm_parts(tag):
        if tag.startswith("mem"):
            return MT, (lambda i: mem_tok[:, i, :]), "mem_loaded", MEM_G, mem_hi, mem_lo
        base = {"mix": MIX_G, "xa": XA_G, "ffn": FFN_G, "fin": 0}[tag[:-1]]
        l = int(tag[-1])
        return TT, (lambda i: h[:, i, :]), f"h_{tag}", base + l * KD, a_hi, a_lo

    def source_ready(eng, tag, i):
        _, _, name, *_ = norm_parts(tag)
        if tag == "mix0":
            eng.wait_ge(*have(f"x_loaded{i}", 16))
        elif tag.startswith("mem"):
            eng.wait_ge(*have(f"mem_loaded{tag[-1]}", 16))
            if tag == "mem1":
                for s in range(2):
                    eng.wait_ge(*have(f"xn_stored0_{s}", 16 * (TT // 2)))
        elif tag in ("mix1", "fin1"):
            eng.wait_ge(*have(f"combined{0 if tag == 'mix1' else 1}", 2 * i + 2))
        else:
            eng.wait_ge(*have(name, i + 1))

    OFF = {0: 512, 2: 512 + 384, 1: 1024}

    block = ctx.enter_context(nc.Block())

    @block.sync
    def _(sp):
        for i in range(TT):
            sp.dma_start(h[:, i, :], x[0, i * P:(i + 1) * P, :]).then_inc(sem(f"x_loaded{i}"), 16)
        n = 0
        while n < len(stream):
            key = stream[n]
            if key[0] == "dense":
                ring_free(sp, n)
                sp.dma_start(raw[:, n % RING, :].rearrange("p (k n) -> p k n", k=GC),
                             dense[key[1]]).then_inc(sem(f"raw_loaded{n % RING}"), 16)
                n += 1
                continue
            l = key[1]
            for e in range(2):
                for part in range(3):
                    m = n + 3 * e + part
                    ring_free(sp, m)
                    load_expert(sp, l, e, part, raw[:, m % RING, :], sem(f"raw_loaded{m % RING}"))
            with sp.Fori(1, NE // 2) as i:
                for e in range(2):
                    for part in range(3):
                        s = (n + 3 * e + part) % RING
                        sp.wait_ge(*have(f"expert_w_used{l}", 6 * i + (3 * e + part + 1 - 6)))
                        load_expert(sp, l, 2 * i + e, part, raw[:, s, :], sem(f"raw_loaded{s}"))
            n += 3 * NE
        for i in range(TT):
            sp.wait_ge(*have("out_ready", i + 1))
            sp.dma_start(out[0, i * P:(i + 1) * P, :], xn[:, i % 2, :]).then_inc(sem(f"out_stored{i % 2}"), 16)
        for i in range(2):
            sp.wait_ge(*have(f"out_stored{i}", 16 * (TT // 2)))

    @block.gpsimd
    def _(pool):
        pool_done = sem("pool_steps")
        n_own = [0]

        def own(ins):
            n_own[0] += 1
            ins.then_inc(pool_done, 1)
            pool.wait_ge(pool_done, n_own[0])

        last_row = pool.to_reg(T - 1)

        nc.gpsimd.memset(ones[:], 1.0).then_inc(sem("consts"), 1)
        own(nc.gpsimd.memset(ident[:], 1.0))
        nc.gpsimd.affine_select(out=ident[:], in_=ident[:], pattern=[[-1, P]], compare_op=ALU.is_equal,
                                fill=0.0, base=0, channel_multiplier=1).then_inc(sem("consts"), 1)
        own(nc.gpsimd.memset(tri[:], 1.0))
        nc.gpsimd.affine_select(out=tri[:], in_=tri[:], pattern=[[-1, P]], compare_op=ALU.is_ge,
                                fill=0.0, base=0, channel_multiplier=1).then_inc(sem("consts"), 1)
        own(nc.gpsimd.memset(causal[:], 0.0))
        nc.gpsimd.affine_select(out=causal[:], in_=causal[:], pattern=[[1, P]], compare_op=ALU.is_gt,
                                fill=-1e30, base=0, channel_multiplier=-1).then_inc(sem("consts"), 1)
        for t, pattern, base, ch in ((iota4, [[1, NG]], 0, 0), (iota_b, [[1, NB]], 0, 0),
                                     (slot_lo, [[P, NE]], 0, 0), (tok_no, [[P, TT]], 1, 1)):
            nc.gpsimd.iota(t[:], pattern, base=base, channel_multiplier=ch,
                           allow_small_or_imprecise_dtypes=True).then_inc(sem("consts"), 1)
        pool.wait_ge(*have("vecs_ready", 2))
        nc.gpsimd.memset(conv_in[:, :, 0:PAD], 0.0).then_inc(sem("conv_padded"), 1)

        def gather_results(l, blocks):
            for j in range(2 * TT):
                if j >= 4:
                    pool.wait_ge(*have(f"combined{l}", j - 3))
                col = (j % 2) * TT + j // 2
                pool.indirect_dma_start(out=y_back[:, j % 4, :], out_offset=None, in_=ys_dram[l][0:blocks * P, :],
                                        in_offset=bass.IndirectOffsetOnAxis(ap=slot_i[:, col:col + 1], axis=0)
                                        ).then_inc(sem(f"y_gathered{l}_{j % 4}"), 16)

        def moe(l):
            pool.wait_ge(*have(f"h_xa{l}", 1))
            nc.gpsimd.memset(before[:], 1.0).then_inc(sem(f"router_consts{l}"), 1)
            pool.wait_ge(*have(f"router_consts{l}", 1))
            nc.gpsimd.affine_select(out=before[:], in_=before[:], pattern=[[1, P]], compare_op=ALU.is_gt,
                                    fill=0.0, base=0, channel_multiplier=-1).then_inc(sem(f"router_consts{l}"), 1)
            nc.gpsimd.iota(iota_p[:], [[1, P]], base=0, channel_multiplier=0,
                           allow_small_or_imprecise_dtypes=True).then_inc(sem(f"router_consts{l}"), 1)
            with nc.allow_non_contiguous_dma(reason="router weights are narrow"):
                pool.dma_start(rt_w[:, :, 0:NG], rt_wg[l].rearrange("(k p) n -> p k n", p=P)
                               ).then_inc(sem(f"router_loaded{l}"), 16)
                pool.dma_start(rt_w[:, :, NG:], rt_we[l].rearrange("(k p) n -> p k n", p=P)
                               ).then_inc(sem(f"router_loaded{l}"), 16)
                pool.dma_start(rt_b[:, 0:NG], rt_bg[l:l + 1, :].to_broadcast([P, NG])
                               ).then_inc(sem(f"router_loaded{l}"), 16)
                pool.dma_start(rt_b[:, NG:], rt_be[l:l + 1, :].to_broadcast([P, NE])
                               ).then_inc(sem(f"router_loaded{l}"), 16)
            if l == 0:
                pool.wait_ge(*have("h_ffn0", 1))
                pool.dma_start(mem_tok[:], mem[0].rearrange("(i p) d -> p i d", p=P)
                               ).then_inc(sem("mem_loaded1"), 16)
            for i in range(TT):
                pool.wait_ge(*have(f"xn_ffn{l}", i + 1))
                pool.dma_start(xn_dram[l][i * P:(i + 1) * P, :], xn[:, i % 2, :]
                               ).then_inc(sem(f"xn_stored{l}_{i % 2}"), 16)
            pool.wait_ge(*have(f"h_ffn{l}", TT))
            nc.gpsimd.memset(xs[:], 0.0).then_inc(sem(f"xs_cleared{l}"), 1)
            pool.wait_ge(*have(f"xs_cleared{l}", 1))
            for s in range(2):
                pool.wait_ge(*have(f"xn_stored{l}_{s}", 16 * (TT // 2)))
            pool.wait_ge(*have(f"table_ready{l}", 1))
            for b in range(NE):
                if b >= 2:
                    pool.wait_ge(*have(f"xs_t_in_psum{l}", b - 1))
                pool.indirect_dma_start(out=xs[:, b % 2, :], out_offset=None, in_=xn_dram[l],
                                        in_offset=bass.IndirectOffsetOnAxis(ap=tok_i[:, b:b + 1], axis=0),
                                        bounds_check=last_row, oob_is_err=False
                                        ).then_inc(sem(f"gathered{l}_{b % 2}"), 16)
            for s in range(2):
                pool.wait_ge(*have(f"y_stored{l}_{s}", 16 * (NE // 2)))
            pool.wait_ge(*have(f"overflow_known{l}", 1))
            n_over = pool.value_load(nov_i[0:1, 0:1])
            with pool.If(n_over > 0):
                with pool.Fori(0, OVERFLOW) as j:
                    pool.wait_ge(*have(f"over_index{l}", j + 1))
                    e = pool.value_load(own_i[0:1, bass.ds(j, 1)], min_val=0, max_val=NE - 1)
                    for part in range(3):
                        load_expert(pool, l, e, part, over_w[part][:], sem(f"over_w{l}"))
                    pool.indirect_dma_start(out=xs[:, 0, :], out_offset=None, in_=xn_dram[l],
                                            in_offset=bass.IndirectOffsetOnAxis(ap=idx_c[:, 0:1], axis=0),
                                            bounds_check=last_row, oob_is_err=False
                                            ).then_inc(sem(f"over_x{l}"), 16)
                    pool.wait_ge(*have(f"over_y{l}", 2 * j + 2))
                    pool.dma_start(ys_dram[l][bass.ds(j * P + NE * P, P), :], y_sb[:, 0, :]
                                   ).then_inc(sem(f"over_stored{l}"), 16)
                    pool.wait_ge(*have(f"over_stored{l}", 16 * j + 16))
            with pool.If(n_over > 0):
                gather_results(l, NE + OVERFLOW)
            with pool.If(n_over < 1):
                gather_results(l, NE)

        moe(0)
        pool.dma_start(ws_in[:], c_ws[0].rearrange("g t s -> t g s")).then_inc(sem("ws_loaded"), 16)
        pool.wait_ge(*have("ws_loaded", 16))
        nc.gpsimd.affine_select(out=ws_in[:], in_=ws_in[:], pattern=[[0, GM], [-1, P]], compare_op=ALU.is_ge,
                                fill=0.0, base=0, channel_multiplier=1).then_inc(sem("ws_masked"), 1)
        pool.dma_start(vg_b[:], c_vnorm_g[0:1, :].to_broadcast([P, D])).then_inc(sem("vnorm_loaded"), 16)
        pool.dma_start(vb_b[:], c_vnorm_b[0:1, :].to_broadcast([P, D])).then_inc(sem("vnorm_loaded"), 16)
        pool.wait_ge(*have("dense_used", first["vx1"] + 4))
        pool.dma_start(bs_b[:], c_bs[0:1].to_broadcast([P, GM, P])).then_inc(sem("bs_loaded"), 16)
        for g in range(KD):
            pool.wait_ge(*have("gated_hi", g + 1))
            nc.gpsimd.tensor_tensor(a_lo[:, g, :], u_c[:, g, :], a_hi[:, g, :].bitcast(fp32), ALU.subtract
                                    ).then_inc(sem("gated_lo"), 1)
        moe(1)
        pool.dma_start(fg_b[:], final_norm_g.rearrange("(o d) -> o d", o=1).to_broadcast([P, D])
                       ).then_inc(sem("final_gain_loaded"), 16)

    @block.tensor
    def _(pe):
        mm = nc.tensor.matmul

        def granule(d, j, banks, feature_major, n_m, hi, lo, part=slice(0, BANK), ready=None):
            pe.wait_ge(*have("w_lo_ready", d + 1))
            s = d % SPLIT
            for kk in range(GC):
                k = GC * j + kk
                if ready is not None:
                    pe.wait_ge(*have(ready, k + 1))
                for m in range(n_m):
                    o = ps[:, banks + m, part]
                    cut = slice(m * P, (m + 1) * P)
                    for c, (wt, act) in enumerate(((w_hi, hi), (w_hi, lo), (w_lo, hi))):
                        if feature_major:
                            lhs, rhs = wt[:, s, kk, cut], act[:, k, :]
                        else:
                            lhs, rhs = act[:, k, cut], wt[:, s, kk, :]
                        last = mm(o, lhs, rhs, start=(k == 0 and c == 0), stop=(k == KD - 1 and c == 2))
            last.then_inc(sem("dense_used"), 1)

        def transposes(tag):
            n = norm_parts(tag)[0]
            per = BANK // (n * P)
            b0 = 4 if n == MT else 0
            for i in range(n):
                pe.wait_ge(*have(f"xn_{tag}", i + 1))
                for k in range(KD):
                    src = mem_tok[:, i, k * P:(k + 1) * P] if n == MT else xn[:, i % 2, k * P:(k + 1) * P]
                    c0 = (k % per) * n * P + i * P
                    last = nc.tensor.transpose(ps[:, b0 + k // per, c0:c0 + P], src, ident[:])
                name = f"mem_t_in_psum{tag[-1]}" if n == MT else f"xn_t_in_psum_{tag}"
                last.then_inc(sem(name), 1)

        pe.wait_ge(*have("consts", 8))
        pe.wait_ge(*have("vecs_loaded", 16 * 8))
        nc.tensor.transpose(ps[:, 0, 0:NV], vec_in[0:NV, :], ident[0:NV, 0:NV]).then_inc(sem("vecs_in_psum"), 1)
        for m in range(CC):
            last = nc.tensor.transpose(ps[:, 1, m * TAPS:(m + 1) * TAPS], tap_in[0:TAPS, m * P:(m + 1) * P],
                                       ident[0:TAPS, 0:TAPS])
        last.then_inc(sem("vecs_in_psum"), 1)
        pe.wait_ge(*have("vecs_ready", 2))

        transposes("mix0")
        pe.wait_ge(*have("split_lo_mix0", 4))
        granule(0, 0, 0, True, CC, a_hi, a_lo, ready="split_lo_mix0")
        granule(1, 1, 0, True, CC, a_hi, a_lo, ready="split_lo_mix0")
        for j in range(2):
            granule(first["sb_a"] + j, j, 4, True, CC, a_hi, a_lo)
        pe.wait_ge(*have("gate_done", 1))
        for j in range(2):
            granule(first["sb_q"] + j, j, 0, True, CC, a_hi, a_lo)
        pe.wait_ge(*have("glu_done", 1))
        for j in range(2):
            granule(first["sb_k"] + j, j, 4, True, CC, a_hi, a_lo)
        pe.wait_ge(*have("q_ready", 1))
        granule(first["sb_v"], 0, 0, False, TT, a_hi, a_lo)
        pe.wait_ge(*have("k_ready", 1))
        transposes("mem0")
        granule(first["sb_v"] + 1, 1, 0, False, TT, a_hi, a_lo)

        def mem_keys(l, s, bank):
            for j in range(2):
                granule(first[f"kx{l}"] + 2 * s + j, j, bank, True, 4, mem_hi, mem_lo, part=slice(0, M),
                        ready=f"mem_split_lo{l}" if s == 0 else None)

        def mem_values(l, s, bank):
            for j in range(2):
                granule(first[f"vx{l}"] + 2 * s + j, j, bank, False, MT, mem_hi, mem_lo)

        pe.wait_ge(*have("v_ready", 1))
        mem_keys(0, 0, 0)
        pe.wait_ge(*have("mem_split_lo0", KD))
        mem_keys(0, 1, 4)
        pe.wait_ge(*have("kx_ready0", 1))
        mem_values(0, 0, 0)
        mem_values(0, 1, 2)
        pe.wait_ge(*have("kx_ready0", 2))

        def head(hd):
            return slice((hd % 2) * SB_DH, (hd % 2 + 1) * SB_DH), hd // 2

        def scores(hd):
            rows, c = head(hd)
            if hd:
                pe.wait_ge(*have("z_diag", hd))
                pe.wait_ge(*have("z_off", hd))
            for j in range(TT):
                cut = slice(j * P, (j + 1) * P)
                last = mm(ps[:, 4, cut], k_t[rows, c, cut], q_t[rows, c, cut], start=True, stop=True)
                if j < TT - 1:
                    o = OFF[j]
                    bank, o = 4 + o // BANK, o % BANK
                    last = mm(ps[:, bank, o:o + T - (j + 1) * P], k_t[rows, c, cut], q_t[rows, c, (j + 1) * P:],
                              start=True, stop=True)
            last.then_inc(sem("z_in_psum"), 1)

        def sums(hd):
            pe.wait_ge(*have("softplus", hd + 1))
            if hd:
                pe.wait_ge(*have("log_w", hd))
            else:
                pe.wait_ge(*have("vx_ready0", 2))
            s = sbuf[:, hd % 2, :]
            mm(ps[:, 0, :], tri[:], s[:, 0:512], start=True, stop=True)
            mm(ps[:, 1, :], tri[:], s[:, 512:1024], start=True, stop=False, skip_group_check=True)
            mm(ps[:, 2, 0:256], tri[:], s[:, 1024:1280], start=True, stop=False, skip_group_check=True)
            mm(ps[:, 1, 0:384], ones[:], s[:, 128:512], start=False, stop=False, skip_group_check=True)
            mm(ps[:, 1, 128:384], ones[:], s[:, 1024:1280], start=False, stop=False, skip_group_check=True)
            mm(ps[:, 1, 256:384], ones[:], s[:, 896:1024], start=False, stop=False, skip_group_check=True)
            mm(ps[:, 1, 384:512], ones[:], s[:, 384:512], start=False, stop=True, skip_group_check=True)
            mm(ps[:, 2, 0:256], ones[:], s[:, 256:512], start=False, stop=False, skip_group_check=True)
            mm(ps[:, 2, 128:256], ones[:], s[:, 896:1024], start=False, stop=True, skip_group_check=True
               ).then_inc(sem("sums_in_psum"), 1)

        def values(hd):
            rows, c = head(hd)
            pe.wait_ge(*have("weights", hd + 1))
            if hd >= 2 and hd % 2 == 0:
                pe.wait_ge(*have("heads_lo", hd // 2))
            w = zbuf[:, hd % 2, :]
            o = ps[rows, 3, :]
            vcol = slice(hd * SB_DH, (hd + 1) * SB_DH)
            for j in range(TT):
                v = v_s[:, j, vcol]
                last = mm(o[:, j * P:(j + 1) * P], v, w[:, j * P:(j + 1) * P], start=(j == 0), stop=(j == TT - 1),
                          skip_group_check=True)
                if j < TT - 1:
                    n = T - (j + 1) * P
                    last = mm(o[:, (j + 1) * P:], v, w[:, OFF[j]:OFF[j] + n], start=False, stop=False,
                              skip_group_check=True)
            last.then_inc(sem("heads_in_psum"), 1)

        scores(0)
        for hd in range(SB_HEADS):
            if hd + 1 < SB_HEADS:
                scores(hd + 1)
            if hd:
                values(hd - 1)
            sums(hd)
            if hd == 5:
                pe.wait_ge(*have("conv_taps", CC * TAPS))
                for m in range(CC):
                    last = mm(ps[:, 7, :], ones[:], conv_acc[:, m, :], start=(m == 0), stop=(m == CC - 1))
                last.then_inc(sem("conv_mean"), 1)
            if hd == 6:
                pe.wait_ge(*have("conv_squared", 1))
                for m in range(CC):
                    last = mm(ps[:, 7, :], ones[:], conv_sq[:, m, :], start=(m == 0), stop=(m == CC - 1))
                last.then_inc(sem("conv_var"), 1)
        values(SB_HEADS - 1)

        def project_out(l):
            if l == 0:
                pe.wait_ge(*have("heads_lo", SB_HEADS // 2))
                pe.wait_ge(*have("conv_lo", CC))
                pe.wait_ge(*have("log_w", SB_HEADS))
            for s in range(2):
                for j in range(2):
                    granule(first[f"mix_out{l}"] + 2 * s + j, j, 4 * s, False, TT, a_hi, a_lo,
                            ready="gated_lo" if l and s == 0 else None)

        def cross(l):
            transposes(f"xa{l}")
            for s in range(2):
                pe.wait_ge(*have(f"split_lo_xa{l}", 4 * (s + 1)))
                for j in range(2):
                    granule(first[f"xq{l}"] + 2 * s + j, j, 4 * s, True, 4, a_hi, a_lo,
                            ready=f"split_lo_xa{l}" if s == 0 else None)

            def xscores(hd):
                if hd < 2:
                    pe.wait_ge(*have(f"xq_ready{l}", hd + 1))
                else:
                    pe.wait_ge(*have(f"x_exp{l}", TT * (hd - 1)))
                for i in range(TT):
                    b = 2 * (hd % 2) + i // 2
                    for c in range(2):
                        last = mm(ps[:, b, (i % 2) * M:(i % 2 + 1) * M], xq[:, 2 * hd + c, i * P:(i + 1) * P],
                                  kx[:, 2 * hd + c, :], start=(c == 0), stop=(c == 1))
                last.then_inc(sem(f"x_scores{l}"), 1)

            def xvalues(hd):
                pe.wait_ge(*have(f"x_probs{l}", hd + 1))
                if hd:
                    pe.wait_ge(*have(f"x_probs_t{l}", hd))
                for i in range(TT):
                    for c in range(MT):
                        last = nc.tensor.transpose(ps[:, 4 + c, i * P:(i + 1) * P], xp[:, hd % 2, i, c * P:(c + 1) * P],
                                                   ident[:])
                last.then_inc(sem(f"x_probs_t_in_psum{l}"), 1)
                pe.wait_ge(*have(f"x_probs_t{l}", hd + 1))
                if hd:
                    pe.wait_ge(*have(f"x_heads_lo{l}", 2 * hd))
                for c2 in range(2):
                    f0 = hd * XD + c2 * P
                    for c in range(MT):
                        last = mm(ps[:, 6 + c2, :], vx[:, c, f0:f0 + P], xpt[:, hd % 2, c, :], start=(c == 0),
                                  stop=(c == MT - 1))
                last.then_inc(sem(f"x_heads_in_psum{l}"), 1)

            xscores(0)
            pe.wait_ge(*have(f"xq_ready{l}", 2))
            for hd in range(XH):
                if hd + 1 < XH:
                    xscores(hd + 1)
                xvalues(hd)
            for s in range(2):
                if s == 0:
                    pe.wait_ge(*have(f"x_exp{l}", TT * XH))
                for j in range(2):
                    granule(first[f"xo{l}"] + 2 * s + j, j, 4 * s, False, TT, a_hi, a_lo,
                            ready=f"x_heads_lo{l}" if s == 0 else None)

        def experts(l):
            transposes(f"ffn{l}")
            pe.wait_ge(*have(f"router_loaded{l}", 64))
            pe.wait_ge(*have(f"a_full{l}", KD))
            W = NG + NE
            for i in range(TT):
                for k in range(KD):
                    last = mm(ps[:, 0, i * W:(i + 1) * W], a_full[:, k, i * P:(i + 1) * P], rt_w[:, k, :],
                              start=(k == 0), stop=(k == KD - 1))
            last.then_inc(sem(f"logits{l}"), 1)
            if l == 0:
                transposes("mem1")
                pe.wait_ge(*have("mem_split_lo1", KD))
                mem_keys(1, 0, 4)
            pe.wait_ge(*have(f"assigned{l}", 1))
            pe.wait_ge(*have(f"router_consts{l}", 3))
            for i in range(TT):
                for j in range(i + 1):
                    mm(ps[:, 1, i * NE:(i + 1) * NE], (before if j == i else ones)[:], e_sum[:, j, :],
                       start=(j == 0), stop=(j == i))
            for j in range(TT):
                last = mm(ps[:, 1, TT * NE:(TT + 1) * NE], ones[:], e_sum[:, j, :], start=(j == 0), stop=(j == TT - 1))
            last.then_inc(sem(f"ranks{l}"), 1)
            if l == 0:
                pe.wait_ge(*have("kx_ready1", 1))
                granule(first["kx1"] + 2, 0, 4, True, 4, mem_hi, mem_lo, part=slice(0, M))
            pe.wait_ge(*have(f"hots{l}", 2))
            for j in range(2 * TT):
                last = mm(ps[:, 2, 0:NB], slot_hot[:, j, :], blk_hot[:, j, :], start=(j == 0), stop=(j == 2 * TT - 1))
            last.then_inc(sem(f"table{l}"), 1)
            if l == 0:
                granule(first["kx1"] + 3, 1, 4, True, 4, mem_hi, mem_lo, part=slice(0, M))

            n0 = stream.index(("moe", l, 0, 0))

            def xs_transposes(s):
                for k in range(KD):
                    last = nc.tensor.transpose(ps[:, k // 4, (k % 4) * P:(k % 4 + 1) * P],
                                               xs[:, s, k * P:(k + 1) * P], ident[:])
                last.then_inc(sem(f"xs_t_in_psum{l}"), 1)

            if l == 0:
                pe.wait_ge(*have("kx_ready1", 2))
            pe.wait_ge(*have(f"table_ready{l}", 1))
            pe.wait_ge(*have(f"gathered{l}_0", 16))
            xs_transposes(0)

            def block_of(i, e, first_pair, last_pair):
                b = 2 * i + e

                def loaded(part):
                    s = ring_pos[("moe", l, e, part)]
                    step = ring_count[("moe", l, 2 + e, part)] - ring_count[("moe", l, e, part)]
                    pe.wait_ge(*have(f"raw_loaded{s}", i * step + ring_count[("moe", l, e, part)]))
                    return raw[:, s, :]

                pe.wait_ge(*have(f"xs_t_ready{l}", b + 1))
                if not first_pair:
                    pe.wait_ge(*have(f"hidden{l}", b - 1))
                for part in range(2):
                    w = loaded(part)
                    for kk in range(GC):
                        k = GC * part + kk
                        last = mm(ps[:, 2 + e, :], xs_t[:, e, k, :], w[:, kk * BANK:(kk + 1) * BANK],
                                  start=(k == 0), stop=(k == KD - 1))
                    last.then_inc(sem(f"expert_w_used{l}"), 1)
                if not (last_pair and e == 1):
                    pe.wait_ge(*have(f"gathered{l}_{1 - e}", 16 * i + (16 if e == 0 else 32)))
                    xs_transposes(1 - e)
                pe.wait_ge(*have(f"hidden{l}", b + 1))
                for c in range(2):
                    last = nc.tensor.transpose(ps[:, 4, c * P:(c + 1) * P], hid[:, e, c * P:(c + 1) * P], ident[:])
                last.then_inc(sem(f"hidden_t_in_psum{l}"), 1)
                w = loaded(2)
                pe.wait_ge(*have(f"hidden_t{l}", b + 1))
                if not (first_pair and e == 0):
                    pe.wait_ge(*have(f"y_left{l}", b))
                    pe.wait_ge(*have(f"y_right{l}", b))
                for half in range(2):
                    for c in range(2):
                        last = mm(ps[:, 5 + half, :], hid_t[:, e, c, :], w[:, c * D + half * BANK:c * D + (half + 1) * BANK],
                                  start=(c == 0), stop=(c == 1))
                last.then_inc(sem(f"expert_w_used{l}"), 1)

            for e in range(2):
                block_of(0, e, True, False)
            with pe.Fori(1, NE // 2 - 1) as i:
                for e in range(2):
                    block_of(i, e, False, False)
            for e in range(2):
                block_of(NE // 2 - 1, e, False, True)

            pe.wait_ge(*have(f"y_left{l}", NE))
            pe.wait_ge(*have(f"y_right{l}", NE))
            pe.wait_ge(*have(f"overflow_known{l}", 1))
            n_over = pe.value_load(nov_i[0:1, 0:1])
            with pe.If(n_over > 0):
                with pe.Fori(0, OVERFLOW) as j:
                    pe.wait_ge(*have(f"over_x{l}", 16 * j + 16))
                    for k in range(KD):
                        last = nc.tensor.transpose(ps[:, k // 4, (k % 4) * P:(k % 4 + 1) * P],
                                                   xs[:, 0, k * P:(k + 1) * P], ident[:])
                    last.then_inc(sem(f"over_x_t_in_psum{l}"), 1)
                    pe.wait_ge(*have(f"over_w{l}", 80 * j + 80))
                    pe.wait_ge(*have(f"over_x_t{l}", j + 1))
                    for k in range(KD):
                        last = mm(ps[:, 2, :], xs_t[:, 0, k, :], over_w[k // GC][:, (k % GC) * BANK:(k % GC + 1) * BANK],
                                  start=(k == 0), stop=(k == KD - 1))
                    last.then_inc(sem(f"over_gate_up{l}"), 1)
                    pe.wait_ge(*have(f"over_hidden{l}", j + 1))
                    for c in range(2):
                        last = nc.tensor.transpose(ps[:, 4, c * P:(c + 1) * P], hid[:, 0, c * P:(c + 1) * P], ident[:])
                    last.then_inc(sem(f"over_hidden_t_in_psum{l}"), 1)
                    pe.wait_ge(*have(f"over_hidden_t{l}", j + 1))
                    for half in range(2):
                        for c in range(2):
                            last = mm(ps[:, 5 + half, :], hid_t[:, 0, c, :],
                                      over_w[2][:, c * D + half * BANK:c * D + (half + 1) * BANK],
                                      start=(c == 0), stop=(c == 1))
                    last.then_inc(sem(f"over_down{l}"), 1)
                    pe.wait_ge(*have(f"over_y{l}", 2 * j + 2))

        project_out(0)
        cross(0)
        experts(0)

        for s in range(2):
            mem_values(1, s, 2 * s)
        pe.wait_ge(*have("vx_ready1", 2))
        transposes("mix1")
        pe.wait_ge(*have("split_lo_mix1", 4))
        granule(first["c_v"], 0, 0, False, TT, a_hi, a_lo, ready="split_lo_mix1")
        pe.wait_ge(*have("split_lo_mix1", KD))
        pe.wait_ge(*have("ws_masked", 1))
        for g in range(GM):
            last = nc.tensor.transpose(ps[:, 4 + g // 4, (g % 4) * P:(g % 4 + 1) * P], ws_in[:, g, :], ident[:])
        last.then_inc(sem("ws_t_in_psum"), 1)
        granule(first["c_v"] + 1, 1, 0, False, TT, a_hi, a_lo)
        pe.wait_ge(*have("ws_t_ready", 1))
        for j in range(2):
            granule(first["c_v"] + 2 + j, j, 4, False, TT, a_hi, a_lo)
        for s in range(2):
            pe.wait_ge(*have("v_gelu", s + 1))
            for j in range(2):
                granule(first["c_u"] + 2 * s + j, j, 4 * s, True, 4, a_hi, a_lo)
        pe.wait_ge(*have("v_normed", TT))
        for g in range(GM):
            if g in (0, 4):
                pe.wait_ge(*have("u_gelu", g // 4 + 1))
            for c in range(TT):
                last = mm(ps[:, g, c * P:(c + 1) * P], v_c[:, c, g * P:(g + 1) * P], ws_t[:, g, :], start=True, stop=True)
            last.then_inc(sem("mixed_in_psum"), 1)
        pe.wait_ge(*have("gated", GM))
        project_out(1)
        cross(1)
        experts(1)

    @block.scalar
    def _(act):
        A = nc.scalar.activation

        for t, n, src in ((0, KD, mem_norm_g.rearrange("(k p) -> k p", p=P)),
                          (MIX_G, NL * KD, norm_mix.rearrange("l (k p) -> (l k) p", p=P)),
                          (XA_G, NL * KD, norm_xa.rearrange("l (k p) -> (l k) p", p=P)),
                          (FFN_G, NL * KD, norm_ffn.rearrange("l (k p) -> (l k) p", p=P)),
                          (CONV_B, CC, ab_conv_b.rearrange("l (k p) -> (l k) p", p=P)),
                          (CN_G, CC, ab_cnorm_g.rearrange("l (k p) -> (l k) p", p=P)),
                          (CN_B, CC, ab_cnorm_b.rearrange("l (k p) -> (l k) p", p=P)),):
            act.dma_start(vec_in[t:t + n, :], src).then_inc(sem("vecs_loaded"), 16)
        act.dma_start(tap_in[0:TAPS, :], ab_conv_w[0]).then_inc(sem("vecs_loaded"), 16)
        act.dma_start(mem_tok[:], mem[0].rearrange("(i p) d -> p i d", p=P)).then_inc(sem("mem_loaded0"), 16)

        n_prep = [0]

        def prep(upto):
            while n_prep[0] < upto:
                d = n_prep[0]
                n_prep[0] += 1
                key = ("dense", d)
                act.wait_ge(*have(f"raw_loaded{ring_pos[key]}", ring_count[key]))
                if d >= SPLIT:
                    act.wait_ge(*have("dense_used", d - SPLIT + 1))
                A(w_hi[:, d % SPLIT].rearrange("p k n -> p (k n)"), raw[:, ring_pos[key], :], ACT.Copy
                  ).then_inc(sem("w_hi_ready"), 1)

        def squares(tag):
            n, src, *_ = norm_parts(tag)
            for i in range(n // 2):
                source_ready(act, tag, i)
                if i:
                    act.wait_ge(*have(f"squares_act_{tag}", i))
                A(xn[:, 0, :], src(i), ACT.Square, accum_out=n_ss[:, i:i + 1]).then_inc(sem(f"squares_act_{tag}"), 1)
            act.wait_ge(*have(f"norm_var_{tag}", 1))
            A(n_y[:, 0:n], n_var[:, 0:n], ACT.Sqrt).then_inc(sem(f"norm_root_{tag}"), 1)

        def split(tag, done):
            n, _, _, g0, hi, lo = norm_parts(tag)
            per = BANK // (n * P)
            b0 = 4 if n == MT else 0
            name = f"mem_t_in_psum{tag[-1]}" if n == MT else f"xn_t_in_psum_{tag}"
            act.wait_ge(*have(name, n))
            for k in range(KD):
                c0 = (k % per) * n * P
                A(hi[:, k, :], ps[:, b0 + k // per, c0:c0 + n * P], ACT.Copy, scale=vecs[:, g0 + k:g0 + k + 1]
                  ).then_inc(sem(done), 1)

        def used(d):
            act.wait_ge(*have("dense_used", d + 1))

        def copy_out(name, dst, src, scale=1.0):
            A(dst, src, ACT.Copy, scale=scale).then_inc(sem(name), 1)

        act.wait_ge(*have("vecs_ready", 2))
        prep(2)
        squares("mix0")
        split("mix0", "split_hi_mix0")
        prep(3)
        squares("mem0")
        used(1)
        A(conv_acc[:].rearrange("p k n -> p (k n)"), ps[:, 0:4, :].rearrange("p k n -> p (k n)"), ACT.Sigmoid
          ).then_inc(sem("gate_done"), 1)
        prep(7)
        used(first["sb_q"] + 1)
        copy_out("q_ready", q_t[:], ps[:, 0:4, :], SB_DH ** -0.5)
        prep(9)
        used(first["sb_k"] + 1)
        copy_out("k_ready", k_t[:], ps[:, 4:8, :])
        prep(10)
        split("mem0", "mem_split_hi0")
        prep(11)
        used(first["sb_v"] + 1)
        copy_out("v_ready", v_s[:], ps[:, 0:4, :])
        prep(13)

        def mem_keys_out(l, s, bank):
            used(first[f"kx{l}"] + 2 * s + 1)
            copy_out(f"kx_ready{l}", kx[:, 4 * s:4 * s + 4, :], ps[:, bank:bank + 4, 0:M])

        def mem_values_out(l, s, bank):
            used(first[f"vx{l}"] + 2 * s + 1)
            copy_out(f"vx_ready{l}", vx[:, :, s * BANK:(s + 1) * BANK], ps[:, bank:bank + MT, :])

        prep(14)
        mem_keys_out(0, 0, 0)
        prep(15)
        prep(16)
        mem_keys_out(0, 1, 4)
        prep(18)
        mem_values_out(0, 0, 0)
        prep(19)
        mem_values_out(0, 1, 2)
        prep(20)

        def z_part(hd):
            s = hd % 2
            act.wait_ge(*have("z_in_psum", hd + 1))
            if hd >= 2:
                act.wait_ge(*have("heads_in_psum", hd - 1))
            else:
                act.wait_ge(*have("dense_used", first["vx0"] + 4))
            A(zbuf[:, s, 512:1280], ps[:, 5:7, :].rearrange("p k n -> p (k n)")[:, 0:768], ACT.Copy
              ).then_inc(sem("z_off"), 1)
            act.wait_ge(*have("minus_abs_z", hd + 1))
            A(sbuf[:, s, :], sbuf[:, s, :], ACT.Exp).then_inc(sem("exp_abs"), 1)
            act.wait_ge(*have("exp_abs", hd + 1))
            A(sbuf[:, s, :], sbuf[:, s, :], ACT.Ln, bias=1.0).then_inc(sem("ln_done"), 1)

        def w_part(hd):
            act.wait_ge(*have("log_w", hd + 1))
            A(zbuf[:, hd % 2, :], zbuf[:, hd % 2, :], ACT.Exp).then_inc(sem("weights"), 1)

        def heads_hi(pair):
            act.wait_ge(*have("heads_in_psum", 2 * pair + 2))
            copy_out("heads_hi", a_hi[:, CC + pair, :], ps[:, 3, :])

        z_part(0)
        for hd in range(SB_HEADS):
            if hd + 1 < SB_HEADS:
                z_part(hd + 1)
            if hd in (2, 4, 6):
                heads_hi(hd // 2 - 1)
            w_part(hd)
            if hd == 6:
                act.wait_ge(*have("conv_centred", 1))
                A(conv_sq[:].rearrange("p k n -> p (k n)"), conv_acc[:].rearrange("p k n -> p (k n)"), ACT.Square
                  ).then_inc(sem("conv_squared"), 1)
        act.wait_ge(*have("conv_var_ready", 1))
        A(conv_rs[:, 1, :], conv_rs[:, 0, :], ACT.Sqrt).then_inc(sem("conv_root"), 1)
        heads_hi(3)
        act.wait_ge(*have("conv_normed", 1))
        for m in range(CC):
            A(conv_sq[:, m, :], conv_acc[:, m, :], ACT.Silu, bias=vecs[:, CN_B + m:CN_B + m + 1],
              scale=vecs[:, CN_G + m:CN_G + m + 1]).then_inc(sem("conv_silu"), 1)
        for m in range(CC):
            act.wait_ge(*have("conv_silu", m + 1))
            copy_out("conv_hi", a_hi[:, m, :], conv_sq[:, m, :])
        prep(first["xq0"] + 2)

        def cross(l):
            d = first[f"xq{l}"]
            squares(f"xa{l}")
            split(f"xa{l}", f"split_hi_xa{l}")
            prep(d + 3)
            used(d + 1)
            copy_out(f"xq_ready{l}", xq[:, 0:4, :], ps[:, 0:4, :], XD ** -0.5)
            prep(d + 5)
            used(d + 3)
            copy_out(f"xq_ready{l}", xq[:, 4:8, :], ps[:, 4:8, :], XD ** -0.5)
            prep(d + 6)

            def x_exp(hd):
                act.wait_ge(*have(f"x_max{l}", hd + 1))
                if hd >= 2:
                    act.wait_ge(*have(f"x_probs_t_in_psum{l}", hd - 1))
                for i in range(TT):
                    b = 2 * (hd % 2) + i // 2
                    A(xp[:, hd % 2, i, :], ps[:, b, (i % 2) * M:(i % 2 + 1) * M], ACT.Exp, bias=x_max[:, i:i + 1],
                      accum_out=x_sum[:, i:i + 1]).then_inc(sem(f"x_exp{l}"), 1)

            x_exp(0)
            for hd in range(XH):
                act.wait_ge(*have(f"x_probs_t_in_psum{l}", hd + 1))
                if hd >= 2:
                    act.wait_ge(*have(f"x_heads_in_psum{l}", hd - 1))
                copy_out(f"x_probs_t{l}", xpt[:, hd % 2], ps[:, 4:6, :])
                if hd + 1 < XH:
                    x_exp(hd + 1)
                act.wait_ge(*have(f"x_heads_in_psum{l}", hd + 1))
                for c in range(2):
                    copy_out(f"x_heads_hi{l}", a_hi[:, 2 * hd + c, :], ps[:, 6 + c, :])
            prep(min(d + 10, ND))

        def experts(l):
            squares(f"ffn{l}")
            act.wait_ge(*have(f"xn_t_in_psum_ffn{l}", TT))
            for k in range(KD // 2):
                A(a_full[:, k, :], ps[:, k, :], ACT.Copy, scale=vecs[:, FFN_G + l * KD + k:FFN_G + l * KD + k + 1]
                  ).then_inc(sem(f"a_full{l}"), 1)
            if l == 0:
                squares("mem1")
                split("mem1", "mem_split_hi1")
            act.wait_ge(*have(f"r_args{l}", 1))
            A(r4b[:], r4a[:], ACT.Exp).then_inc(sem(f"r_exp{l}"), 1)
            act.wait_ge(*have(f"r_args{l}", 2))
            A(r1b[:], r1a[:], ACT.Exp).then_inc(sem(f"r_exp{l}"), 1)
            if l == 0:
                prep(33)
                mem_keys_out(1, 0, 4)
                prep(34)
                mem_keys_out(1, 1, 4)

            def block_of(i, e, first_pair):
                b = 2 * i + e
                act.wait_ge(*have(f"expert_w_used{l}", 3 * b + 2))
                if not first_pair:
                    act.wait_ge(*have(f"hidden{l}", b - 1))
                A(silu_g[:, e, :], ps[:, 2 + e, 0:FE], ACT.Silu).then_inc(sem(f"silu{l}"), 1)
                act.wait_ge(*have(f"hidden_t_in_psum{l}", b + 1))
                A(hid_t[:, e].rearrange("p c n -> p (c n)"), ps[:, 4, 0:2 * P], ACT.Copy
                  ).then_inc(sem(f"hidden_t{l}"), 1)
                act.wait_ge(*have(f"expert_w_used{l}", 3 * b + 3))
                if not first_pair:
                    act.wait_ge(*have(f"y_stored{l}_{e}", 16 * i))
                A(y_sb[:, e, 0:BANK], ps[:, 5, :], ACT.Copy).then_inc(sem(f"y_left{l}"), 1)
                act.wait_ge(*have(f"y_left{l}", b + 1))
                act.wait_ge(*have(f"y_right{l}", b + 1))
                act.dma_start(ys_dram[l][b * P:(b + 1) * P, :] if isinstance(b, int) else
                              ys_dram[l][bass.ds(b * P, P), :], y_sb[:, e, :]
                              ).then_inc(sem(f"y_stored{l}_{e}"), 16)

            for e in range(2):
                block_of(0, e, True)
            with act.Fori(1, NE // 2) as i:
                for e in range(2):
                    block_of(i, e, False)

            act.wait_ge(*have(f"y_stored{l}_0", 16 * (NE // 2)))
            act.wait_ge(*have(f"overflow_known{l}", 1))
            n_over = act.value_load(nov_i[0:1, 0:1])
            with act.If(n_over > 0):
                with act.Fori(0, OVERFLOW) as j:
                    act.wait_ge(*have(f"over_gate_up{l}", j + 1))
                    A(silu_g[:, 0, :], ps[:, 2, 0:FE], ACT.Silu).then_inc(sem(f"over_silu{l}"), 1)
                    act.wait_ge(*have(f"over_hidden_t_in_psum{l}", j + 1))
                    A(hid_t[:, 0].rearrange("p c n -> p (c n)"), ps[:, 4, 0:2 * P], ACT.Copy
                      ).then_inc(sem(f"over_hidden_t{l}"), 1)
                    act.wait_ge(*have(f"over_down{l}", j + 1))
                    A(y_sb[:, 0, 0:BANK], ps[:, 5, :], ACT.Copy).then_inc(sem(f"over_y{l}"), 1)
                    act.wait_ge(*have(f"over_stored{l}", 16 * j + 16))

        cross(0)
        experts(0)

        prep(38)
        mem_values_out(1, 0, 0)
        prep(40)
        mem_values_out(1, 1, 2)
        squares("mix1")
        split("mix1", "split_hi_mix1")
        d = first["c_v"]
        prep(d + 3)
        act.wait_ge(*have("ws_t_in_psum", 1))
        copy_out("ws_t_ready", ws_t[:].rearrange("p g t -> p (g t)"), ps[:, 4:6, :].rearrange("p a b -> p (a b)"))
        prep(d + 4)
        used(d + 1)
        A(v_c[:, :, 0:BANK], ps[:, 0:4, :], ACT.Gelu).then_inc(sem("v_gelu"), 1)
        prep(d + 6)
        used(d + 3)
        A(v_c[:, :, BANK:], ps[:, 4:8, :], ACT.Gelu).then_inc(sem("v_gelu"), 1)
        act.wait_ge(*have("norm_var_v", 1))
        A(n_y[:], n_var[:], ACT.Sqrt).then_inc(sem("norm_root_v"), 1)
        prep(d + 8)
        used(d + 5)
        A(u_c[:, 0:4, :], ps[:, 0:4, :], ACT.Gelu).then_inc(sem("u_gelu"), 1)
        prep(d + 10)
        used(d + 7)
        A(u_c[:, 4:8, :], ps[:, 4:8, :], ACT.Gelu).then_inc(sem("u_gelu"), 1)
        for g in range(GM):
            act.wait_ge(*have("gated", g + 1))
            copy_out("gated_hi", a_hi[:, g, :], u_c[:, g, :])
        prep(first["xq1"] + 2)
        cross(1)
        experts(1)
        squares("fin1")

    @block.vector
    def _(dve):
        V = nc.vector
        own_sem = sem("dve_steps")
        n_own = [0]

        def own(ins):
            n_own[0] += 1
            ins.then_inc(own_sem, 1)
            dve.wait_ge(own_sem, n_own[0])

        n_prep = [0]

        def prep(upto):
            while n_prep[0] < upto:
                d = n_prep[0]
                n_prep[0] += 1
                dve.wait_ge(*have("w_hi_ready", d + 1))
                V.tensor_tensor(w_lo[:, d % SPLIT].rearrange("p k n -> p (k n)"), raw[:, ring_pos[("dense", d)], :],
                                w_hi[:, d % SPLIT].rearrange("p k n -> p (k n)").bitcast(fp32), ALU.subtract
                                ).then_inc(sem("w_lo_ready"), 1)

        def rstd(tag, n, var):
            dve.wait_ge(*have(f"norm_root_{tag}", 1))
            y, t = n_y[:, 0:n], n_t[:, 0:n]
            own(V.reciprocal(y, y))
            own(V.tensor_tensor(t, y, y, ALU.mult))
            own(V.scalar_tensor_tensor(out=t, in0=t, scalar=-0.5, in1=var, op0=ALU.mult, op1=ALU.mult))
            own(V.scalar_tensor_tensor(out=y, in0=t, scalar=1.5, in1=y, op0=ALU.add, op1=ALU.mult))

        def norm(tag):
            n, src, *_ = norm_parts(tag)
            for i in range(n // 2, n):
                source_ready(dve, tag, i)
                own(V.scalar_tensor_tensor(out=xn[:, 1, :], in0=src(i), scalar=1.0, in1=src(i), op0=ALU.mult,
                                           op1=ALU.mult, accum_out=n_ss[:, i:i + 1]))
            dve.wait_ge(*have(f"squares_act_{tag}", n // 2))
            V.tensor_scalar(n_var[:, 0:n], n_ss[:, 0:n], 1.0 / D, EPS, ALU.mult, ALU.add
                            ).then_inc(sem(f"norm_var_{tag}"), 1)
            rstd(tag, n, n_var[:, 0:n])

        def norm_tiles(tag):
            n, src, *_ = norm_parts(tag)
            for i in range(n):
                if n == MT:
                    V.tensor_scalar(src(i), src(i), n_y[:, i:i + 1], None, ALU.mult).then_inc(sem(f"xn_{tag}"), 1)
                    continue
                if i >= 2:
                    dve.wait_ge(*have(f"xn_t_in_psum_{tag}", i - 1))
                    if tag[:3] == "ffn":
                        dve.wait_ge(*have(f"xn_stored{tag[-1]}_{i % 2}", 16))
                V.tensor_scalar(xn[:, i % 2, :], src(i), n_y[:, i:i + 1], None, ALU.mult
                                ).then_inc(sem(f"xn_{tag}"), 1)

        def split(tag, hi_done, done):
            n, _, _, g0, hi, lo = norm_parts(tag)
            per = BANK // (n * P)
            b0 = 4 if n == MT else 0
            for k in range(KD):
                c0 = (k % per) * n * P
                dve.wait_ge(*have(hi_done, (k // per + 1) * per))
                V.scalar_tensor_tensor(out=lo[:, k, :], in0=ps[:, b0 + k // per, c0:c0 + n * P],
                                       scalar=vecs[:, g0 + k:g0 + k + 1], in1=hi[:, k, :].bitcast(fp32),
                                       op0=ALU.mult, op1=ALU.subtract).then_inc(sem(done), 1)

        def low(name, dst, src, hi):
            V.tensor_tensor(dst, src, hi.bitcast(fp32), ALU.subtract).then_inc(sem(name), 1)

        def residual(name, s, i):
            cut = slice(s * BANK, (s + 1) * BANK)
            V.tensor_tensor(h[:, i, cut], ps[:, 4 * s + i, :], h[:, i, cut], ALU.add).then_inc(sem(name), 1)

        dve.wait_ge(*have("vecs_in_psum", 2))
        V.tensor_copy(vecs[:], ps[:, 0, 0:NV]).then_inc(sem("vecs_ready"), 1)
        V.tensor_copy(taps[:].rearrange("p c t -> p (c t)"), ps[:, 1, 0:CC * TAPS]).then_inc(sem("vecs_ready"), 1)
        norm("mix0")
        norm_tiles("mix0")
        prep(2)
        split("mix0", "split_hi_mix0", "split_lo_mix0")
        prep(3)
        norm("mem0")
        norm_tiles("mem0")
        prep(5)

        dve.wait_ge(*have("gate_done", 1))
        dve.wait_ge(*have("conv_padded", 1))
        dve.wait_ge(*have("dense_used", first["sb_a"] + 2))
        V.tensor_tensor(conv_in[:, :, PAD:], ps[:, 4:8, :], conv_acc[:], ALU.mult).then_inc(sem("glu_done"), 1)
        dve.wait_ge(*have("glu_done", 1))

        tap = [0]

        def conv(n):
            for _ in range(n):
                j = tap[0]
                if j >= TAPS:
                    return
                tap[0] += 1
                for m in range(CC):
                    if j:
                        dve.wait_ge(*have("conv_taps", CC * (j - 1) + m + 1))
                        V.scalar_tensor_tensor(out=conv_acc[:, m, :], in0=conv_in[:, m, j:j + T],
                                               scalar=taps[:, m, j:j + 1], in1=conv_acc[:, m, :], op0=ALU.mult,
                                               op1=ALU.add).then_inc(sem("conv_taps"), 1)
                    else:
                        V.tensor_scalar(conv_acc[:, m, :], conv_in[:, m, 0:T], taps[:, m, 0:1],
                                        vecs[:, CONV_B + m:CONV_B + m + 1], ALU.mult, ALU.add
                                        ).then_inc(sem("conv_taps"), 1)

        prep(6)
        conv(3)
        for d in range(7, 11):
            prep(d)
            conv(4 if d < 10 else 3)
        split("mem0", "mem_split_hi0", "mem_split_lo0")
        for d in range(11, 19):
            prep(d)
            conv(1)

        def z_part(hd):
            s = hd % 2
            dve.wait_ge(*have("z_in_psum", hd + 1))
            if hd >= 2:
                dve.wait_ge(*have("heads_in_psum", hd - 1))
                dve.wait_ge(*have("sums_in_psum", hd - 1))
            else:
                dve.wait_ge(*have("dense_used", first["vx0"] + 4))
            V.tensor_tensor(zbuf[:, s, 0:512].rearrange("p (j q) -> p j q", j=TT),
                            ps[:, 4, :].rearrange("p (j q) -> p j q", j=TT),
                            causal[:].unsqueeze(1).to_broadcast([P, TT, P]), ALU.add).then_inc(sem("z_diag"), 1)
            dve.wait_ge(*have("z_diag", hd + 1))
            dve.wait_ge(*have("z_off", hd + 1))
            V.scalar_tensor_tensor(out=sbuf[:, s, :], in0=zbuf[:, s, :], scalar=-1.0, in1=zbuf[:, s, :],
                                   op0=ALU.mult, op1=ALU.min).then_inc(sem("minus_abs_z"), 1)

        def softplus(hd):
            s = hd % 2
            dve.wait_ge(*have("ln_done", hd + 1))
            V.scalar_tensor_tensor(out=sbuf[:, s, :], in0=zbuf[:, s, :], scalar=0.0, in1=sbuf[:, s, :], op0=ALU.max,
                                   op1=ALU.add).then_inc(sem("softplus"), 1)

        def log_w(hd):
            s = hd % 2
            dve.wait_ge(*have("sums_in_psum", hd + 1))
            V.tensor_tensor(zbuf[:, s, :], zbuf[:, s, :], ps[:, 0:3, :].rearrange("p k n -> p (k n)")[:, 0:ZW],
                            ALU.subtract).then_inc(sem("log_w"), 1)

        def heads_lo(pair):
            dve.wait_ge(*have("heads_hi", pair + 1))
            low("heads_lo", a_lo[:, CC + pair, :], ps[:, 3, :], a_hi[:, CC + pair, :])

        z_part(0)
        softplus(0)
        for hd in range(SB_HEADS):
            if hd + 1 < SB_HEADS:
                z_part(hd + 1)
            if hd in (2, 4, 6):
                heads_lo(hd // 2 - 1)
            if hd < 4:
                conv(2)
            if hd + 1 < SB_HEADS:
                softplus(hd + 1)
            log_w(hd)
            if hd == 0:
                prep(20)
            if hd == 4:
                assert tap[0] == TAPS
            if hd == 6:
                dve.wait_ge(*have("conv_mean", 1))
                V.scalar_tensor_tensor(out=conv_acc[:], in0=ps[:, 7, :].unsqueeze(1).to_broadcast([P, CC, T]),
                                       scalar=-1.0 / CH, in1=conv_acc[:], op0=ALU.mult, op1=ALU.add
                                       ).then_inc(sem("conv_centred"), 1)
        dve.wait_ge(*have("conv_var", 1))
        V.tensor_scalar(conv_rs[:, 0, :], ps[:, 7, :], 1.0 / CH, EPS, ALU.mult, ALU.add
                        ).then_inc(sem("conv_var_ready"), 1)
        heads_lo(3)
        dve.wait_ge(*have("conv_root", 1))
        own(V.reciprocal(conv_rs[:, 1, :], conv_rs[:, 1, :]))
        own(V.tensor_tensor(sbuf[:, 0, 0:T], conv_rs[:, 1, :], conv_rs[:, 1, :], ALU.mult))
        own(V.scalar_tensor_tensor(out=sbuf[:, 0, 0:T], in0=sbuf[:, 0, 0:T], scalar=-0.5, in1=conv_rs[:, 0, :],
                                   op0=ALU.mult, op1=ALU.mult))
        own(V.scalar_tensor_tensor(out=conv_rs[:, 1, :], in0=sbuf[:, 0, 0:T], scalar=1.5, in1=conv_rs[:, 1, :],
                                   op0=ALU.add, op1=ALU.mult))
        V.tensor_tensor(conv_acc[:], conv_acc[:], conv_rs[:, 1, :].unsqueeze(1).to_broadcast([P, CC, T]), ALU.mult
                        ).then_inc(sem("conv_normed"), 1)
        for m in range(CC):
            dve.wait_ge(*have("conv_hi", m + 1))
            low("conv_lo", a_lo[:, m, :], conv_sq[:, m, :], a_hi[:, m, :])

        def residual_stage(name, part_name, d):
            prep(d + 3)
            dve.wait_ge(*have("dense_used", d + 2))
            for i in range(TT):
                residual(part_name, 0, i)
            prep(min(d + 5, ND))
            dve.wait_ge(*have("dense_used", d + 4))
            for i in range(TT):
                residual(name, 1, i)
            prep(min(d + 6, ND))

        def cross(l):
            d = first[f"xq{l}"]
            norm(f"xa{l}")
            norm_tiles(f"xa{l}")
            split(f"xa{l}", f"split_hi_xa{l}", f"split_lo_xa{l}")
            prep(d + 6)
            for hd in range(XH + 1):
                if hd < XH:
                    dve.wait_ge(*have(f"x_scores{l}", hd + 1))
                    if hd:
                        dve.wait_ge(*have(f"x_exp{l}", TT * hd))
                    b = 2 * (hd % 2)
                    V.tensor_reduce(out=x_max[:], in_=ps[:, b:b + 2, :].rearrange("p a (i m) -> p (a i) m", m=M),
                                    axis=AX.X, op=ALU.max, negate=True).then_inc(sem(f"x_max{l}"), 1)
                if hd < XH:
                    dve.wait_ge(*have(f"x_exp{l}", TT * (hd + 1)))
                    own(V.reciprocal(x_rec[:], x_sum[:]))
                    V.tensor_tensor(xp[:, hd % 2], xp[:, hd % 2], x_rec[:].unsqueeze(2).to_broadcast([P, TT, M]),
                                    ALU.mult).then_inc(sem(f"x_probs{l}"), 1)
                if hd:
                    for c in range(2):
                        dve.wait_ge(*have(f"x_heads_hi{l}", 2 * hd - 1 + c))
                        low(f"x_heads_lo{l}", a_lo[:, 2 * hd - 2 + c, :], ps[:, 6 + c, :], a_hi[:, 2 * hd - 2 + c, :])

        def bc(ap, shape):
            return ap.to_broadcast(shape)

        def router(l):
            dve.wait_ge(*have(f"logits{l}", 1))
            dve.wait_ge(*have(f"router_loaded{l}", 64))
            own(V.tensor_tensor(lg[:], ps[:, 0, 0:TT * (NG + NE)].rearrange("p (i n) -> p i n", i=TT),
                                bc(rt_b[:].unsqueeze(1), [P, TT, NG + NE]), ALU.add))
            S4 = [P, TT, NG]
            S44 = [P, TT, NG, EPG]
            four = bc(iota4[:].unsqueeze(1), S4)

            def argmax(src, hot, top):
                own(V.tensor_reduce(out=top[:], in_=src, axis=AX.X, op=ALU.max))
                own(V.tensor_tensor(r4c[:], src, bc(top[:].unsqueeze(2), S4), ALU.is_equal))
                own(V.scalar_tensor_tensor(out=r4c[:], in0=r4c[:], scalar=-FAR, in1=four, op0=ALU.mult, op1=ALU.add))
                own(V.tensor_reduce(out=slot_f[:, 0:TT], in_=r4c[:], axis=AX.X, op=ALU.min))
                own(V.tensor_tensor(hot[:], r4c[:], bc(slot_f[:, 0:TT].unsqueeze(2), S4), ALU.is_equal))

            argmax(lg[:, :, 0:NG], oh_g, r1a)
            V.tensor_tensor(r4a[:], lg[:, :, 0:NG], bc(r1a[:].unsqueeze(2), S4), ALU.subtract
                            ).then_inc(sem(f"r_args{l}"), 1)
            experts4 = lg[:, :, NG:].rearrange("p i (g e) -> p i g e", g=NG)
            own(V.tensor_tensor(e_tmp[:], experts4, bc(oh_g[:].unsqueeze(3), S44), ALU.mult))
            own(V.tensor_reduce(out=le[:], in_=e_tmp[:].rearrange("p i g e -> p i e g"), axis=AX.X, op=ALU.add))
            dve.wait_ge(*have(f"r_exp{l}", 1))
            own(V.tensor_reduce(out=p_top[:], in_=r4b[:], axis=AX.X, op=ALU.add))
            own(V.reciprocal(p_top[:], p_top[:]))
            argmax(le[:], oh_1, r1a)
            own(V.scalar_tensor_tensor(out=le[:], in0=oh_1[:], scalar=-1e30, in1=le[:], op0=ALU.mult, op1=ALU.add))
            argmax(le[:], oh_2, gate1)
            V.tensor_tensor(r1a[:], gate1[:], r1a[:], ALU.subtract).then_inc(sem(f"r_args{l}"), 1)
            own(V.tensor_tensor(e_1[:].rearrange("p i (g e) -> p i g e", g=NG), bc(oh_g[:].unsqueeze(3), S44),
                                bc(oh_1[:].unsqueeze(2), S44), ALU.mult))
            own(V.tensor_tensor(e_2[:].rearrange("p i (g e) -> p i g e", g=NG), bc(oh_g[:].unsqueeze(3), S44),
                                bc(oh_2[:].unsqueeze(2), S44), ALU.mult))
            V.tensor_tensor(e_sum[:], e_1[:], e_2[:], ALU.add).then_inc(sem(f"assigned{l}"), 1)
            dve.wait_ge(*have(f"r_exp{l}", 2))
            own(V.tensor_scalar(r1a[:], r1b[:], 1.0, None, ALU.add))
            own(V.reciprocal(r1a[:], r1a[:]))
            own(V.tensor_tensor(gate1[:], r1a[:], p_top[:], ALU.mult))
            own(V.tensor_tensor(gate2[:], gate1[:], r1b[:], ALU.mult))
            if l == 0:
                prep(33)
            dve.wait_ge(*have(f"ranks{l}", 1))
            own(V.tensor_copy(count[:], ps[:, 1, TT * NE:(TT + 1) * NE]))
            own(V.tensor_copy(rank[:], ps[:, 1, 0:TT * NE].rearrange("p (i e) -> p i e", i=TT)))
            own(V.tensor_scalar(over[:], count[:], P + 0.5, None, ALU.is_gt))
            for n in range(2, T // P):
                own(V.scalar_tensor_tensor(out=over[:], in0=count[:], scalar=n * P + 0.5, in1=over[:],
                                           op0=ALU.is_gt, op1=ALU.add))
            own(V.memset(scan[:], 0.0))
            own(V.tensor_copy(scan[:, 0, NE:], over[:]))
            cur, step = 0, 1
            while step < NE:
                own(V.tensor_tensor(scan[:, 1 - cur, NE:], scan[:, cur, NE:], scan[:, cur, NE - step:2 * NE - step],
                                    ALU.add))
                cur, step = 1 - cur, 2 * step
            incl = scan[:, cur, NE:]
            own(V.tensor_tensor(b_hi[:], incl, over[:], ALU.subtract))
            own(V.tensor_scalar(b_hi[:], b_hi[:], float(P), float(P * (NE - 1)), ALU.mult, ALU.add))
            own(V.tensor_tensor(b_hi[:], b_hi[:], slot_lo[:], ALU.subtract))
            SE = [P, TT, NE]
            own(V.tensor_scalar(slots[:], rank[:], P - 0.5, None, ALU.is_gt))
            own(V.tensor_tensor(slots[:], slots[:], bc(b_hi[:].unsqueeze(1), SE), ALU.mult))
            own(V.tensor_tensor(slots[:], slots[:], bc(slot_lo[:].unsqueeze(1), SE), ALU.add))
            own(V.tensor_tensor(slots[:], slots[:], rank[:], ALU.add))
            for c, e_c in enumerate((e_1, e_2)):
                own(V.tensor_tensor(rank[:], slots[:], e_c[:], ALU.mult))
                own(V.tensor_reduce(out=slot_f[:, c * TT:(c + 1) * TT], in_=rank[:], axis=AX.X, op=ALU.add))
            own(V.tensor_copy(slot_i[:], slot_f[:]))
            own(V.tensor_single_scalar(row_i[:], slot_i[:], P - 1, ALU.bitwise_and))
            own(V.tensor_single_scalar(blk_i[:], slot_i[:], 7, ALU.logical_shift_right))
            own(V.tensor_copy(row_f[:], row_i[:]))
            own(V.tensor_copy(blk_f[:], blk_i[:]))
            J = 2 * TT
            V.tensor_tensor(slot_hot[:], bc(iota_p[:].unsqueeze(1), [P, J, P]), bc(row_f[:].unsqueeze(2), [P, J, P]),
                            ALU.is_equal).then_inc(sem(f"hots{l}"), 1)
            own(V.tensor_tensor(blk_hot[:], bc(iota_b[:].unsqueeze(1), [P, J, NB]), bc(blk_f[:].unsqueeze(2), [P, J, NB]),
                                ALU.is_equal))
            V.tensor_tensor(blk_hot[:].rearrange("p (c i) b -> p c i b", c=2),
                            blk_hot[:].rearrange("p (c i) b -> p c i b", c=2),
                            bc(tok_no[:].unsqueeze(1).unsqueeze(3), [P, 2, TT, NB]), ALU.mult
                            ).then_inc(sem(f"hots{l}"), 1)
            own(V.tensor_tensor(own_cmp[:], bc(incl.unsqueeze(1), [P, OVERFLOW, NE]),
                                bc(iota_b[:, 0:OVERFLOW].unsqueeze(2), [P, OVERFLOW, NE]), ALU.is_le))
            own(V.tensor_reduce(out=own_f[:], in_=own_cmp[:], axis=AX.X, op=ALU.add))
            own(V.tensor_scalar(own_f[:], own_f[:], float(NE - 1), None, ALU.min))
            own(V.tensor_copy(own_i[:], own_f[:]))
            V.tensor_copy(nov_i[:], incl[:, NE - 1:NE]).then_inc(sem(f"overflow_known{l}"), 1)
            dve.wait_ge(*have(f"table{l}", 1))
            own(V.tensor_copy(tok_f[:], ps[:, 2, 0:NB]))
            own(V.tensor_scalar(tok_e[:], tok_f[:], 0.0, FAR, ALU.is_equal, ALU.mult))
            own(V.scalar_tensor_tensor(out=tok_f[:], in0=tok_f[:], scalar=-1.0, in1=tok_e[:], op0=ALU.add,
                                       op1=ALU.add))
            V.tensor_copy(tok_i[:], tok_f[:]).then_inc(sem(f"table_ready{l}"), 1)

        def experts(l):
            gain = vecs[:, FFN_G + l * KD:FFN_G + (l + 1) * KD]
            norm(f"ffn{l}")
            norm_tiles(f"ffn{l}")
            dve.wait_ge(*have(f"xn_t_in_psum_ffn{l}", TT))
            for k in range(KD // 2, KD):
                V.tensor_scalar(a_full[:, k, :], ps[:, k, :], gain[:, k:k + 1], None, ALU.mult
                                ).then_inc(sem(f"a_full{l}"), 1)
            if l == 0:
                norm("mem1")
                norm_tiles("mem1")
                prep(31)
                split("mem1", "mem_split_hi1", "mem_split_lo1")
            router(l)
            if l == 0:
                prep(34)

            def rows_out(count, dst, name):
                V.tensor_tensor(dst, ps[:, 0:2, :].rearrange("p a (b n) -> p (a b) n", n=P),
                                bc(gain.unsqueeze(2), [P, KD, P]), ALU.mult).then_inc(sem(name), 1)

            dve.wait_ge(*have(f"xs_t_in_psum{l}", 1))
            rows_out(0, xs_t[:, 0], f"xs_t_ready{l}")

            def block_of(i, e, first_pair, last_pair):
                b = 2 * i + e
                if not (last_pair and e == 1):
                    dve.wait_ge(*have(f"xs_t_in_psum{l}", b + 2))
                    rows_out(b + 1, xs_t[:, 1 - e], f"xs_t_ready{l}")
                dve.wait_ge(*have(f"silu{l}", b + 1))
                V.tensor_tensor(hid[:, e, :], ps[:, 2 + e, FE:2 * FE], silu_g[:, e, :], ALU.mult
                                ).then_inc(sem(f"hidden{l}"), 1)
                dve.wait_ge(*have(f"expert_w_used{l}", 3 * b + 3))
                if not first_pair:
                    dve.wait_ge(*have(f"y_stored{l}_{e}", 16 * i))
                V.tensor_copy(y_sb[:, e, BANK:], ps[:, 6, :]).then_inc(sem(f"y_right{l}"), 1)

            for e in range(2):
                block_of(0, e, True, False)
            with dve.Fori(1, NE // 2 - 1) as i:
                for e in range(2):
                    block_of(i, e, False, False)
            for e in range(2):
                block_of(NE // 2 - 1, e, False, True)

            dve.wait_ge(*have(f"y_stored{l}_0", 16 * (NE // 2)))
            n_over = dve.value_load(nov_i[0:1, 0:1])
            with dve.If(n_over > 0):
                with dve.Fori(0, OVERFLOW) as j:
                    V.tensor_copy(idx_c[:], tok_i[:, bass.ds(j + NE, 1)]).then_inc(sem(f"over_index{l}"), 1)
                    dve.wait_ge(*have(f"over_x_t_in_psum{l}", j + 1))
                    rows_out(0, xs_t[:, 0], f"over_x_t{l}")
                    dve.wait_ge(*have(f"over_silu{l}", j + 1))
                    V.tensor_tensor(hid[:, 0, :], ps[:, 2, FE:2 * FE], silu_g[:, 0, :], ALU.mult
                                    ).then_inc(sem(f"over_hidden{l}"), 1)
                    dve.wait_ge(*have(f"over_down{l}", j + 1))
                    V.tensor_copy(y_sb[:, 0, BANK:], ps[:, 6, :]).then_inc(sem(f"over_y{l}"), 1)
                    dve.wait_ge(*have(f"over_stored{l}", 16 * j + 16))

            for j in range(2 * TT):
                i, c = j // 2, j % 2
                if l == 0 and j % 2 == 0:
                    prep(36 + j // 2)
                dve.wait_ge(*have(f"y_gathered{l}_{j % 4}", 16 * (j // 4 + 1)))
                if c:
                    dve.wait_ge(*have(f"combined{l}", j))
                V.scalar_tensor_tensor(out=h[:, i, :], in0=y_back[:, j % 4, :],
                                       scalar=(gate2 if c else gate1)[:, i:i + 1], in1=h[:, i, :],
                                       op0=ALU.mult, op1=ALU.add).then_inc(sem(f"combined{l}"), 1)

        residual_stage("h_xa0", "h_part_xa0", first["mix_out0"])
        cross(0)
        residual_stage("h_ffn0", "h_part_ffn0", first["xo0"])
        experts(0)

        prep(40)
        norm("mix1")
        norm_tiles("mix1")
        split("mix1", "split_hi_mix1", "split_lo_mix1")
        d = first["c_v"]
        prep(d + 6)
        for s in range(2):
            dve.wait_ge(*have("v_gelu", s + 1))
            for i in range(TT):
                V.bn_stats(v_st[:, i, s, :], v_c[:, i, s * BANK:(s + 1) * BANK]).then_inc(sem("v_stats"), 1)
        for i in range(TT):
            dve.wait_ge(*have("v_stats", TT + i + 1))
            own(V.bn_aggr(v_mv[:, i, :], v_st[:, i].rearrange("p a b -> p (a b)")))
        V.tensor_scalar(n_var[:], v_mv[:, :, 1], EPS, None, ALU.add).then_inc(sem("norm_var_v"), 1)
        dve.wait_ge(*have("norm_var_v", 1))
        rstd("v", TT, n_var[:])
        prep(d + 7)
        dve.wait_ge(*have("vnorm_loaded", 32))
        for i in range(TT):
            V.tensor_scalar(v_c[:, i, :], v_c[:, i, :], v_mv[:, i, 0:1], n_y[:, i:i + 1], ALU.subtract, ALU.mult
                            ).then_inc(sem("v_centred"), 1)
        for i in range(TT):
            dve.wait_ge(*have("v_centred", i + 1))
            V.tensor_tensor(v_c[:, i, :], v_c[:, i, :], vg_b[:], ALU.mult).then_inc(sem("v_gained"), 1)
        prep(d + 8)
        for i in range(TT):
            dve.wait_ge(*have("v_gained", i + 1))
            V.tensor_tensor(v_c[:, i, :], v_c[:, i, :], vb_b[:], ALU.add).then_inc(sem("v_normed"), 1)
        prep(d + 10)
        dve.wait_ge(*have("bs_loaded", 16))
        for g in range(GM):
            dve.wait_ge(*have("mixed_in_psum", g + 1))
            m3 = ps[:, g, :].rearrange("p (c t) -> p c t", c=TT)
            own(V.tensor_tensor(m3, m3, bs_b[:, g, :].unsqueeze(1).to_broadcast([P, TT, P]), ALU.add))
            V.tensor_tensor(u_c[:, g, :], ps[:, g, :], u_c[:, g, :], ALU.mult).then_inc(sem("gated"), 1)
        residual_stage("h_xa1", "h_part_xa1", first["mix_out1"])
        cross(1)
        residual_stage("h_ffn1", "h_part_ffn1", first["xo1"])
        experts(1)
        norm("fin1")
        dve.wait_ge(*have("final_gain_loaded", 16))
        for i in range(TT):
            if i >= 2:
                dve.wait_ge(*have(f"out_stored{i % 2}", 16))
            V.scalar_tensor_tensor(out=xn[:, i % 2, :], in0=h[:, i, :], scalar=n_y[:, i:i + 1], in1=fg_b[:],
                                   op0=ALU.mult, op1=ALU.mult).then_inc(sem("out_ready"), 1)

    ctx.close()


_INS = ["x", "mem", "mem_norm_g", "norm_mix", "norm_xa", "norm_ffn", "final_norm_g",
        "ab_w_in", "ab_conv_w", "ab_conv_b", "ab_cnorm_g", "ab_cnorm_b", "ab_w_out",
        "c_w_in", "c_vnorm_g", "c_vnorm_b", "c_ws", "c_bs", "c_w_out",
        "xa_wq", "xa_wk", "xa_wv", "xa_wo", "rt_wg", "rt_bg", "rt_we", "rt_be",
        "ex_w_gate", "ex_w_up", "ex_w_down"]


def kernel(**inputs):
    import numpy as _np
    import concourse.bacc as _bacc
    from concourse import mybir as _mybir
    from concourse.bass_utils import run_bass_kernel_spmd as _run

    nc = _bacc.Bacc("TRN2", target_bir_lowering=False, num_devices=1)
    arrays, args = {}, []
    for name in _INS:
        a = _np.ascontiguousarray(inputs[name])
        arrays[f"in_{name}"] = a
        args.append(nc.dram_tensor(f"in_{name}", a.shape, _mybir.dt.from_np(a.dtype), kind="ExternalInput").ap())
    shape = tuple(inputs["x"].shape)
    args.append(nc.dram_tensor("out_0", shape, _mybir.dt.float32, kind="ExternalOutput").ap())
    trunk_program(nc, *args)
    return _run(nc, [arrays], core_ids=[0]).results[0]["out_0"]
```

```python
import concourse.bass as bass
from concourse import mybir
from contextlib import ExitStack


def trunk_program(nc, x, mem, mem_norm_g, norm_mix, norm_xa, norm_ffn, final_norm_g,
                  ab_w_in, ab_conv_w, ab_conv_b, ab_cnorm_g, ab_cnorm_b, ab_w_out,
                  c_w_in, c_vnorm_g, c_vnorm_b, c_ws, c_bs, c_w_out,
                  xa_wq, xa_wk, xa_wv, xa_wo, rt_wg, rt_bg, rt_we, rt_be,
                  ex_w_gate, ex_w_up, ex_w_down, out):
    fp32, fp32r, i32 = mybir.dt.float32, mybir.dt.float32r, mybir.dt.int32
    ALU, ACT, AX = mybir.AluOpType, mybir.ActivationFunctionType, mybir.AxisListType

    P = 128
    _, T, D = x.shape
    M = mem.shape[1]
    EPS = 1e-6
    TT, KD, MT = T // P, D // P, M // P
    BANK = 512
    NL = norm_mix.shape[0]
    TAPS, CH = ab_conv_w.shape[1], ab_conv_w.shape[2]
    CC = CH // P
    PAD = TAPS - 1
    SB_HEADS, SB_DH = 8, 64
    XH = 4
    XD = D // XH
    NG, EPG = rt_wg.shape[2], rt_we.shape[2] // rt_wg.shape[2]
    NE = NG * EPG
    FE = ex_w_gate.shape[3]
    OVERFLOW = (2 * T) // (P + 1)
    NB = NE + OVERFLOW + 1
    GC = 4
    RING, SPLIT = 6, 3
    GM = c_ws.shape[1]
    FAR = 1000.0

    ctx = ExitStack()
    sems, place = {}, {}

    def family(shared, members):
        base = 0
        for name, n in members:
            place[name] = (shared, base)
            base += n

    def sem(name):
        shared = place.get(name, (name, 0))[0]
        if shared not in sems:
            sems[shared] = ctx.enter_context(nc.semaphore(shared))
        return sems[shared]

    def have(name, n):
        return sem(name), n + place.get(name, (name, 0))[1]

    for name, n in (("a_full", TT), ("assigned", 1), ("combined", 2 * TT), ("xs_hi", NE),
                    ("hidden", NE), ("hidden_hi", NE), ("hidden_lo", NE), ("hidden_t_in_psum", NE), ("hots", 2), ("logits", TT),
                    ("overflow_known", 1), ("r_exp", 2), ("r_args", 2), ("ranks", 1),
                    ("silu", NE), ("table", 1), ("table_ready", 1),
                    ("x_exp", TT * XH), ("x_heads_hi", KD), ("x_heads_in_psum", XH), ("x_heads_lo", KD),
                    ("x_max", XH), ("x_probs", XH), ("x_probs_t", XH), ("x_probs_t_in_psum", XH), ("x_scores", XH),
                    ("xq_ready", 2), ("xs_cleared", 1), ("xs_t_in_psum", NE), ("xs_lo", NE), ("down_lo_pool", NE), ("xn_gained", TT), ("y_left", NE),
                    ("y_right", NE), ("kx_ready", 2), ("vx_ready", 2), ("mem_t_in_psum", MT),
                    ("mem_split_hi", KD), ("mem_split_lo", KD), ("h_xa", TT), ("h_ffn", TT), ("h_part_xa", TT),
                    ("h_part_ffn", TT), ("tile_xa", TT - 1), ("tile_ffn", TT - 1)):
        family(name, [(f"{name}{l}", n) for l in range(NL)])
    for name, slots_of, n in (("gathered", 2, 8 * NE), ("xn_stored", 2, 8 * TT), ("y_stored", 2, 8 * NE),
                              ("y_gathered", 4, 8 * TT)):
        for s in range(slots_of):
            family(f"{name}_{s}", [(f"{name}{l}_{s}", n) for l in range(NL)])
    NORMS = [("mix0", TT), ("mem0", MT), ("xa0", TT), ("mem1", MT), ("ffn0", TT), ("mix1", TT), ("v", 0),
             ("xa1", TT), ("ffn1", TT), ("fin1", TT)]
    family("squares_act", [(f"squares_act_{tag}", n if tag[:3] == "ffn" else n // 2) for tag, n in NORMS])
    family("norm_var", [(f"norm_var_{tag}", 1) for tag, n in NORMS])
    family("norm_root", [(f"norm_root_{tag}", 1) for tag, n in NORMS])
    LATE = ("xa0", "mix1", "xa1")
    family("xn", [(f"xn_{tag}", n) for tag, n in NORMS if tag not in LATE])
    family("xn_t_in_psum", [(f"xn_t_in_psum_{tag}", 2 if tag in LATE else n) for tag, n in NORMS if tag[:3] != "mem"])
    for name in ("diag_ready", "factors_in_psum", "factors_ready"):
        family(name, [(f"{name}_{tag}", 1) for tag in LATE])
    family("mixer0_act", [("gate_done", 1), ("q_ready", 1), ("k_ready", 1), ("v_ready", 1)])
    family("mixer1_act", [("ws_t_ready", 1), ("v_gelu", 2 * TT), ("u_gelu", 2), ("gated_hi", KD)])
    family("mixer1_dve", [("v_stats", 2 * TT), ("v_centred", TT), ("v_gained", TT), ("v_normed", TT),
                          ("u_scaled", 2), ("gated", KD)])
    family("mixer1_pe", [("ws_t_in_psum", 1), ("mixed_in_psum", KD)])
    for part in ("split_hi", "split_lo"):
        family(part, [(f"{part}_{tag}", KD) for tag in ("mix0", "xa0", "mix1", "xa1")])

    BASE = 16512
    K = 1024

    def at(name, shape, dt, offset):
        return nc.alloc_sbuf_tensor_at(name, shape, dt, offset=BASE + int(offset))

    raw = at("raw", [P, RING, GC * BANK], fp32, 0)
    w_lo = at("w_lo", [P, RING, GC * BANK], fp32r, 0)
    w_hi = at("w_hi", [P, SPLIT, GC * BANK], fp32r, 48 * K)
    h = at("h", [P, TT, D], fp32, 80 * K)
    a_hi = at("a_hi", [P, KD, T], fp32r, 96 * K)
    a_lo = at("a_lo", [P, KD, T], fp32r, 112 * K)
    mem_hi = at("mem_hi", [P, KD, M], fp32r, 128 * K)
    mem_lo = at("mem_lo", [P, KD, M], fp32r, 136 * K)
    xn = at("xn", [P, 2, D], fp32, 148 * K)
    xn_more = at("xn_more", [P, 2, D], fp32, 120 * K)
    mem_tok = at("mem_tok", [P, MT, D], fp32, 180 * K)
    q_t = at("q_t", [P, CC, T], fp32, 148 * K)
    k_t = at("k_t", [P, CC, T], fp32, 156 * K)
    v_s = at("v_s", [P, TT, CH], fp32, 164 * K)
    ZW = 1280
    zbuf = at("zbuf", [P, 2, ZW], fp32, 128 * K)
    sbuf = at("sbuf", [P, 2, ZW], fp32, 138 * K)
    CIN_W = T + PAD
    conv_in = at("conv_in", [P, CC, CIN_W], fp32, 188 * K)
    conv_sq = at("conv_sq", [P, CC, T], fp32, 188 * K)
    conv_acc = at("conv_acc", [P, CC, T], fp32, 196.5 * K)
    conv_rs = at("conv_rs", [P, 2, T], fp32, 148 * K)
    conv_t = at("conv_t", [P, T], fp32, 156 * K)
    diag = at("diag", [P, TT, P], fp32, 136 * K)
    factors = at("factors", [P, T], fp32, 134 * K)
    kx = at("kx", [P, KD, M], fp32, 172 * K)
    vx = at("vx", [P, MT, D], fp32, 180 * K)
    xq = at("xq", [P, KD, T], fp32, 148 * K)
    xp = at("xp", [P, 2, TT, M], fp32, 188 * K)
    xpt = at("xpt", [P, 2, MT, T], fp32, 164 * K)
    v_c = at("v_c", [P, TT, D], fp32, 148 * K)
    u_c = at("u_c", [P, KD, T], fp32, 188 * K)
    vg_b = at("vg_b", [P, D], fp32, 164 * K)
    vb_b = at("vb_b", [P, D], fp32, 168 * K)
    ws_in = at("ws_in", [P, GM, P], fp32, 160 * K)
    ws_t = at("ws_t", [P, GM, P], fp32, 144 * K)
    bs_b = at("bs_b", [P, GM, P], fp32, 128 * K)
    a_full = at("a_full", [P, KD, T], fp32, 96 * K)
    xs = at("xs", [P, 2, D], fp32, 112 * K)
    gain_b = at("gain_b", [P, D], fp32, 76 * K)
    xg = at("xg", [P, 2, D], fp32, 164 * K)
    xs_hi = at("xs_hi", [P, 2, KD, P], fp32r, 164 * K)
    xs_lo = at("xs_lo", [P, 2, KD, P], fp32r, 96 * K)
    xs_full = at("xs_full", [P, KD, P], fp32, 164 * K)
    y_sb = at("y_sb", [P, 2, D], fp32, 188 * K)
    silu_g = at("silu_g", [P, 2, FE], fp32, 196 * K)
    hid = at("hid", [P, 2, FE], fp32, 198 * K)
    hid_hi = at("hid_hi", [P, 2, 2, P], fp32r, 200 * K)
    hid_lo = at("hid_lo", [P, 2, 2, P], fp32r, 160 * K)
    hid_full = at("hid_full", [P, 2, P], fp32, 200 * K)
    y_back = at("y_back", [P, 4, D], fp32, 96 * K)
    over_w = [at(f"over_w{i}", [P, GC * BANK], fp32, o * K) for i, o in enumerate((96, 104, 148))]
    slot_hot = at("slot_hot", [P, 2 * TT, P], fp32r, 188 * K)
    before_f = at("before_f", [P, P], fp32, 202 * K)
    before = at("before", [P, P], fp32r, 72 * K)
    ones_r = at("ones_r", [P, P], fp32r, 72.5 * K)
    iota_p = at("iota_p", [P, P], fp32, 73 * K)
    rt_w = at("rt_w", [P, NL, KD, NG + NE], fp32, 73.5 * K)
    rt_b = at("rt_b", [P, NL, NG + NE], fp32, 75 * K)
    rt_off = [144 * K]

    def small(name, shape, dt=fp32):
        n = 1
        for s in shape:
            n *= s
        if rt_off[0] < 148 * K < rt_off[0] + 4 * n:
            rt_off[0] = 156 * K
        assert rt_off[0] + 4 * n <= 160 * K
        t = at(name, [P] + shape, dt, rt_off[0])
        rt_off[0] += (4 * n + 31) // 32 * 32
        return t

    lg = small("lg", [TT, NG + NE])
    r4a, r4b, r4c = (small(f"r4_{c}", [TT, NG]) for c in "abc")
    oh_g, oh_1, oh_2 = (small(n, [TT, NG]) for n in ("oh_g", "oh_1", "oh_2"))
    le = small("le", [TT, EPG])
    r1a, r1b, p_top, gate1, gate2 = (small(n, [TT]) for n in ("r1a", "r1b", "p_top", "gate1", "gate2"))
    e_1, e_2, rank, slots = (small(n, [TT, NE]) for n in ("e_1", "e_2", "rank", "slots"))
    e_sum = small("e_sum", [TT, NE], fp32r)
    e_tmp = small("e_tmp", [TT, NG, EPG])
    count, over, b_hi = (small(n, [NE]) for n in ("count", "over", "b_hi"))
    scan = small("scan", [2, 2 * NE])
    slot_f = small("slot_f", [2 * TT])
    slot_i = small("slot_i", [2 * TT], i32)
    row_i, blk_i = small("row_i", [2 * TT], i32), small("blk_i", [2 * TT], i32)
    row_f, blk_f = small("row_f", [2 * TT]), small("blk_f", [2 * TT])
    blk_hot = small("blk_hot", [2 * TT, NB])
    tok_hot = small("tok_hot", [2 * TT, NB], fp32r)
    tok_f, tok_e = small("tok_f", [NB]), small("tok_e", [NB])
    tok_i = small("tok_i", [NB], i32)
    own_cmp = small("own_cmp", [OVERFLOW, NE])
    own_f = small("own_f", [OVERFLOW])
    own_i = small("own_i", [OVERFLOW], i32)
    nov_i = small("nov_i", [1], i32)
    idx_c = small("idx_c", [1], i32)

    c_pool = at("constants", [P, (229344 - BASE - 209408) // 4], fp32, 204.5 * K)
    c_off = [0]

    def const(name, shape):
        n = 1
        for s in shape:
            n *= s
        t = c_pool[:, c_off[0]:c_off[0] + n]
        c_off[0] += n
        assert c_off[0] <= c_pool.shape[1], c_off
        return t if len(shape) == 1 else t.rearrange("p (a b) -> p a b", a=shape[0])

    ident, ones, tri, causal = (const(n, [P]) for n in ("ident", "ones", "tri", "causal"))
    NV = (1 + 3 * NL) * KD + 3 * CC
    vecs = const("vecs", [NV])
    taps = const("taps", [CC, TAPS])
    iota4, iota_b, slot_lo, tok_no = (const(n, s) for n, s in (
        ("iota4", [NG]), ("iota_b", [NB]), ("slot_lo", [NE]), ("tok_no", [TT])))
    n_ss, n_var, n_y, n_t = (const(n, [4]) for n in ("n_ss", "n_var", "n_y", "n_t"))
    x_max, x_sum, x_rec = (const(n, [TT]) for n in ("x_max", "x_sum", "x_rec"))
    v_st, v_mv = at("v_st", [P, TT, 2, 6], fp32, 132 * K), at("v_mv", [P, TT, 2], fp32, 132 * K + 256)
    vec_in = at("vec_in", [P, P], fp32, 188 * K)
    tap_in = at("tap_in", [P, CH], fp32, 189 * K)
    fg_b = at("fg_b", [P, D], fp32, 164 * K)

    MEM_G, MIX_G, XA_G, FFN_G = 0, KD, (1 + NL) * KD, (1 + 2 * NL) * KD
    CONV_B, CN_G, CN_B = (1 + 3 * NL) * KD, (1 + 3 * NL) * KD + CC, (1 + 3 * NL) * KD + 2 * CC

    ps = ctx.enter_context(nc.psum_tensor("ps", [P, 8, BANK], fp32))

    xn_dram = [nc.dram_tensor(f"xn_dram{l}", [T, D], fp32, kind="Internal").ap() for l in range(NL)]
    ys_dram = [nc.dram_tensor(f"ys_dram{l}", [(NB - 1) * P, D], fp32, kind="Internal").ap() for l in range(NL)]

    def slabs(w, cols):
        return [w[:, c:c + BANK] for c in cols]

    stream, ring_pos, ring_count, first, slot_total = [], [], [], {}, [0] * RING

    def push(what, arrivals):
        slot = len(stream) % RING
        slot_total[slot] += 16 * arrivals
        ring_pos.append(slot)
        ring_count.append(slot_total[slot])
        stream.append(what)

    def plan(name, sl):
        first[name] = len(stream)
        for w in sl:
            for half in range(2):
                push((w[half * GC * P:(half + 1) * GC * P, :].rearrange("(k p) n -> p k n", p=P),), 1)

    def plan_experts(l):
        first[f"moe{l}"] = len(stream)
        for b in range(NE + 1):
            for e, part in ((b, 0), (b, 1), (b - 1, 2)):
                if 0 <= e < NE:
                    push((l, e, part), 2 if part < 2 else 1)

    def entry(l, g, i):
        n0 = first[f"moe{l}"]
        if isinstance(i, int):
            n = n0 + 6 * i + g
            return n, ring_pos[n], ring_count[n], n % SPLIT
        n = n0 + 6 + g
        step = ring_count[n + 6] - ring_count[n]
        return 6 * i + (n0 + g), ring_pos[n], step * i + (ring_count[n] - step), n % SPLIT

    cols = lambda lo, n: range(lo, lo + n * BANK, BANK)
    plan("sb_gate", slabs(ab_w_in[0], [BANK]))
    plan("sb_a", slabs(ab_w_in[0], [0]))
    plan("sb_q", slabs(ab_w_in[0], [2 * BANK]))
    plan("sb_k", slabs(ab_w_in[0], [3 * BANK]))
    plan("sb_v", slabs(ab_w_in[0], [4 * BANK]))
    plan("kx0", slabs(xa_wk[0], cols(0, 2)))
    plan("vx0", slabs(xa_wv[0], cols(0, 2)))
    plan("mix_out0", slabs(ab_w_out[0], cols(0, 2)))
    plan("xq0", slabs(xa_wq[0], cols(0, 2)))
    plan("xo0", slabs(xa_wo[0], cols(0, 2)))
    plan("kx1", slabs(xa_wk[1], cols(0, 2)))
    plan("vx1", slabs(xa_wv[1], cols(0, 2)))
    plan_experts(0)
    plan("c_v", slabs(c_w_in[0], cols(D, 2)))
    plan("c_u", slabs(c_w_in[0], cols(0, 2)))
    plan("mix_out1", slabs(c_w_out[0], cols(0, 2)))
    plan("xq1", slabs(xa_wq[1], cols(0, 2)))
    plan("xo1", slabs(xa_wo[1], cols(0, 2)))
    plan_experts(1)

    def expert_views(l, e, part):
        pick = (lambda w: w[l, bass.ds(e, 1)]) if not isinstance(e, int) else (lambda w: w[l, e:e + 1])
        if part < 2:
            rows = slice(part * GC * P, (part + 1) * GC * P)
            return [pick(w)[:, rows, :].rearrange("o (k p) n -> p (o k) n", p=P) for w in (ex_w_gate, ex_w_up)]
        return [pick(ex_w_down).rearrange("o (k p) n -> p (o k) n", p=P)]

    def load_expert(eng, l, e, part, dst, done):
        views = expert_views(l, e, part)
        if part < 2:
            d4 = dst.rearrange("p (k n) -> p k n", k=GC)
            eng.dma_start(d4[:, :, 0:FE], views[0]).then_inc(done, 16)
            eng.dma_start(d4[:, :, FE:2 * FE], views[1]).then_inc(done, 16)
        else:
            eng.dma_start(dst.rearrange("p (k n) -> p k n", k=2), views[0]).then_inc(done, 16)

    def norm_parts(tag):
        if tag.startswith("mem"):
            return MT, (lambda i: mem_tok[:, i, :]), "mem_loaded", MEM_G, mem_hi, mem_lo
        base = {"mix": MIX_G, "xa": XA_G, "ffn": FFN_G, "fin": 0}[tag[:-1]]
        l = int(tag[-1])
        return TT, (lambda i: h[:, i, :]), f"h_{tag}", base + l * KD, a_hi, a_lo

    def xn_tile(i):
        return xn[:, i, :] if i < 2 else xn_more[:, i - 2, :]

    def source_ready(eng, tag, i):
        _, _, name, *_ = norm_parts(tag)
        if tag == "mix0":
            eng.wait_ge(*have(f"x_loaded{i}", 16))
        elif tag.startswith("mem"):
            eng.wait_ge(*have(f"mem_loaded{tag[-1]}", 16))
            if tag == "mem1":
                eng.wait_ge(*have("x_scores0", XH))
        elif tag in ("mix1", "fin1"):
            eng.wait_ge(*have(f"combined{0 if tag == 'mix1' else 1}", 2 * i + 2))
        else:
            eng.wait_ge(*have(name, i + 1))

    OFF = {0: 512, 2: 512 + 384, 1: 1024}

    block = ctx.enter_context(nc.Block())

    @block.sync
    def _(sp):
        for i in range(TT):
            sp.dma_start(h[:, i, :], x[0, i * P:(i + 1) * P, :]).then_inc(sem(f"x_loaded{i}"), 16)
        sp.wait_ge(*have("vecs_loaded", 16 * 8))

        def load(n):
            if n >= RING:
                sp.wait_ge(*have("w_used", n - RING + 1))
            dst, done = raw[:, n % RING, :], sem(f"raw_loaded{n % RING}")
            if len(stream[n]) == 1:
                sp.dma_start(dst.rearrange("p (k n) -> p k n", k=GC), stream[n][0]).then_inc(done, 16)
            else:
                load_expert(sp, *stream[n], dst, done)

        def load_experts(l):
            for n in range(first[f"moe{l}"], first[f"moe{l}"] + 5):
                load(n)
            with sp.Fori(1, NE // 2) as i:
                for g, (e, part) in enumerate(((0, 0), (0, 1), (-1, 2), (1, 0), (1, 1), (0, 2)), -1):
                    n, slot, _, _ = entry(l, g, i)
                    sp.wait_ge(*have("w_used", n - (RING - 1)))
                    load_expert(sp, l, 2 * i + e, part, raw[:, slot, :], sem(f"raw_loaded{slot}"))
            load(first[f"moe{l}"] + 3 * NE - 1)

        for n in range(first["moe0"]):
            load(n)
        load_experts(0)
        for n in range(first["c_v"], first["moe1"]):
            load(n)
        load_experts(1)
        for i in range(TT):
            sp.wait_ge(*have("out_ready", i + 1))
            sp.dma_start(out[0, i * P:(i + 1) * P, :], xn[:, i % 2, :]).then_inc(sem(f"out_stored{i % 2}"), 16)
        for i in range(2):
            sp.wait_ge(*have(f"out_stored{i}", 16 * (TT // 2)))

    @block.gpsimd
    def _(pool):
        pool_done = sem("pool_steps")
        n_own = [0]

        def own(ins):
            n_own[0] += 1
            ins.then_inc(pool_done, 1)
            pool.wait_ge(pool_done, n_own[0])

        last_row = pool.to_reg(T - 1)

        nc.gpsimd.memset(ones[:], 1.0).then_inc(sem("consts"), 1)
        own(nc.gpsimd.memset(ident[:], 1.0))
        nc.gpsimd.affine_select(out=ident[:], in_=ident[:], pattern=[[-1, P]], compare_op=ALU.is_equal,
                                fill=0.0, base=0, channel_multiplier=1).then_inc(sem("consts"), 1)
        own(nc.gpsimd.memset(tri[:], 1.0))
        nc.gpsimd.affine_select(out=tri[:], in_=tri[:], pattern=[[-1, P]], compare_op=ALU.is_ge,
                                fill=0.0, base=0, channel_multiplier=1).then_inc(sem("consts"), 1)
        own(nc.gpsimd.memset(causal[:], 0.0))
        nc.gpsimd.affine_select(out=causal[:], in_=causal[:], pattern=[[1, P]], compare_op=ALU.is_gt,
                                fill=-1e30, base=0, channel_multiplier=-1).then_inc(sem("consts"), 1)
        for t, pattern, base, ch in ((iota4, [[1, NG]], 0, 0), (iota_b, [[1, NB]], 0, 0),
                                     (slot_lo, [[P, NE]], 0, 0), (tok_no, [[P, TT]], 1, 1)):
            nc.gpsimd.iota(t[:], pattern, base=base, channel_multiplier=ch,
                           allow_small_or_imprecise_dtypes=True).then_inc(sem("consts"), 1)
        own(nc.gpsimd.memset(before_f[:], 1.0))
        nc.gpsimd.affine_select(out=before_f[:], in_=before_f[:], pattern=[[1, P]], compare_op=ALU.is_gt,
                                fill=0.0, base=0, channel_multiplier=-1).then_inc(sem("router_consts"), 1)
        nc.gpsimd.iota(iota_p[:], [[1, P]], base=0, channel_multiplier=0,
                       allow_small_or_imprecise_dtypes=True).then_inc(sem("router_consts"), 1)
        with nc.allow_non_contiguous_dma(reason="router weights are narrow"):
            for l in range(NL):
                pool.dma_start(rt_w[:, l, :, 0:NG], rt_wg[l].rearrange("(k p) n -> p k n", p=P)
                               ).then_inc(sem("router_loaded"), 16)
                pool.dma_start(rt_w[:, l, :, NG:], rt_we[l].rearrange("(k p) n -> p k n", p=P)
                               ).then_inc(sem("router_loaded"), 16)
                pool.dma_start(rt_b[:, l, 0:NG], rt_bg[l:l + 1, :].to_broadcast([P, NG])
                               ).then_inc(sem("router_loaded"), 16)
                pool.dma_start(rt_b[:, l, NG:], rt_be[l:l + 1, :].to_broadcast([P, NE])
                               ).then_inc(sem("router_loaded"), 16)
        pool.wait_ge(*have("vecs_ready", 2))
        nc.gpsimd.memset(conv_in[:, :, 0:PAD], 0.0).then_inc(sem("conv_padded"), 1)

        def gather_results(l, blocks):
            for j in range(2 * TT):
                if j >= 4:
                    pool.wait_ge(*have(f"combined{l}", j - 3))
                col = (j % 2) * TT + j // 2
                pool.indirect_dma_start(out=y_back[:, j % 4, :], out_offset=None, in_=ys_dram[l][0:blocks * P, :],
                                        in_offset=bass.IndirectOffsetOnAxis(ap=slot_i[:, col:col + 1], axis=0)
                                        ).then_inc(sem(f"y_gathered{l}_{j % 4}"), 16)

        def moe(l):
            pool.dma_start(gain_b[:], norm_ffn[l:l + 1, :].to_broadcast([P, D])).then_inc(sem(f"gain_loaded{l}"), 16)
            if l == 0:
                pool.wait_ge(*have("x_heads_in_psum0", XH))
                pool.dma_start(mem_tok[:], mem[0].rearrange("(i p) d -> p i d", p=P)
                               ).then_inc(sem("mem_loaded1"), 16)
            pool.wait_ge(*have(f"h_ffn{l}", 1))
            nc.gpsimd.memset(xs[:], 0.0).then_inc(sem(f"xs_cleared{l}"), 1)
            pool.wait_ge(*have(f"gain_loaded{l}", 16))
            for i in range(TT):
                pool.wait_ge(*have(f"xn_ffn{l}", i + 1))
                if i >= 2:
                    pool.wait_ge(*have(f"xn_stored{l}_{i % 2}", 16))
                nc.gpsimd.tensor_tensor(xg[:, i % 2, :], xn_tile(i), gain_b[:], ALU.mult
                                        ).then_inc(sem(f"xn_gained{l}"), 1)
                pool.wait_ge(*have(f"xn_gained{l}", i + 1))
                pool.dma_start(xn_dram[l][i * P:(i + 1) * P, :], xg[:, i % 2, :]
                               ).then_inc(sem(f"xn_stored{l}_{i % 2}"), 16)
            pool.wait_ge(*have(f"xs_cleared{l}", 1))
            for s in range(2):
                pool.wait_ge(*have(f"xn_stored{l}_{s}", 16 * (TT // 2)))
            pool.wait_ge(*have(f"table_ready{l}", 1))

            def gather(b):
                pool.indirect_dma_start(out=xs[:, b % 2, :], out_offset=None, in_=xn_dram[l],
                                        in_offset=bass.IndirectOffsetOnAxis(ap=tok_i[:, b:b + 1], axis=0),
                                        bounds_check=last_row, oob_is_err=False
                                        ).then_inc(sem(f"gathered{l}_{b % 2}"), 16)

            gather(0)
            gather(1)
            for b in range(NE):
                if b + 2 < NE:
                    pool.wait_ge(*have(f"xs_t_in_psum{l}", b + 1))
                    gather(b + 2)
                n = stream.index((l, b, 2))
                half = slice(GC * BANK // 2, GC * BANK)
                pool.wait_ge(*have("w_hi_ready", n + 1))
                nc.gpsimd.tensor_tensor(w_lo[:, n % RING, half], raw[:, n % RING, half],
                                        w_hi[:, n % SPLIT, half].bitcast(fp32), ALU.subtract
                                        ).then_inc(sem(f"down_lo_pool{l}"), 1)
            for s in range(2):
                pool.wait_ge(*have(f"y_stored{l}_{s}", 16 * (NE // 2)))
            pool.wait_ge(*have(f"overflow_known{l}", 1))
            n_over = pool.value_load(nov_i[0:1, 0:1])
            with pool.If(n_over > 0):
                with pool.Fori(0, OVERFLOW) as j:
                    pool.wait_ge(*have(f"over_index{l}", j + 1))
                    e = pool.value_load(own_i[0:1, bass.ds(j, 1)], min_val=0, max_val=NE - 1)
                    for part in range(3):
                        load_expert(pool, l, e, part, over_w[part][:], sem(f"over_w{l}"))
                    pool.indirect_dma_start(out=xs[:, 0, :], out_offset=None, in_=xn_dram[l],
                                            in_offset=bass.IndirectOffsetOnAxis(ap=idx_c[:, 0:1], axis=0),
                                            bounds_check=last_row, oob_is_err=False
                                            ).then_inc(sem(f"over_x{l}"), 16)
                    pool.wait_ge(*have(f"over_y{l}", 2 * j + 2))
                    pool.dma_start(ys_dram[l][bass.ds(j * P + NE * P, P), :], y_sb[:, 0, :]
                                   ).then_inc(sem(f"over_stored{l}"), 16)
                    pool.wait_ge(*have(f"over_stored{l}", 16 * j + 16))
            with pool.If(n_over > 0):
                gather_results(l, NE + OVERFLOW)
            with pool.If(n_over < 1):
                gather_results(l, NE)

        moe(0)
        pool.dma_start(ws_in[:], c_ws[0].rearrange("g t s -> t g s")).then_inc(sem("ws_loaded"), 16)
        pool.wait_ge(*have("ws_loaded", 16))
        nc.gpsimd.affine_select(out=ws_in[:], in_=ws_in[:], pattern=[[0, GM], [-1, P]], compare_op=ALU.is_ge,
                                fill=0.0, base=0, channel_multiplier=1).then_inc(sem("ws_masked"), 1)
        pool.dma_start(vg_b[:], c_vnorm_g[0:1, :].to_broadcast([P, D])).then_inc(sem("vnorm_loaded"), 16)
        pool.dma_start(vb_b[:], c_vnorm_b[0:1, :].to_broadcast([P, D])).then_inc(sem("vnorm_loaded"), 16)
        pool.wait_ge(*have("w_used", first["vx1"] + 4))
        pool.dma_start(bs_b[:], c_bs[0:1].to_broadcast([P, GM, P])).then_inc(sem("bs_loaded"), 16)
        for g in range(KD):
            pool.wait_ge(*have("gated_hi", g + 1))
            nc.gpsimd.tensor_tensor(a_lo[:, g, :], u_c[:, g, :], a_hi[:, g, :].bitcast(fp32), ALU.subtract
                                    ).then_inc(sem("gated_lo"), 1)
        moe(1)
        pool.dma_start(fg_b[:], final_norm_g.rearrange("(o d) -> o d", o=1).to_broadcast([P, D])
                       ).then_inc(sem("final_gain_loaded"), 16)

    @block.tensor
    def _(pe):
        mm = nc.tensor.matmul

        def granule(d, j, banks, feature_major, n_m, hi, lo, part=slice(0, BANK), ready=None, tile_done=None):
            pe.wait_ge(*have("w_lo_ready", d + 1))
            w_parts = [w.rearrange("p (k n) -> p k n", k=GC) for w in (w_hi[:, d % SPLIT, :], w_lo[:, d % RING, :])]
            steps = [(kk, m) for kk in range(GC) for m in range(n_m)]
            if tile_done is not None:
                steps.sort(key=lambda step: step[1])
            for kk, m in steps:
                k = GC * j + kk
                if ready is not None and m == 0:
                    pe.wait_ge(*have(ready, k + 1))
                o = ps[:, banks + m, part]
                cut = slice(m * P, (m + 1) * P)
                for c, (wt, act) in enumerate(((w_parts[0], hi), (w_parts[0], lo), (w_parts[1], hi))):
                    if feature_major:
                        lhs, rhs = wt[:, kk, cut], act[:, k, :]
                    else:
                        lhs, rhs = act[:, k, cut], wt[:, kk, :]
                    last = mm(o, lhs, rhs, start=(k == 0 and c == 0), stop=(k == KD - 1 and c == 2))
                if tile_done is not None and kk == GC - 1 and m < n_m - 1:
                    last.then_inc(sem(tile_done), 1)
            last.then_inc(sem("w_used"), 1)

        def transposes(tag):
            n = norm_parts(tag)[0]
            per = BANK // (n * P)
            b0 = 4 if n == MT else 0
            for i in range(n):
                pe.wait_ge(*have(f"xn_{tag}", i + 1))
                for k in range(KD):
                    src = mem_tok[:, i, k * P:(k + 1) * P] if n == MT else xn_tile(i)[:, k * P:(k + 1) * P]
                    c0 = (k % per) * n * P + i * P
                    last = nc.tensor.transpose(ps[:, b0 + k // per, c0:c0 + P], src, ident[:])
                name = f"mem_t_in_psum{tag[-1]}" if n == MT else f"xn_t_in_psum_{tag}"
                last.then_inc(sem(name), 1)

        def late_transposes(tag):
            for half in range(2):
                for i in range(TT):
                    source_ready(pe, tag, i)
                    for k in range(half * CC, (half + 1) * CC):
                        last = nc.tensor.transpose(ps[:, k, i * P:(i + 1) * P], h[:, i, k * P:(k + 1) * P], ident[:])
                last.then_inc(sem(f"xn_t_in_psum_{tag}"), 1)

        def token_factors(tag):
            pe.wait_ge(*have(f"diag_ready_{tag}", 1))
            pe.wait_ge(*have(f"split_lo_{tag}", KD))
            mm(ps[:, 7, :], ones[:], diag[:].rearrange("p i t -> p (i t)"), start=True, stop=True
               ).then_inc(sem(f"factors_in_psum_{tag}"), 1)

        pe.wait_ge(*have("consts", 8))
        pe.wait_ge(*have("vecs_loaded", 16 * 8))
        nc.tensor.transpose(ps[:, 0, 0:NV], vec_in[0:NV, :], ident[0:NV, 0:NV]).then_inc(sem("vecs_in_psum"), 1)
        for m in range(CC):
            last = nc.tensor.transpose(ps[:, 1, m * TAPS:(m + 1) * TAPS], tap_in[0:TAPS, m * P:(m + 1) * P],
                                       ident[0:TAPS, 0:TAPS])
        last.then_inc(sem("vecs_in_psum"), 1)
        pe.wait_ge(*have("vecs_ready", 2))

        transposes("mix0")
        pe.wait_ge(*have("split_lo_mix0", 4))
        granule(first["sb_gate"], 0, 0, True, CC, a_hi, a_lo, ready="split_lo_mix0")
        granule(first["sb_gate"] + 1, 1, 0, True, CC, a_hi, a_lo, ready="split_lo_mix0")
        for j in range(2):
            granule(first["sb_a"] + j, j, 4, True, CC, a_hi, a_lo)
        pe.wait_ge(*have("gate_done", 1))
        for j in range(2):
            granule(first["sb_q"] + j, j, 0, True, CC, a_hi, a_lo)
        pe.wait_ge(*have("glu_done", 1))
        for j in range(2):
            granule(first["sb_k"] + j, j, 4, True, CC, a_hi, a_lo)
        pe.wait_ge(*have("q_ready", 1))
        granule(first["sb_v"], 0, 0, False, TT, a_hi, a_lo)
        pe.wait_ge(*have("k_ready", 1))
        transposes("mem0")
        granule(first["sb_v"] + 1, 1, 0, False, TT, a_hi, a_lo)

        def mem_keys(l, s, bank):
            for j in range(2):
                granule(first[f"kx{l}"] + 2 * s + j, j, bank, True, 4, mem_hi, mem_lo, part=slice(0, M),
                        ready=f"mem_split_lo{l}" if s == 0 else None)

        def mem_values(l, s, bank):
            for j in range(2):
                granule(first[f"vx{l}"] + 2 * s + j, j, bank, False, MT, mem_hi, mem_lo)

        pe.wait_ge(*have("v_ready", 1))
        mem_keys(0, 0, 0)
        pe.wait_ge(*have("mem_split_lo0", KD))
        mem_keys(0, 1, 4)
        pe.wait_ge(*have("kx_ready0", 1))
        mem_values(0, 0, 0)
        mem_values(0, 1, 2)
        pe.wait_ge(*have("kx_ready0", 2))

        def head(hd):
            return slice((hd % 2) * SB_DH, (hd % 2 + 1) * SB_DH), hd // 2

        def scores(hd):
            rows, c = head(hd)
            if hd:
                pe.wait_ge(*have("z_diag", hd))
                pe.wait_ge(*have("z_off", hd))
            for j in range(TT):
                cut = slice(j * P, (j + 1) * P)
                last = mm(ps[:, 4, cut], k_t[rows, c, cut], q_t[rows, c, cut], start=True, stop=True)
                if j < TT - 1:
                    o = OFF[j]
                    bank, o = 4 + o // BANK, o % BANK
                    last = mm(ps[:, bank, o:o + T - (j + 1) * P], k_t[rows, c, cut], q_t[rows, c, (j + 1) * P:],
                              start=True, stop=True)
            last.then_inc(sem("z_in_psum"), 1)

        def sums(hd):
            pe.wait_ge(*have("softplus", hd + 1))
            if hd:
                pe.wait_ge(*have("log_w", hd))
            else:
                pe.wait_ge(*have("vx_ready0", 2))
            s = sbuf[:, hd % 2, :]
            mm(ps[:, 0, :], tri[:], s[:, 0:512], start=True, stop=True)
            mm(ps[:, 1, :], tri[:], s[:, 512:1024], start=True, stop=False, skip_group_check=True)
            mm(ps[:, 2, 0:256], tri[:], s[:, 1024:1280], start=True, stop=False, skip_group_check=True)
            mm(ps[:, 1, 0:384], ones[:], s[:, 128:512], start=False, stop=False, skip_group_check=True)
            mm(ps[:, 1, 128:384], ones[:], s[:, 1024:1280], start=False, stop=False, skip_group_check=True)
            mm(ps[:, 1, 256:384], ones[:], s[:, 896:1024], start=False, stop=False, skip_group_check=True)
            mm(ps[:, 1, 384:512], ones[:], s[:, 384:512], start=False, stop=True, skip_group_check=True)
            mm(ps[:, 2, 0:256], ones[:], s[:, 256:512], start=False, stop=False, skip_group_check=True)
            mm(ps[:, 2, 128:256], ones[:], s[:, 896:1024], start=False, stop=True, skip_group_check=True
               ).then_inc(sem("sums_in_psum"), 1)

        def values(hd):
            rows, c = head(hd)
            pe.wait_ge(*have("weights", hd + 1))
            if hd >= 2 and hd % 2 == 0:
                pe.wait_ge(*have("heads_lo", hd // 2))
            w = zbuf[:, hd % 2, :]
            o = ps[rows, 3, :]
            vcol = slice(hd * SB_DH, (hd + 1) * SB_DH)
            for j in range(TT):
                v = v_s[:, j, vcol]
                last = mm(o[:, j * P:(j + 1) * P], v, w[:, j * P:(j + 1) * P], start=(j == 0), stop=(j == TT - 1),
                          skip_group_check=True)
                if j < TT - 1:
                    n = T - (j + 1) * P
                    last = mm(o[:, (j + 1) * P:], v, w[:, OFF[j]:OFF[j] + n], start=False, stop=False,
                              skip_group_check=True)
            last.then_inc(sem("heads_in_psum"), 1)

        scores(0)
        for hd in range(SB_HEADS):
            if hd + 1 < SB_HEADS:
                scores(hd + 1)
            if hd:
                values(hd - 1)
            sums(hd)
            if hd == 3:
                pe.wait_ge(*have("conv_taps", CC * TAPS))
                for m in range(CC):
                    last = mm(ps[:, 7, :], ones[:], conv_acc[:, m, :], start=(m == 0), stop=(m == CC - 1))
                last.then_inc(sem("conv_mean"), 1)
            if hd == 5:
                pe.wait_ge(*have("conv_squared", 1))
                for m in range(CC):
                    last = mm(ps[:, 7, :], ones[:], conv_sq[:, m, :], start=(m == 0), stop=(m == CC - 1))
                last.then_inc(sem("conv_var"), 1)
        values(SB_HEADS - 1)

        def project_out(l):
            if l == 0:
                pe.wait_ge(*have("heads_lo", SB_HEADS // 2))
                pe.wait_ge(*have("log_w", SB_HEADS))
            for s in range(2):
                for j in range(2):
                    granule(first[f"mix_out{l}"] + 2 * s + j, j, 4 * s, False, TT, a_hi, a_lo,
                            ready=None if s else "gated_lo" if l else "conv_lo" if j == 0 else None,
                            tile_done=f"tile_xa{l}" if s == j == 1 else None)

        def cross(l):
            pe.wait_ge(*have(f"h_part_xa{l}", TT))
            late_transposes(f"xa{l}")
            for s in range(2):
                pe.wait_ge(*have(f"split_lo_xa{l}", 4 * (s + 1)))
                if s:
                    pe.wait_ge(*have(f"factors_ready_xa{l}", 1))
                for j in range(2):
                    granule(first[f"xq{l}"] + 2 * s + j, j, 4 * s, True, 4, a_hi, a_lo,
                            ready=f"split_lo_xa{l}" if s == 0 else None)
                    if s == j == 0:
                        token_factors(f"xa{l}")

            def xscores(hd):
                if hd < 2:
                    pe.wait_ge(*have(f"xq_ready{l}", hd + 1))
                else:
                    pe.wait_ge(*have(f"x_exp{l}", TT * (hd - 1)))
                for i in range(TT):
                    b = 2 * (hd % 2) + i // 2
                    for c in range(2):
                        last = mm(ps[:, b, (i % 2) * M:(i % 2 + 1) * M], xq[:, 2 * hd + c, i * P:(i + 1) * P],
                                  kx[:, 2 * hd + c, :], start=(c == 0), stop=(c == 1))
                last.then_inc(sem(f"x_scores{l}"), 1)

            def xvalues(hd):
                pe.wait_ge(*have(f"x_probs{l}", hd + 1))
                if hd:
                    pe.wait_ge(*have(f"x_probs_t{l}", hd))
                for i in range(TT):
                    for c in range(MT):
                        last = nc.tensor.transpose(ps[:, 4 + c, i * P:(i + 1) * P], xp[:, hd % 2, i, c * P:(c + 1) * P],
                                                   ident[:])
                last.then_inc(sem(f"x_probs_t_in_psum{l}"), 1)
                pe.wait_ge(*have(f"x_probs_t{l}", hd + 1))
                if hd:
                    pe.wait_ge(*have(f"x_heads_lo{l}", 2 * hd))
                for c2 in range(2):
                    f0 = hd * XD + c2 * P
                    for c in range(MT):
                        last = mm(ps[:, 6 + c2, :], vx[:, c, f0:f0 + P], xpt[:, hd % 2, c, :], start=(c == 0),
                                  stop=(c == MT - 1))
                last.then_inc(sem(f"x_heads_in_psum{l}"), 1)

            xscores(0)
            pe.wait_ge(*have(f"xq_ready{l}", 2))
            for hd in range(XH):
                if hd + 1 < XH:
                    xscores(hd + 1)
                xvalues(hd)
            for s in range(2):
                if s == 0:
                    pe.wait_ge(*have(f"x_exp{l}", TT * XH))
                for j in range(2):
                    if l == 0 and s == 1 and j == 0:
                        pe.wait_ge(*have("mem_split_lo1", KD))
                    granule(first[f"xo{l}"] + 2 * s + j, j, 4 * s, False, TT, a_hi, a_lo,
                            ready=f"x_heads_lo{l}" if s == 0 else None,
                            tile_done=f"tile_ffn{l}" if s == j == 1 else None)
                    if l == 0 and s == 0 and j == 0:
                        pe.wait_ge(*have(f"x_heads_lo{l}", KD))
                        transposes("mem1")

        def experts(l):
            W = NG + NE
            small_bank = 4 if l == 0 else 0
            pe.wait_ge(*have(f"h_part_ffn{l}", TT))
            if l == 0:
                mem_keys(1, 0, 0)
                pe.wait_ge(*have(f"h_ffn{l}", TT))

            def tile_transposes(i):
                b0 = (small_bank + 2 * i) % 8
                if l == 0 and i == 2:
                    pe.wait_ge(*have("kx_ready1", 1))
                pe.wait_ge(*have(f"h_ffn{l}", TT if l and i == 3 else i + 1))
                for k in range(KD):
                    last = nc.tensor.transpose(ps[:, b0 + k // 4, (k % 4) * P:(k % 4 + 1) * P],
                                               h[:, i, k * P:(k + 1) * P], ident[:])
                last.then_inc(sem(f"xn_t_in_psum_ffn{l}"), 1)

            def logits(i):
                pe.wait_ge(*have(f"a_full{l}", i + 1))
                for k in range(KD):
                    last = mm(ps[:, small_bank, i * W:(i + 1) * W], a_full[:, k, i * P:(i + 1) * P], rt_w[:, l, k, :],
                              start=(k == 0), stop=(k == KD - 1))
                last.then_inc(sem(f"logits{l}"), 1)

            tile_transposes(0)
            pe.wait_ge(*have("router_loaded", 64 * NL))
            for i in range(1, TT):
                tile_transposes(i)
                logits(i - 1)
            logits(TT - 1)
            if l == 0:
                mem_keys(1, 1, 0)
            pe.wait_ge(*have(f"assigned{l}", 1))
            for i in range(TT):
                for j in range(i + 1):
                    mm(ps[:, small_bank + 1, i * NE:(i + 1) * NE], (before if j == i else ones_r)[:], e_sum[:, j, :],
                       start=(j == 0), stop=(j == i))
            for j in range(TT):
                last = mm(ps[:, small_bank + 1, TT * NE:(TT + 1) * NE], ones_r[:], e_sum[:, j, :], start=(j == 0),
                          stop=(j == TT - 1))
            last.then_inc(sem(f"ranks{l}"), 1)
            if l == 0:
                pe.wait_ge(*have("kx_ready1", 2))
                mem_values(1, 0, 0)
            pe.wait_ge(*have(f"hots{l}", 2))
            for j in range(2 * TT):
                last = mm(ps[:, small_bank, 0:NB], slot_hot[:, j, :], tok_hot[:, j, :], start=(j == 0),
                          stop=(j == 2 * TT - 1))
            last.then_inc(sem(f"table{l}"), 1)
            if l == 0:
                mem_values(1, 1, 6)

            def xs_transposes(s):
                for k in range(KD):
                    last = nc.tensor.transpose(ps[:, k // 4, (k % 4) * P:(k % 4 + 1) * P],
                                               xs[:, s, k * P:(k + 1) * P], ident[:])
                last.then_inc(sem(f"xs_t_in_psum{l}"), 1)

            def gate_up(e, part, granule_at):
                n, slot, _, hs = granule_at
                pe.wait_ge(*have("w_lo_ready", n + 1))
                w = w_hi[:, hs, :], w_lo[:, slot, :]
                for kk in range(GC):
                    k = GC * part + kk
                    for c, (x_part, w_part) in enumerate(((xs_hi, w[0]), (xs_lo, w[0]), (xs_hi, w[1]))):
                        last = mm(ps[:, 2 + e, :], x_part[:, e, k, :], w_part[:, kk * BANK:(kk + 1) * BANK],
                                  start=(k == 0 and c == 0), stop=(k == KD - 1 and c == 2))
                last.then_inc(sem("w_used"), 1)

            def hidden_transposes(e, b):
                pe.wait_ge(*have(f"hidden{l}", b + 1))
                for c in range(2):
                    last = nc.tensor.transpose(ps[:, 4, c * P:(c + 1) * P], hid[:, e, c * P:(c + 1) * P], ident[:])
                last.then_inc(sem(f"hidden_t_in_psum{l}"), 1)

            def down(e, b, granule_at, first_block):
                n, slot, _, hs = granule_at
                pe.wait_ge(*have("w_lo_ready", n + 1))
                pe.wait_ge(*have(f"down_lo_pool{l}", b + 1))
                pe.wait_ge(*have(f"hidden_lo{l}", b + 1))
                if not first_block:
                    pe.wait_ge(*have(f"y_left{l}", b))
                    pe.wait_ge(*have(f"y_right{l}", b))
                w = w_hi[:, hs, :], w_lo[:, slot, :]
                for half in range(2):
                    for c in range(2):
                        cut = slice(c * D + half * BANK, c * D + (half + 1) * BANK)
                        for m, (h_part, w_part) in enumerate(((hid_hi, w[0]), (hid_lo, w[0]), (hid_hi, w[1]))):
                            last = mm(ps[:, 5 + half, :], h_part[:, e, c, :], w_part[:, cut],
                                      start=(c == 0 and m == 0), stop=(c == 1 and m == 2))
                last.then_inc(sem("w_used"), 1)

            if l == 0:
                pe.wait_ge(*have("vx_ready1", 1))
            pe.wait_ge(*have(f"table_ready{l}", 1))
            pe.wait_ge(*have(f"gathered{l}_0", 16))
            xs_transposes(0)

            def block_of(i, e, first_pair, last_pair):
                b = 2 * i + e
                pe.wait_ge(*have(f"xs_lo{l}", b + 1))
                if not first_pair:
                    pe.wait_ge(*have(f"hidden{l}", b - 1))
                gate_up(e, 0, entry(l, 0 if first_pair and e == 0 else 3 * e - 1, i))
                if not (last_pair and e == 1):
                    pe.wait_ge(*have(f"gathered{l}_{1 - e}", 16 * i + (16 if e == 0 else 32)))
                    xs_transposes(1 - e)
                if not (first_pair and e == 0):
                    hidden_transposes(1 - e, b - 1)
                gate_up(e, 1, entry(l, 1 if first_pair and e == 0 else 3 * e, i))
                if l == 0 and first_pair and e == 1:
                    pe.wait_ge(*have("vx_ready1", 2))
                if not (first_pair and e == 0):
                    down(1 - e, b - 1, entry(l, 3 * e + 1, i), first_pair)

            for e in range(2):
                block_of(0, e, True, False)
            with pe.Fori(1, NE // 2 - 1) as i:
                for e in range(2):
                    block_of(i, e, False, False)
            for e in range(2):
                block_of(NE // 2 - 1, e, False, True)
            hidden_transposes(1, NE - 1)
            down(1, NE - 1, entry(l, 3 * NE - 1, 0), False)

            pe.wait_ge(*have(f"y_left{l}", NE))
            pe.wait_ge(*have(f"y_right{l}", NE))
            pe.wait_ge(*have(f"overflow_known{l}", 1))
            n_over = pe.value_load(nov_i[0:1, 0:1])
            with pe.If(n_over > 0):
                with pe.Fori(0, OVERFLOW) as j:
                    pe.wait_ge(*have(f"over_x{l}", 16 * j + 16))
                    for k in range(KD):
                        last = nc.tensor.transpose(ps[:, k // 4, (k % 4) * P:(k % 4 + 1) * P],
                                                   xs[:, 0, k * P:(k + 1) * P], ident[:])
                    last.then_inc(sem(f"over_products{l}"), 1)
                    pe.wait_ge(*have(f"over_w{l}", 80 * j + 80))
                    pe.wait_ge(*have(f"over_x_t{l}", j + 1))
                    for k in range(KD):
                        last = mm(ps[:, 2, :], xs_full[:, k, :], over_w[k // GC][:, (k % GC) * BANK:(k % GC + 1) * BANK],
                                  start=(k == 0), stop=(k == KD - 1))
                    last.then_inc(sem(f"over_products{l}"), 1)
                    pe.wait_ge(*have(f"over_hidden{l}", j + 1))
                    for c in range(2):
                        last = nc.tensor.transpose(ps[:, 4, c * P:(c + 1) * P], hid[:, 0, c * P:(c + 1) * P], ident[:])
                    last.then_inc(sem(f"over_products{l}"), 1)
                    pe.wait_ge(*have(f"over_hidden_t{l}", j + 1))
                    for half in range(2):
                        for c in range(2):
                            last = mm(ps[:, 5 + half, :], hid_full[:, c, :],
                                      over_w[2][:, c * D + half * BANK:c * D + (half + 1) * BANK],
                                      start=(c == 0), stop=(c == 1))
                    last.then_inc(sem(f"over_products{l}"), 1)
                    pe.wait_ge(*have(f"over_y{l}", 2 * j + 2))

        project_out(0)
        cross(0)
        experts(0)

        late_transposes("mix1")
        pe.wait_ge(*have("split_lo_mix1", 4))
        granule(first["c_v"], 0, 0, False, TT, a_hi, a_lo, ready="split_lo_mix1")
        token_factors("mix1")
        pe.wait_ge(*have("ws_masked", 1))
        for g in range(GM):
            last = nc.tensor.transpose(ps[:, 4 + g // 4, (g % 4) * P:(g % 4 + 1) * P], ws_in[:, g, :], ident[:])
        last.then_inc(sem("ws_t_in_psum"), 1)
        granule(first["c_v"] + 1, 1, 0, False, TT, a_hi, a_lo)
        pe.wait_ge(*have("ws_t_ready", 1))
        pe.wait_ge(*have("factors_ready_mix1", 1))
        for j in range(2):
            granule(first["c_v"] + 2 + j, j, 4, False, TT, a_hi, a_lo)
        for s in range(2):
            pe.wait_ge(*have("v_gelu", TT * (s + 1)))
            for j in range(2):
                granule(first["c_u"] + 2 * s + j, j, 4 * s, True, 4, a_hi, a_lo)
        pe.wait_ge(*have("v_normed", TT))
        for g in range(GM):
            if g in (0, 4):
                pe.wait_ge(*have("u_scaled", g // 4 + 1))
            for c in range(TT):
                last = mm(ps[:, g, c * P:(c + 1) * P], v_c[:, c, g * P:(g + 1) * P], ws_t[:, g, :], start=True, stop=True)
            last.then_inc(sem("mixed_in_psum"), 1)
        pe.wait_ge(*have("gated", GM))
        project_out(1)
        cross(1)
        experts(1)

    @block.scalar
    def _(act):
        A = nc.scalar.activation

        for t, n, src in ((0, KD, mem_norm_g.rearrange("(k p) -> k p", p=P)),
                          (MIX_G, NL * KD, norm_mix.rearrange("l (k p) -> (l k) p", p=P)),
                          (XA_G, NL * KD, norm_xa.rearrange("l (k p) -> (l k) p", p=P)),
                          (FFN_G, NL * KD, norm_ffn.rearrange("l (k p) -> (l k) p", p=P)),
                          (CONV_B, CC, ab_conv_b.rearrange("l (k p) -> (l k) p", p=P)),
                          (CN_G, CC, ab_cnorm_g.rearrange("l (k p) -> (l k) p", p=P)),
                          (CN_B, CC, ab_cnorm_b.rearrange("l (k p) -> (l k) p", p=P)),):
            act.dma_start(vec_in[t:t + n, :], src).then_inc(sem("vecs_loaded"), 16)
        act.dma_start(tap_in[0:TAPS, :], ab_conv_w[0]).then_inc(sem("vecs_loaded"), 16)
        act.dma_start(mem_tok[:], mem[0].rearrange("(i p) d -> p i d", p=P)).then_inc(sem("mem_loaded0"), 16)

        n_prep = [0]

        def hi_part(n, slot, arrivals, hs):
            act.wait_ge(*have(f"raw_loaded{slot}", arrivals))
            if not isinstance(n, int) or n >= SPLIT:
                act.wait_ge(*have("w_used", n - (SPLIT - 1)))
            A(w_hi[:, hs, :], raw[:, slot, :], ACT.Copy).then_inc(sem("w_hi_ready"), 1)

        def prep(upto):
            while n_prep[0] < upto:
                d = n_prep[0]
                n_prep[0] += 1
                hi_part(d, ring_pos[d], ring_count[d], d % SPLIT)

        def squares(tag):
            n, src, *_ = norm_parts(tag)
            for i in range(n if tag[:3] == "ffn" else n // 2):
                source_ready(act, tag, i)
                if i:
                    act.wait_ge(*have(f"squares_act_{tag}", i))
                A(xn[:, 0, :], src(i), ACT.Square, accum_out=n_ss[:, i:i + 1]).then_inc(sem(f"squares_act_{tag}"), 1)
            if tag not in LATE:
                roots(tag)

        def roots(tag):
            n = norm_parts(tag)[0]
            act.wait_ge(*have(f"norm_var_{tag}", 1))
            A(n_y[:, 0:n], n_var[:, 0:n], ACT.Sqrt).then_inc(sem(f"norm_root_{tag}"), 1)

        def split(tag, done):
            n, _, _, g0, hi, lo = norm_parts(tag)
            per = BANK // (n * P)
            b0 = 4 if n == MT else 0
            name = f"mem_t_in_psum{tag[-1]}" if n == MT else f"xn_t_in_psum_{tag}"
            if tag not in LATE:
                act.wait_ge(*have(name, n))
            for k in range(KD):
                if tag in LATE and k % CC == 0:
                    act.wait_ge(*have(name, k // CC + 1))
                c0 = (k % per) * n * P
                A(hi[:, k, :], ps[:, b0 + k // per, c0:c0 + n * P], ACT.Copy, scale=vecs[:, g0 + k:g0 + k + 1]
                  ).then_inc(sem(done), 1)

        def used(d):
            act.wait_ge(*have("w_used", d + 1))

        def copy_out(name, dst, src, scale=1.0):
            A(dst, src, ACT.Copy, scale=scale).then_inc(sem(name), 1)

        squares("mix0")
        act.wait_ge(*have("vecs_ready", 2))
        prep(2)
        split("mix0", "split_hi_mix0")
        prep(3)
        squares("mem0")
        used(1)
        A(conv_acc[:].rearrange("p k n -> p (k n)"), ps[:, 0:4, :].rearrange("p k n -> p (k n)"), ACT.Sigmoid
          ).then_inc(sem("gate_done"), 1)
        prep(7)
        used(first["sb_q"] + 1)
        copy_out("q_ready", q_t[:], ps[:, 0:4, :], SB_DH ** -0.5)
        prep(9)
        used(first["sb_k"] + 1)
        copy_out("k_ready", k_t[:], ps[:, 4:8, :])
        prep(10)
        split("mem0", "mem_split_hi0")
        prep(11)
        used(first["sb_v"] + 1)
        copy_out("v_ready", v_s[:], ps[:, 0:4, :])
        prep(13)

        def mem_keys_out(l, s, bank):
            used(first[f"kx{l}"] + 2 * s + 1)
            copy_out(f"kx_ready{l}", kx[:, 4 * s:4 * s + 4, :], ps[:, bank:bank + 4, 0:M])

        def mem_values_out(l, s, bank):
            used(first[f"vx{l}"] + 2 * s + 1)
            copy_out(f"vx_ready{l}", vx[:, :, s * BANK:(s + 1) * BANK], ps[:, bank:bank + MT, :])

        prep(14)
        mem_keys_out(0, 0, 0)
        prep(15)
        prep(16)
        mem_keys_out(0, 1, 4)
        prep(18)
        mem_values_out(0, 0, 0)
        prep(19)
        mem_values_out(0, 1, 2)
        prep(21)

        def z_part(hd):
            s = hd % 2
            act.wait_ge(*have("z_in_psum", hd + 1))
            if hd >= 2:
                act.wait_ge(*have("heads_in_psum", hd - 1))
            else:
                act.wait_ge(*have("w_used", first["vx0"] + 4))
            A(zbuf[:, s, 512:1280], ps[:, 5:7, :].rearrange("p k n -> p (k n)")[:, 0:768], ACT.Copy
              ).then_inc(sem("z_off"), 1)
            act.wait_ge(*have("minus_abs_z", hd + 1))
            A(sbuf[:, s, :], sbuf[:, s, :], ACT.Exp).then_inc(sem("exp_abs"), 1)
            act.wait_ge(*have("exp_abs", hd + 1))
            A(sbuf[:, s, :], sbuf[:, s, :], ACT.Ln, bias=1.0).then_inc(sem("ln_done"), 1)

        def w_part(hd):
            act.wait_ge(*have("log_w", hd + 1))
            A(zbuf[:, hd % 2, :], zbuf[:, hd % 2, :], ACT.Exp).then_inc(sem("weights"), 1)

        def heads_hi(pair):
            act.wait_ge(*have("heads_in_psum", 2 * pair + 2))
            copy_out("heads_hi", a_hi[:, CC + pair, :], ps[:, 3, :])

        nc.scalar.preload_act_table_set("natural_log_exp_and_others")
        z_part(0)
        for hd in range(SB_HEADS):
            if hd + 1 < SB_HEADS:
                z_part(hd + 1)
            if hd in (2, 4, 6):
                heads_hi(hd // 2 - 1)
            if hd == 6:
                act.wait_ge(*have("conv_var_ready", 1))
                A(conv_rs[:, 1, :], conv_rs[:, 0, :], ACT.Ln).then_inc(sem("conv_root"), 1)
                act.wait_ge(*have("conv_root", 1))
                A(conv_rs[:, 1, :], conv_rs[:, 1, :], ACT.Exp, scale=-0.5).then_inc(sem("conv_root"), 1)
            w_part(hd)
            if hd == 4:
                act.wait_ge(*have("conv_centred", 1))
                A(conv_sq[:].rearrange("p k n -> p (k n)"), conv_acc[:].rearrange("p k n -> p (k n)"), ACT.Square
                  ).then_inc(sem("conv_squared"), 1)
        heads_hi(3)
        act.wait_ge(*have("conv_normed", 1))
        for m in range(CC):
            A(conv_sq[:, m, :], conv_acc[:, m, :], ACT.Silu, bias=vecs[:, CN_B + m:CN_B + m + 1],
              scale=vecs[:, CN_G + m:CN_G + m + 1]).then_inc(sem("conv_silu"), 1)
            act.wait_ge(*have("conv_silu", m + 1))
            copy_out("conv_hi", a_hi[:, m, :], conv_sq[:, m, :])
        prep(first["xq0"] + 2)

        def factors_out(tag, scale):
            act.wait_ge(*have(f"factors_in_psum_{tag}", 1))
            copy_out(f"factors_ready_{tag}", factors[:], ps[:, 7, :], scale)

        def cross(l):
            d = first[f"xq{l}"]
            squares(f"xa{l}")
            split(f"xa{l}", f"split_hi_xa{l}")
            prep(d + 3)
            roots(f"xa{l}")
            factors_out(f"xa{l}", XD ** -0.5)
            prep(d + 6)

            def x_exp(hd):
                act.wait_ge(*have(f"x_max{l}", hd + 1))
                if hd >= 2:
                    act.wait_ge(*have(f"x_probs_t_in_psum{l}", hd - 1))
                for i in range(TT):
                    b = 2 * (hd % 2) + i // 2
                    A(xp[:, hd % 2, i, :], ps[:, b, (i % 2) * M:(i % 2 + 1) * M], ACT.Exp, bias=x_max[:, i:i + 1],
                      accum_out=x_sum[:, i:i + 1]).then_inc(sem(f"x_exp{l}"), 1)

            x_exp(0)
            for hd in range(XH):
                act.wait_ge(*have(f"x_probs_t_in_psum{l}", hd + 1))
                if hd >= 2:
                    act.wait_ge(*have(f"x_heads_in_psum{l}", hd - 1))
                copy_out(f"x_probs_t{l}", xpt[:, hd % 2], ps[:, 4:6, :])
                if hd + 1 < XH:
                    x_exp(hd + 1)
                act.wait_ge(*have(f"x_heads_in_psum{l}", hd + 1))
                for c in range(2):
                    copy_out(f"x_heads_hi{l}", a_hi[:, 2 * hd + c, :], ps[:, 6 + c, :])
            if l == 0:
                prep(d + 7)
                squares("mem1")
                split("mem1", "mem_split_hi1")
            prep(d + 10)
            if l == 0:
                prep(d + 11)

        def experts(l):
            squares(f"ffn{l}")
            m = first[f"moe{l}"]
            if l == 0:
                k1, v1 = first["kx1"], first["vx1"]
                prep(k1 + 4)
                mem_keys_out(1, 0, 0)
                prep(v1 + 1)
            act.wait_ge(*have(f"r_args{l}", 1))
            A(r4b[:], r4a[:], ACT.Exp).then_inc(sem(f"r_exp{l}"), 1)
            act.wait_ge(*have(f"r_args{l}", 2))
            A(r1b[:], r1a[:], ACT.Exp).then_inc(sem(f"r_exp{l}"), 1)
            if l == 0:
                prep(v1 + 2)
                mem_keys_out(1, 1, 0)
                prep(v1 + 4)
                mem_values_out(1, 0, 0)
                prep(m + 2)
                mem_values_out(1, 1, 6)
            prep(m + 2)

            def rows_hi(e):
                A(xs_hi[:, e].rearrange("p k n -> p (k n)"), ps[:, 0:2, :].rearrange("p a n -> p (a n)"), ACT.Copy
                  ).then_inc(sem(f"xs_hi{l}"), 1)

            def hidden_hi(e, b):
                act.wait_ge(*have(f"hidden_t_in_psum{l}", b + 1))
                A(hid_hi[:, e].rearrange("p c n -> p (c n)"), ps[:, 4, 0:2 * P], ACT.Copy
                  ).then_inc(sem(f"hidden_hi{l}"), 1)

            def y_left(e, n):
                act.wait_ge(*have("w_used", n + 1))
                A(y_sb[:, e, 0:BANK], ps[:, 5, :], ACT.Copy).then_inc(sem(f"y_left{l}"), 1)

            def store(e, b):
                act.wait_ge(*have(f"y_left{l}", b + 1))
                act.wait_ge(*have(f"y_right{l}", b + 1))
                act.dma_start(ys_dram[l][b * P:(b + 1) * P, :] if isinstance(b, int) else
                              ys_dram[l][bass.ds(b * P, P), :], y_sb[:, e, :]
                              ).then_inc(sem(f"y_stored{l}_{e}"), 16)

            def block_of(i, e, first_pair, last_pair):
                b = 2 * i + e
                last_block = last_pair and e == 1
                if not last_block:
                    act.wait_ge(*have(f"xs_t_in_psum{l}", b + 2))
                    rows_hi(1 - e)
                if not (first_pair and e == 0):
                    hidden_hi(1 - e, b - 1)
                hi_part(*entry(l, 3 * e + 2, i))
                act.wait_ge(*have("w_used", entry(l, 1 if first_pair and e == 0 else 3 * e, i)[0] + 1))
                if not first_pair:
                    act.wait_ge(*have(f"hidden{l}", b - 1))
                A(silu_g[:, e, :], ps[:, 2 + e, 0:FE], ACT.Silu).then_inc(sem(f"silu{l}"), 1)
                if not last_block:
                    hi_part(*entry(l, 3 * e + 3, i))
                if not (first_pair and e == 0):
                    if not first_pair:
                        act.wait_ge(*have(f"y_stored{l}_{e}", 16 * i))
                    y_left(1 - e, entry(l, 3 * e + 1, i)[0])
                if not last_block:
                    hi_part(*entry(l, 3 * e + 4, i))
                if not (first_pair and e == 0):
                    store(1 - e, b - 1)

            act.wait_ge(*have(f"xs_t_in_psum{l}", 1))
            rows_hi(0)
            for e in range(2):
                block_of(0, e, True, False)
            with act.Fori(1, NE // 2 - 1) as i:
                for e in range(2):
                    block_of(i, e, False, False)
            for e in range(2):
                block_of(NE // 2 - 1, e, False, True)
            hidden_hi(1, NE - 1)
            y_left(1, first[f"moe{l}"] + 3 * NE - 1)
            store(1, NE - 1)
            n_prep[0] += 3 * NE - 2

            act.wait_ge(*have(f"y_stored{l}_1", 16 * (NE // 2)))
            act.wait_ge(*have(f"y_stored{l}_0", 16 * (NE // 2)))
            act.wait_ge(*have(f"overflow_known{l}", 1))
            n_over = act.value_load(nov_i[0:1, 0:1])
            with act.If(n_over > 0):
                with act.Fori(0, OVERFLOW) as j:
                    act.wait_ge(*have(f"over_products{l}", 4 * j + 2))
                    A(silu_g[:, 0, :], ps[:, 2, 0:FE], ACT.Silu).then_inc(sem(f"over_silu{l}"), 1)
                    act.wait_ge(*have(f"over_products{l}", 4 * j + 3))
                    A(hid_full[:].rearrange("p c n -> p (c n)"), ps[:, 4, 0:2 * P], ACT.Copy
                      ).then_inc(sem(f"over_hidden_t{l}"), 1)
                    act.wait_ge(*have(f"over_products{l}", 4 * j + 4))
                    A(y_sb[:, 0, 0:BANK], ps[:, 5, :], ACT.Copy).then_inc(sem(f"over_y{l}"), 1)
                    act.wait_ge(*have(f"over_stored{l}", 16 * j + 16))

        cross(0)
        experts(0)

        prep(first["c_v"] + 2)
        squares("mix1")
        split("mix1", "split_hi_mix1")
        d = first["c_v"]
        prep(d + 3)
        roots("mix1")
        factors_out("mix1", 1.0)
        act.wait_ge(*have("ws_t_in_psum", 1))
        copy_out("ws_t_ready", ws_t[:].rearrange("p g t -> p (g t)"), ps[:, 4:6, :].rearrange("p a b -> p (a b)"))
        prep(d + 4)
        used(d + 1)
        for i in range(TT):
            A(v_c[:, i, 0:BANK], ps[:, i, :], ACT.Gelu, scale=n_y[:, i:i + 1]).then_inc(sem("v_gelu"), 1)
        prep(d + 6)
        used(d + 3)
        for i in range(TT):
            A(v_c[:, i, BANK:], ps[:, 4 + i, :], ACT.Gelu, scale=n_y[:, i:i + 1]).then_inc(sem("v_gelu"), 1)
        act.wait_ge(*have("norm_var_v", 1))
        A(n_y[:], n_var[:], ACT.Sqrt).then_inc(sem("norm_root_v"), 1)
        prep(d + 8)
        act.wait_ge(*have("u_scaled", 1))
        A(u_c[:, 0:4, :], u_c[:, 0:4, :], ACT.Gelu).then_inc(sem("u_gelu"), 1)
        prep(d + 10)
        act.wait_ge(*have("u_scaled", 2))
        A(u_c[:, 4:8, :], u_c[:, 4:8, :], ACT.Gelu).then_inc(sem("u_gelu"), 1)
        for g in range(GM):
            act.wait_ge(*have("gated", g + 1))
            copy_out("gated_hi", a_hi[:, g, :], u_c[:, g, :])
        prep(first["xq1"] + 2)
        cross(1)
        experts(1)
        squares("fin1")

    @block.vector
    def _(dve):
        V = nc.vector
        own_sem = sem("dve_steps")
        n_own = [0]

        def own(ins):
            n_own[0] += 1
            ins.then_inc(own_sem, 1)
            dve.wait_ge(own_sem, n_own[0])

        n_prep = [0]

        def lo_part(n, slot, _, hs, end=GC * BANK):
            dve.wait_ge(*have("w_hi_ready", n + 1))
            V.tensor_tensor(w_lo[:, slot, 0:end], raw[:, slot, 0:end],
                            w_hi[:, hs, 0:end].bitcast(fp32), ALU.subtract).then_inc(sem("w_lo_ready"), 1)

        def prep(upto):
            while n_prep[0] < upto:
                d = n_prep[0]
                n_prep[0] += 1
                lo_part(d, ring_pos[d], ring_count[d], d % SPLIT)

        def rstd(tag, n, var):
            dve.wait_ge(*have(f"norm_root_{tag}", 1))
            y, t = n_y[:, 0:n], n_t[:, 0:n]
            own(V.reciprocal(y, y))
            own(V.tensor_tensor(t, y, y, ALU.mult))
            own(V.scalar_tensor_tensor(out=t, in0=t, scalar=-0.5, in1=var, op0=ALU.mult, op1=ALU.mult))
            own(V.scalar_tensor_tensor(out=y, in0=t, scalar=1.5, in1=y, op0=ALU.add, op1=ALU.mult))

        def norm(tag):
            n, src, *_ = norm_parts(tag)
            for i in range(n if tag[:3] == "ffn" else n // 2, n):
                source_ready(dve, tag, i)
                own(V.scalar_tensor_tensor(out=xn[:, 1, :], in0=src(i), scalar=1.0, in1=src(i), op0=ALU.mult,
                                           op1=ALU.mult, accum_out=n_ss[:, i:i + 1]))
            dve.wait_ge(*have(f"squares_act_{tag}", n if tag[:3] == "ffn" else n // 2))
            V.tensor_scalar(n_var[:, 0:n], n_ss[:, 0:n], 1.0 / D, EPS, ALU.mult, ALU.add
                            ).then_inc(sem(f"norm_var_{tag}"), 1)
            rstd(tag, n, n_var[:, 0:n])

        def late_factors(tag):
            norm(tag)
            V.tensor_tensor(diag[:], ident[:].unsqueeze(1).to_broadcast([P, TT, P]),
                            n_y[:].unsqueeze(2).to_broadcast([P, TT, P]), ALU.mult
                            ).then_inc(sem(f"diag_ready_{tag}"), 1)

        def scaled(dst, s):
            return V.tensor_tensor(dst, ps[:, 4 * s:4 * s + 4, :],
                                   factors[:].unsqueeze(1).to_broadcast([P, 4, T]), ALU.mult)

        def norm_tiles(tag, tiles=None):
            n, src, *_ = norm_parts(tag)
            for i in tiles or range(n):
                if n == MT:
                    V.tensor_scalar(src(i), src(i), n_y[:, i:i + 1], None, ALU.mult).then_inc(sem(f"xn_{tag}"), 1)
                    continue
                V.tensor_scalar(xn_tile(i), src(i), n_y[:, i:i + 1], None, ALU.mult
                                ).then_inc(sem(f"xn_{tag}"), 1)

        def split(tag, hi_done, done):
            n, _, _, g0, hi, lo = norm_parts(tag)
            per = BANK // (n * P)
            b0 = 4 if n == MT else 0
            for k in range(KD):
                c0 = (k % per) * n * P
                dve.wait_ge(*have(hi_done, (k // per + 1) * per))
                V.scalar_tensor_tensor(out=lo[:, k, :], in0=ps[:, b0 + k // per, c0:c0 + n * P],
                                       scalar=vecs[:, g0 + k:g0 + k + 1], in1=hi[:, k, :].bitcast(fp32),
                                       op0=ALU.mult, op1=ALU.subtract).then_inc(sem(done), 1)

        def low(name, dst, src, hi):
            V.tensor_tensor(dst, src, hi.bitcast(fp32), ALU.subtract).then_inc(sem(name), 1)

        def residual(name, s, i):
            cut = slice(s * BANK, (s + 1) * BANK)
            V.tensor_tensor(h[:, i, cut], ps[:, 4 * s + i, :], h[:, i, cut], ALU.add).then_inc(sem(name), 1)

        dve.wait_ge(*have("router_consts", 1))
        V.tensor_copy(before[:], before_f[:]).then_inc(sem("router_rounded"), 1)
        V.tensor_copy(ones_r[:], ones[:]).then_inc(sem("router_rounded"), 1)
        dve.wait_ge(*have("vecs_in_psum", 2))
        V.tensor_copy(vecs[:], ps[:, 0, 0:NV]).then_inc(sem("vecs_ready"), 1)
        V.tensor_copy(taps[:].rearrange("p c t -> p (c t)"), ps[:, 1, 0:CC * TAPS]).then_inc(sem("vecs_ready"), 1)
        norm("mix0")
        norm_tiles("mix0")
        prep(2)
        split("mix0", "split_hi_mix0", "split_lo_mix0")
        prep(3)
        norm("mem0")
        norm_tiles("mem0")
        prep(5)

        dve.wait_ge(*have("gate_done", 1))
        dve.wait_ge(*have("conv_padded", 1))
        dve.wait_ge(*have("w_used", first["sb_a"] + 2))
        V.tensor_tensor(conv_in[:, :, PAD:], ps[:, 4:8, :], conv_acc[:], ALU.mult).then_inc(sem("glu_done"), 1)
        dve.wait_ge(*have("glu_done", 1))

        tap = [0]

        def conv(n):
            for _ in range(n):
                j = tap[0]
                if j >= TAPS:
                    return
                tap[0] += 1
                for m in range(CC):
                    if j:
                        dve.wait_ge(*have("conv_taps", CC * (j - 1) + m + 1))
                        V.scalar_tensor_tensor(out=conv_acc[:, m, :], in0=conv_in[:, m, j:j + T],
                                               scalar=taps[:, m, j:j + 1], in1=conv_acc[:, m, :], op0=ALU.mult,
                                               op1=ALU.add).then_inc(sem("conv_taps"), 1)
                    else:
                        V.tensor_scalar(conv_acc[:, m, :], conv_in[:, m, 0:T], taps[:, m, 0:1],
                                        vecs[:, CONV_B + m:CONV_B + m + 1], ALU.mult, ALU.add
                                        ).then_inc(sem("conv_taps"), 1)

        prep(6)
        conv(3)
        for d in range(7, 11):
            prep(d)
            conv(4 if d < 10 else 3)
        split("mem0", "mem_split_hi0", "mem_split_lo0")
        for d in range(11, 19):
            prep(d)
            conv(1)
        conv(3)

        def z_part(hd):
            s = hd % 2
            dve.wait_ge(*have("z_in_psum", hd + 1))
            if hd >= 2:
                dve.wait_ge(*have("heads_in_psum", hd - 1))
                dve.wait_ge(*have("sums_in_psum", hd - 1))
            else:
                dve.wait_ge(*have("w_used", first["vx0"] + 4))
            V.tensor_tensor(zbuf[:, s, 0:512].rearrange("p (j q) -> p j q", j=TT),
                            ps[:, 4, :].rearrange("p (j q) -> p j q", j=TT),
                            causal[:].unsqueeze(1).to_broadcast([P, TT, P]), ALU.add).then_inc(sem("z_diag"), 1)
            dve.wait_ge(*have("z_diag", hd + 1))
            dve.wait_ge(*have("z_off", hd + 1))
            V.scalar_tensor_tensor(out=sbuf[:, s, :], in0=zbuf[:, s, :], scalar=-1.0, in1=zbuf[:, s, :],
                                   op0=ALU.mult, op1=ALU.min).then_inc(sem("minus_abs_z"), 1)

        def softplus(hd):
            s = hd % 2
            dve.wait_ge(*have("ln_done", hd + 1))
            V.scalar_tensor_tensor(out=sbuf[:, s, :], in0=zbuf[:, s, :], scalar=0.0, in1=sbuf[:, s, :], op0=ALU.max,
                                   op1=ALU.add).then_inc(sem("softplus"), 1)

        def log_w(hd):
            s = hd % 2
            dve.wait_ge(*have("sums_in_psum", hd + 1))
            V.tensor_tensor(zbuf[:, s, :], zbuf[:, s, :], ps[:, 0:3, :].rearrange("p k n -> p (k n)")[:, 0:ZW],
                            ALU.subtract).then_inc(sem("log_w"), 1)

        def heads_lo(pair):
            dve.wait_ge(*have("heads_hi", pair + 1))
            low("heads_lo", a_lo[:, CC + pair, :], ps[:, 3, :], a_hi[:, CC + pair, :])

        z_part(0)
        softplus(0)
        for hd in range(SB_HEADS):
            if hd + 1 < SB_HEADS:
                z_part(hd + 1)
            if hd in (2, 4, 6):
                heads_lo(hd // 2 - 1)
            conv(1)
            log_w(hd)
            if hd + 1 < SB_HEADS:
                softplus(hd + 1)
            conv(1)
            if hd in (4, 5, 7):
                prep({4: 19, 5: 20, 7: 21}[hd])
            if hd == 3:
                assert tap[0] == TAPS
                dve.wait_ge(*have("conv_mean", 1))
                V.scalar_tensor_tensor(out=conv_acc[:], in0=ps[:, 7, :].unsqueeze(1).to_broadcast([P, CC, T]),
                                       scalar=-1.0 / CH, in1=conv_acc[:], op0=ALU.mult, op1=ALU.add
                                       ).then_inc(sem("conv_centred"), 1)
            if hd == 5:
                dve.wait_ge(*have("conv_var", 1))
                V.tensor_scalar(conv_rs[:, 0, :], ps[:, 7, :], 1.0 / CH, EPS, ALU.mult, ALU.add
                                ).then_inc(sem("conv_var_ready"), 1)
            if hd == 6:
                dve.wait_ge(*have("conv_root", 2))
                own(V.tensor_tensor(conv_t[:], conv_rs[:, 1, :], conv_rs[:, 1, :], ALU.mult))
                own(V.scalar_tensor_tensor(out=conv_t[:], in0=conv_t[:], scalar=-0.5, in1=conv_rs[:, 0, :],
                                           op0=ALU.mult, op1=ALU.mult))
                own(V.scalar_tensor_tensor(out=conv_rs[:, 1, :], in0=conv_t[:], scalar=1.5, in1=conv_rs[:, 1, :],
                                           op0=ALU.add, op1=ALU.mult))
                V.tensor_tensor(conv_acc[:], conv_acc[:], conv_rs[:, 1, :].unsqueeze(1).to_broadcast([P, CC, T]),
                                ALU.mult).then_inc(sem("conv_normed"), 1)
        heads_lo(3)
        for m in range(CC):
            dve.wait_ge(*have("conv_hi", m + 1))
            low("conv_lo", a_lo[:, m, :], conv_sq[:, m, :], a_hi[:, m, :])

        def residual_stage(name, part_name, d):
            if name == "h_ffn0":
                prep(d + 2)
                norm("mem1")
                norm_tiles("mem1")
                prep(d + 3)
                split("mem1", "mem_split_hi1", "mem_split_lo1")
            prep(d + 3)
            dve.wait_ge(*have("w_used", d + 2))
            for i in range(TT):
                residual(part_name, 0, i)
            prep(d + 5)
            for i in range(TT):
                dve.wait_ge(*(have(f"tile_{name[2:]}", i + 1) if i < TT - 1 else have("w_used", d + 4)))
                residual(name, 1, i)
            prep(d + 6)

        def cross(l):
            d = first[f"xq{l}"]
            split(f"xa{l}", f"split_hi_xa{l}", f"split_lo_xa{l}")
            late_factors(f"xa{l}")
            prep(d + 4)
            for s in range(2):
                dve.wait_ge(*have("w_used", d + 2 * s + 2))
                dve.wait_ge(*have(f"factors_ready_xa{l}", 1))
                scaled(xq[:, 4 * s:4 * s + 4, :], s).then_inc(sem(f"xq_ready{l}"), 1)
                if s == 0:
                    prep(d + 6)
            for hd in range(XH + 1):
                if hd < XH:
                    dve.wait_ge(*have(f"x_scores{l}", hd + 1))
                    if hd:
                        dve.wait_ge(*have(f"x_exp{l}", TT * hd))
                    b = 2 * (hd % 2)
                    V.tensor_reduce(out=x_max[:], in_=ps[:, b:b + 2, :].rearrange("p a (i m) -> p (a i) m", m=M),
                                    axis=AX.X, op=ALU.max, negate=True).then_inc(sem(f"x_max{l}"), 1)
                if hd < XH:
                    dve.wait_ge(*have(f"x_exp{l}", TT * (hd + 1)))
                    own(V.reciprocal(x_rec[:], x_sum[:]))
                    V.tensor_tensor(xp[:, hd % 2], xp[:, hd % 2], x_rec[:].unsqueeze(2).to_broadcast([P, TT, M]),
                                    ALU.mult).then_inc(sem(f"x_probs{l}"), 1)
                if hd:
                    for c in range(2):
                        dve.wait_ge(*have(f"x_heads_hi{l}", 2 * hd - 1 + c))
                        low(f"x_heads_lo{l}", a_lo[:, 2 * hd - 2 + c, :], ps[:, 6 + c, :], a_hi[:, 2 * hd - 2 + c, :])

        def bc(ap, shape):
            return ap.to_broadcast(shape)

        def router(l):
            dve.wait_ge(*have(f"logits{l}", TT))
            dve.wait_ge(*have("router_loaded", 64 * NL))
            small_bank = 4 if l == 0 else 0
            own(V.tensor_tensor(lg[:], ps[:, small_bank, 0:TT * (NG + NE)].rearrange("p (i n) -> p i n", i=TT),
                                bc(n_y[:].unsqueeze(2), [P, TT, NG + NE]), ALU.mult))
            own(V.tensor_tensor(lg[:], lg[:], bc(rt_b[:, l, :].unsqueeze(1), [P, TT, NG + NE]), ALU.add))
            S4 = [P, TT, NG]
            S44 = [P, TT, NG, EPG]
            four = bc(iota4[:].unsqueeze(1), S4)

            def argmax(src, hot, top):
                own(V.tensor_reduce(out=top[:], in_=src, axis=AX.X, op=ALU.max))
                own(V.tensor_tensor(r4c[:], src, bc(top[:].unsqueeze(2), S4), ALU.is_equal))
                own(V.scalar_tensor_tensor(out=r4c[:], in0=r4c[:], scalar=-FAR, in1=four, op0=ALU.mult, op1=ALU.add))
                own(V.tensor_reduce(out=slot_f[:, 0:TT], in_=r4c[:], axis=AX.X, op=ALU.min))
                own(V.tensor_tensor(hot[:], r4c[:], bc(slot_f[:, 0:TT].unsqueeze(2), S4), ALU.is_equal))

            argmax(lg[:, :, 0:NG], oh_g, r1a)
            V.tensor_tensor(r4a[:], lg[:, :, 0:NG], bc(r1a[:].unsqueeze(2), S4), ALU.subtract
                            ).then_inc(sem(f"r_args{l}"), 1)
            experts4 = lg[:, :, NG:].rearrange("p i (g e) -> p i g e", g=NG)
            own(V.tensor_tensor(e_tmp[:], experts4, bc(oh_g[:].unsqueeze(3), S44), ALU.mult))
            own(V.tensor_reduce(out=le[:], in_=e_tmp[:].rearrange("p i g e -> p i e g"), axis=AX.X, op=ALU.add))
            argmax(le[:], oh_1, r1a)
            own(V.scalar_tensor_tensor(out=le[:], in0=oh_1[:], scalar=-1e30, in1=le[:], op0=ALU.mult, op1=ALU.add))
            argmax(le[:], oh_2, gate1)
            V.tensor_tensor(r1a[:], gate1[:], r1a[:], ALU.subtract).then_inc(sem(f"r_args{l}"), 1)
            own(V.tensor_tensor(e_1[:].rearrange("p i (g e) -> p i g e", g=NG), bc(oh_g[:].unsqueeze(3), S44),
                                bc(oh_1[:].unsqueeze(2), S44), ALU.mult))
            own(V.tensor_tensor(e_2[:].rearrange("p i (g e) -> p i g e", g=NG), bc(oh_g[:].unsqueeze(3), S44),
                                bc(oh_2[:].unsqueeze(2), S44), ALU.mult))
            V.tensor_tensor(e_sum[:], e_1[:], e_2[:], ALU.add).then_inc(sem(f"assigned{l}"), 1)
            if l == 0:
                prep(first["vx1"] + 2)
            dve.wait_ge(*have(f"ranks{l}", 1))
            own(V.tensor_copy(count[:], ps[:, small_bank + 1, TT * NE:(TT + 1) * NE]))
            own(V.tensor_copy(rank[:], ps[:, small_bank + 1, 0:TT * NE].rearrange("p (i e) -> p i e", i=TT)))
            own(V.tensor_scalar(over[:], count[:], P + 0.5, None, ALU.is_gt))
            for n in range(2, T // P):
                own(V.scalar_tensor_tensor(out=over[:], in0=count[:], scalar=n * P + 0.5, in1=over[:],
                                           op0=ALU.is_gt, op1=ALU.add))
            own(V.memset(scan[:], 0.0))
            own(V.tensor_copy(scan[:, 0, NE:], over[:]))
            cur, step = 0, 1
            while step < NE:
                own(V.tensor_tensor(scan[:, 1 - cur, NE:], scan[:, cur, NE:], scan[:, cur, NE - step:2 * NE - step],
                                    ALU.add))
                cur, step = 1 - cur, 2 * step
            incl = scan[:, cur, NE:]
            own(V.tensor_tensor(b_hi[:], incl, over[:], ALU.subtract))
            own(V.tensor_scalar(b_hi[:], b_hi[:], float(P), float(P * (NE - 1)), ALU.mult, ALU.add))
            own(V.tensor_tensor(b_hi[:], b_hi[:], slot_lo[:], ALU.subtract))
            SE = [P, TT, NE]
            own(V.tensor_scalar(slots[:], rank[:], P - 0.5, None, ALU.is_gt))
            own(V.tensor_tensor(slots[:], slots[:], bc(b_hi[:].unsqueeze(1), SE), ALU.mult))
            own(V.tensor_tensor(slots[:], slots[:], bc(slot_lo[:].unsqueeze(1), SE), ALU.add))
            own(V.tensor_tensor(slots[:], slots[:], rank[:], ALU.add))
            for c, e_c in enumerate((e_1, e_2)):
                own(V.tensor_tensor(rank[:], slots[:], e_c[:], ALU.mult))
                own(V.tensor_reduce(out=slot_f[:, c * TT:(c + 1) * TT], in_=rank[:], axis=AX.X, op=ALU.add))
            own(V.tensor_copy(slot_i[:], slot_f[:]))
            own(V.tensor_single_scalar(row_i[:], slot_i[:], P - 1, ALU.bitwise_and))
            own(V.tensor_single_scalar(blk_i[:], slot_i[:], 7, ALU.logical_shift_right))
            own(V.tensor_copy(row_f[:], row_i[:]))
            own(V.tensor_copy(blk_f[:], blk_i[:]))
            J = 2 * TT
            V.tensor_tensor(slot_hot[:], bc(iota_p[:].unsqueeze(1), [P, J, P]), bc(row_f[:].unsqueeze(2), [P, J, P]),
                            ALU.is_equal).then_inc(sem(f"hots{l}"), 1)
            own(V.tensor_tensor(blk_hot[:], bc(iota_b[:].unsqueeze(1), [P, J, NB]), bc(blk_f[:].unsqueeze(2), [P, J, NB]),
                                ALU.is_equal))
            V.tensor_tensor(tok_hot[:].rearrange("p (c i) b -> p c i b", c=2),
                            blk_hot[:].rearrange("p (c i) b -> p c i b", c=2),
                            bc(tok_no[:].unsqueeze(1).unsqueeze(3), [P, 2, TT, NB]), ALU.mult
                            ).then_inc(sem(f"hots{l}"), 1)
            own(V.tensor_tensor(own_cmp[:], bc(incl.unsqueeze(1), [P, OVERFLOW, NE]),
                                bc(iota_b[:, 0:OVERFLOW].unsqueeze(2), [P, OVERFLOW, NE]), ALU.is_le))
            own(V.tensor_reduce(out=own_f[:], in_=own_cmp[:], axis=AX.X, op=ALU.add))
            own(V.tensor_scalar(own_f[:], own_f[:], float(NE - 1), None, ALU.min))
            own(V.tensor_copy(own_i[:], own_f[:]))
            V.tensor_copy(nov_i[:], incl[:, NE - 1:NE]).then_inc(sem(f"overflow_known{l}"), 1)
            if l == 0:
                prep(first["vx1"] + 4)
            dve.wait_ge(*have(f"table{l}", 1))
            own(V.tensor_copy(tok_f[:], ps[:, small_bank, 0:NB]))
            own(V.tensor_scalar(tok_e[:], tok_f[:], 0.0, FAR, ALU.is_equal, ALU.mult))
            own(V.scalar_tensor_tensor(out=tok_f[:], in0=tok_f[:], scalar=-1.0, in1=tok_e[:], op0=ALU.add,
                                       op1=ALU.add))
            V.tensor_copy(tok_i[:], tok_f[:]).then_inc(sem(f"table_ready{l}"), 1)
            dve.wait_ge(*have(f"r_exp{l}", 2))
            own(V.tensor_reduce(out=p_top[:], in_=r4b[:], axis=AX.X, op=ALU.add))
            own(V.reciprocal(p_top[:], p_top[:]))
            own(V.tensor_scalar(r1a[:], r1b[:], 1.0, None, ALU.add))
            own(V.reciprocal(r1a[:], r1a[:]))
            own(V.tensor_tensor(gate1[:], r1a[:], p_top[:], ALU.mult))
            own(V.tensor_tensor(gate2[:], gate1[:], r1b[:], ALU.mult))

        def experts(l):
            gain = vecs[:, FFN_G + l * KD:FFN_G + (l + 1) * KD]
            norm(f"ffn{l}")
            if l == 0:
                prep(first["kx1"] + 3)
            for i in range(TT):
                norm_tiles(f"ffn{l}", [i])
                b0 = (4 * (l == 0) + 2 * i) % 8
                dve.wait_ge(*have(f"xn_t_in_psum_ffn{l}", i + 1))
                V.tensor_tensor(a_full[:, :, i * P:(i + 1) * P],
                                ps[:, b0:b0 + 2, :].rearrange("p a (b n) -> p (a b) n", n=P),
                                bc(gain.unsqueeze(2), [P, KD, P]), ALU.mult).then_inc(sem(f"a_full{l}"), 1)
            if l == 0:
                prep(first["kx1"] + 4)
            router(l)
            prep(first[f"moe{l}"] + 2)

            def rows_lo(e, b):
                dve.wait_ge(*have(f"xs_hi{l}", b + 1))
                V.tensor_tensor(xs_lo[:, e].rearrange("p k n -> p (k n)"), ps[:, 0:2, :].rearrange("p a n -> p (a n)"),
                                xs_hi[:, e].rearrange("p k n -> p (k n)").bitcast(fp32), ALU.subtract
                                ).then_inc(sem(f"xs_lo{l}"), 1)

            def hidden_lo(e, b):
                dve.wait_ge(*have(f"hidden_hi{l}", b + 1))
                V.tensor_tensor(hid_lo[:, e].rearrange("p c n -> p (c n)"), ps[:, 4, 0:2 * P],
                                hid_hi[:, e].rearrange("p c n -> p (c n)").bitcast(fp32), ALU.subtract
                                ).then_inc(sem(f"hidden_lo{l}"), 1)

            def y_right(e, n):
                dve.wait_ge(*have("w_used", n + 1))
                V.tensor_copy(y_sb[:, e, BANK:], ps[:, 6, :]).then_inc(sem(f"y_right{l}"), 1)

            def block_of(i, e, first_pair, last_pair):
                b = 2 * i + e
                last_block = last_pair and e == 1
                if not last_block:
                    rows_lo(1 - e, b + 1)
                if not (first_pair and e == 0):
                    hidden_lo(1 - e, b - 1)
                lo_part(*entry(l, 3 * e + 2, i), end=GC * BANK // 2 if last_block else GC * BANK)
                dve.wait_ge(*have(f"silu{l}", b + 1))
                V.tensor_tensor(hid[:, e, :], ps[:, 2 + e, FE:2 * FE], silu_g[:, e, :], ALU.mult
                                ).then_inc(sem(f"hidden{l}"), 1)
                if not last_block:
                    lo_part(*entry(l, 3 * e + 3, i))
                if not (first_pair and e == 0):
                    if not first_pair:
                        dve.wait_ge(*have(f"y_stored{l}_{e}", 16 * i))
                    y_right(1 - e, entry(l, 3 * e + 1, i)[0])
                if not last_block:
                    lo_part(*entry(l, 3 * e + 4, i), end=GC * BANK // 2)

            rows_lo(0, 0)
            for e in range(2):
                block_of(0, e, True, False)
            with dve.Fori(1, NE // 2 - 1) as i:
                for e in range(2):
                    block_of(i, e, False, False)
            for e in range(2):
                block_of(NE // 2 - 1, e, False, True)
            hidden_lo(1, NE - 1)
            y_right(1, first[f"moe{l}"] + 3 * NE - 1)
            n_prep[0] += 3 * NE - 2

            dve.wait_ge(*have(f"y_stored{l}_1", 16 * (NE // 2)))
            n_over = dve.value_load(nov_i[0:1, 0:1])
            with dve.If(n_over > 0):
                with dve.Fori(0, OVERFLOW) as j:
                    V.tensor_copy(idx_c[:], tok_i[:, bass.ds(j + NE, 1)]).then_inc(sem(f"over_index{l}"), 1)
                    dve.wait_ge(*have(f"over_products{l}", 4 * j + 1))
                    V.tensor_copy(xs_full[:].rearrange("p k n -> p (k n)"), ps[:, 0:2, :].rearrange("p a n -> p (a n)")
                                  ).then_inc(sem(f"over_x_t{l}"), 1)
                    dve.wait_ge(*have(f"over_silu{l}", j + 1))
                    V.tensor_tensor(hid[:, 0, :], ps[:, 2, FE:2 * FE], silu_g[:, 0, :], ALU.mult
                                    ).then_inc(sem(f"over_hidden{l}"), 1)
                    dve.wait_ge(*have(f"over_products{l}", 4 * j + 4))
                    V.tensor_copy(y_sb[:, 0, BANK:], ps[:, 6, :]).then_inc(sem(f"over_y{l}"), 1)
                    dve.wait_ge(*have(f"over_stored{l}", 16 * j + 16))

            for j in range(2 * TT):
                i, c = j // 2, j % 2
                if l == 0 and j in (0, 4):
                    prep(first["c_v"] + 1 + j // 4)
                dve.wait_ge(*have(f"y_gathered{l}_{j % 4}", 16 * (j // 4 + 1)))
                if c:
                    dve.wait_ge(*have(f"combined{l}", j))
                V.scalar_tensor_tensor(out=h[:, i, :], in0=y_back[:, j % 4, :],
                                       scalar=(gate2 if c else gate1)[:, i:i + 1], in1=h[:, i, :],
                                       op0=ALU.mult, op1=ALU.add).then_inc(sem(f"combined{l}"), 1)

        residual_stage("h_xa0", "h_part_xa0", first["mix_out0"])
        cross(0)
        residual_stage("h_ffn0", "h_part_ffn0", first["xo0"])
        experts(0)

        split("mix1", "split_hi_mix1", "split_lo_mix1")
        late_factors("mix1")
        d = first["c_v"]
        prep(d + 6)
        for s in range(2):
            for i in range(TT):
                dve.wait_ge(*have("v_gelu", TT * s + i + 1))
                V.bn_stats(v_st[:, i, s, :], v_c[:, i, s * BANK:(s + 1) * BANK]).then_inc(sem("v_stats"), 1)
        for i in range(TT):
            dve.wait_ge(*have("v_stats", TT + i + 1))
            own(V.bn_aggr(v_mv[:, i, :], v_st[:, i].rearrange("p a b -> p (a b)")))
        V.tensor_scalar(n_var[:], v_mv[:, :, 1], EPS, None, ALU.add).then_inc(sem("norm_var_v"), 1)
        dve.wait_ge(*have("norm_var_v", 1))
        rstd("v", TT, n_var[:])
        prep(d + 7)
        dve.wait_ge(*have("vnorm_loaded", 32))
        for i in range(TT):
            V.tensor_scalar(v_c[:, i, :], v_c[:, i, :], v_mv[:, i, 0:1], n_y[:, i:i + 1], ALU.subtract, ALU.mult
                            ).then_inc(sem("v_centred"), 1)
        for i in range(TT):
            dve.wait_ge(*have("v_centred", i + 1))
            V.tensor_tensor(v_c[:, i, :], v_c[:, i, :], vg_b[:], ALU.mult).then_inc(sem("v_gained"), 1)
        prep(d + 8)
        for i in range(TT):
            dve.wait_ge(*have("v_gained", i + 1))
            V.tensor_tensor(v_c[:, i, :], v_c[:, i, :], vb_b[:], ALU.add).then_inc(sem("v_normed"), 1)
        for s in range(2):
            dve.wait_ge(*have("w_used", d + 6 + 2 * s))
            scaled(u_c[:, 4 * s:4 * s + 4, :], s).then_inc(sem("u_scaled"), 1)
            prep(d + 9 + s)
        dve.wait_ge(*have("bs_loaded", 16))
        for g in range(GM):
            dve.wait_ge(*have("mixed_in_psum", g + 1))
            dve.wait_ge(*have("u_gelu", g // 4 + 1))
            m3 = ps[:, g, :].rearrange("p (c t) -> p c t", c=TT)
            own(V.tensor_tensor(m3, m3, bs_b[:, g, :].unsqueeze(1).to_broadcast([P, TT, P]), ALU.add))
            V.tensor_tensor(u_c[:, g, :], ps[:, g, :], u_c[:, g, :], ALU.mult).then_inc(sem("gated"), 1)
        residual_stage("h_xa1", "h_part_xa1", first["mix_out1"])
        cross(1)
        residual_stage("h_ffn1", "h_part_ffn1", first["xo1"])
        experts(1)
        norm("fin1")
        dve.wait_ge(*have("final_gain_loaded", 16))
        for i in range(TT):
            if i >= 2:
                dve.wait_ge(*have(f"out_stored{i % 2}", 16))
            V.scalar_tensor_tensor(out=xn[:, i % 2, :], in0=h[:, i, :], scalar=n_y[:, i:i + 1], in1=fg_b[:],
                                   op0=ALU.mult, op1=ALU.mult).then_inc(sem("out_ready"), 1)

    ctx.close()


_INS = ["x", "mem", "mem_norm_g", "norm_mix", "norm_xa", "norm_ffn", "final_norm_g",
        "ab_w_in", "ab_conv_w", "ab_conv_b", "ab_cnorm_g", "ab_cnorm_b", "ab_w_out",
        "c_w_in", "c_vnorm_g", "c_vnorm_b", "c_ws", "c_bs", "c_w_out",
        "xa_wq", "xa_wk", "xa_wv", "xa_wo", "rt_wg", "rt_bg", "rt_we", "rt_be",
        "ex_w_gate", "ex_w_up", "ex_w_down"]


def kernel(**inputs):
    import numpy as _np
    import concourse.bacc as _bacc
    from concourse import mybir as _mybir
    from concourse.bass_utils import run_bass_kernel_spmd as _run

    nc = _bacc.Bacc("TRN2", target_bir_lowering=False, num_devices=1)
    arrays, args = {}, []
    for name in _INS:
        a = _np.ascontiguousarray(inputs[name])
        arrays[f"in_{name}"] = a
        args.append(nc.dram_tensor(f"in_{name}", a.shape, _mybir.dt.from_np(a.dtype), kind="ExternalInput").ap())
    shape = tuple(inputs["x"].shape)
    args.append(nc.dram_tensor("out_0", shape, _mybir.dt.float32, kind="ExternalOutput").ap())
    trunk_program(nc, *args)
    return _run(nc, [arrays], core_ids=[0]).results[0]["out_0"]
```

```python
import concourse.bass as bass
from concourse import mybir
from contextlib import ExitStack


def trunk_program(nc, x, mem, mem_norm_g, norm_mix, norm_xa, norm_ffn, final_norm_g,
                  ab_w_in, ab_conv_w, ab_conv_b, ab_cnorm_g, ab_cnorm_b, ab_w_out,
                  c_w_in, c_vnorm_g, c_vnorm_b, c_ws, c_bs, c_w_out,
                  xa_wq, xa_wk, xa_wv, xa_wo, rt_wg, rt_bg, rt_we, rt_be,
                  ex_w_gate, ex_w_up, ex_w_down, out):
    fp32, fp32r, i32 = mybir.dt.float32, mybir.dt.float32r, mybir.dt.int32
    ALU, ACT, AX = mybir.AluOpType, mybir.ActivationFunctionType, mybir.AxisListType

    P = 128
    _, T, D = x.shape
    M = mem.shape[1]
    EPS = 1e-6
    TT, KD, MT = T // P, D // P, M // P
    BANK = 512
    NL = norm_mix.shape[0]
    TAPS, CH = ab_conv_w.shape[1], ab_conv_w.shape[2]
    CC = CH // P
    PAD = TAPS - 1
    SB_HEADS, SB_DH = 8, 64
    XH = 4
    XD = D // XH
    NG, EPG = rt_wg.shape[2], rt_we.shape[2] // rt_wg.shape[2]
    NE = NG * EPG
    FE = ex_w_gate.shape[3]
    OVERFLOW = (2 * T) // (P + 1)
    NB = NE + OVERFLOW + 1
    GC = 4
    RING, SPLIT = 6, 3
    GM = c_ws.shape[1]
    FAR = 1000.0

    ctx = ExitStack()
    sems, place = {}, {}

    def family(shared, members):
        base = 0
        for name, n in members:
            place[name] = (shared, base)
            base += n

    def sem(name):
        shared = place.get(name, (name, 0))[0]
        if shared not in sems:
            sems[shared] = ctx.enter_context(nc.semaphore(shared))
        return sems[shared]

    def have(name, n):
        return sem(name), n + place.get(name, (name, 0))[1]

    for name, n in (("a_even", TT // 2), ("a_odd", TT // 2), ("logits_out", 1), ("logits_t", 1), ("assigned", 1),
                    ("combined", 2 * TT), ("xs_hi", NE),
                    ("hidden", NE), ("hidden_hi", NE), ("hidden_lo", NE), ("hidden_t_in_psum", NE),
                    ("hots", 2), ("logits", TT),
                    ("overflow_known", 1), ("r_exp", 2), ("r_args", 2), ("ranks", 1),
                    ("silu", NE), ("table", 1), ("table_ready", 1),
                    ("x_exp", TT * XH), ("x_heads_hi", KD), ("x_heads_in_psum", XH), ("x_heads_lo", KD),
                    ("x_max", XH), ("x_probs", XH), ("x_probs_t", XH), ("x_probs_t_in_psum", XH), ("x_scores", XH),
                    ("xq_ready", 2), ("xs_cleared", 1), ("xs_t_in_psum", NE), ("xs_lo", NE), ("down_lo_pool", NE),
                    ("xn_gained", TT), ("y_left", NE),
                    ("y_right", NE), ("kx_ready", 2), ("vx_ready", 2), ("mem_t_in_psum", MT),
                    ("mem_split_hi", KD), ("mem_split_lo", KD), ("h_xa", TT), ("h_ffn", TT), ("h_part_xa", TT),
                    ("h_part_ffn", TT), ("tile_xa", TT - 1), ("tile_ffn", TT - 1)):
        family(name, [(f"{name}{l}", n) for l in range(NL)])
    for name, slots_of, n in (("gathered", 2, 8 * NE), ("xn_stored", 2, 8 * TT), ("y_stored", 2, 8 * NE),
                              ("y_gathered", 4, 8 * TT)):
        for s in range(slots_of):
            family(f"{name}_{s}", [(f"{name}{l}_{s}", n) for l in range(NL)])
    NORMS = [("mix0", TT), ("mem0", MT), ("xa0", TT), ("mem1", MT), ("ffn0", TT), ("mix1", TT), ("v", 0),
             ("xa1", TT), ("ffn1", TT)]
    family("squares_act", [(f"squares_act_{tag}", n if tag[:3] == "ffn" else n // 2) for tag, n in NORMS] +
           [("squares_act_fin", TT)])
    family("norm_var", [(f"norm_var_{tag}", 1) for tag, n in NORMS] +
           [("norm_var_fin0", 1), ("fin_factors", 1), ("norm_var_fin1", 1)])
    family("norm_root", [(f"norm_root_{tag}", 1) for tag, n in NORMS] +
           [("norm_root_fin0", 1), ("fin_scaled", 1), ("norm_root_fin1", 1)])
    LATE = ("xa0", "mix1", "xa1")
    family("xn", [(f"xn_{tag}", n) for tag, n in NORMS if tag not in LATE])
    family("xn_t_in_psum", [(f"xn_t_in_psum_{tag}", 2 if tag in LATE else n) for tag, n in NORMS if tag[:3] != "mem"])
    for name in ("diag_ready", "factors_in_psum", "factors_ready"):
        family(name, [(f"{name}_{tag}", 1) for tag in LATE])
    family("mixer0_act", [("gate_done", 1), ("q_ready", 1), ("k_ready", 1), ("v_ready", 1)])
    family("conv_dve", [("glu_done", 1), ("conv_taps", CC * TAPS), ("conv_centred", 1), ("conv_var_ready", 1),
                        ("conv_normed", 1), ("conv_lo", CC)])
    family("conv_act", [("conv_squared", 1), ("conv_root", 2)])
    family("conv_pe", [("conv_mean", 1), ("conv_var", 1)])
    family("mixer1_act", [("ws_t_ready", 1), ("v_gelu", 2 * TT), ("u_gelu", 2), ("gated_hi", KD)])
    family("mixer1_dve", [("v_stats", 2 * TT), ("v_centred", TT), ("v_gained", TT), ("v_normed", TT),
                          ("u_scaled", 2), ("gated", KD)])
    family("mixer1_pe", [("ws_t_in_psum", 1), ("mixed_in_psum", KD)])
    for part in ("split_hi", "split_lo"):
        family(part, [(f"{part}_{tag}", KD) for tag in ("mix0", "xa0", "mix1", "xa1")])

    BASE = 16512
    K = 1024

    def at(name, shape, dt, offset):
        return nc.alloc_sbuf_tensor_at(name, shape, dt, offset=BASE + int(offset))

    raw = at("raw", [P, RING, GC * BANK], fp32, 0)
    w_lo = at("w_lo", [P, RING, GC * BANK], fp32r, 0)
    EXTRA = [{45: 148, 46: 104, 47: 120}, {41: 148, 42: 104, 43: 120, 44: 128, 45: 136, 46: 172, 47: 180}]
    MORE = NE // 2 - 2
    raw_extra, lo_extra = ([{g: at(f"{name}_extra{l}_{g}", [P, GC * BANK], dt, o * K) for g, o in EXTRA[l].items()}
                            for l in range(NL)] for name, dt in (("raw", fp32), ("lo", fp32r)))

    def raw_at(slot):
        return raw[:, slot, :] if isinstance(slot, int) else raw_extra[slot[1]][slot[2]][:]

    def lo_at(slot):
        return w_lo[:, slot, :] if isinstance(slot, int) else lo_extra[slot[1]][slot[2]][:]

    def arrivals_of(slot):
        return sem(f"raw_loaded{slot}" if isinstance(slot, int) else f"raw_extra_loaded{slot[2]}")

    w_hi = at("w_hi", [P, SPLIT, GC * BANK], fp32r, 48 * K)
    h = at("h", [P, TT, D], fp32, 80 * K)
    a_hi = at("a_hi", [P, KD, T], fp32r, 96 * K)
    a_lo = at("a_lo", [P, KD, T], fp32r, 112 * K)
    mem_hi = at("mem_hi", [P, KD, M], fp32r, 128 * K)
    mem_lo = at("mem_lo", [P, KD, M], fp32r, 136 * K)
    xn = at("xn", [P, 2, D], fp32, 148 * K)
    xn_more = at("xn_more", [P, 2, D], fp32, 120 * K)
    mem_tok = at("mem_tok", [P, MT, D], fp32, 180 * K)
    q_t = at("q_t", [P, CC, T], fp32, 148 * K)
    k_t = at("k_t", [P, CC, T], fp32, 156 * K)
    v_s = at("v_s", [P, TT, CH], fp32, 164 * K)
    ZW = 1280
    zbuf = at("zbuf", [P, 2, ZW], fp32, 128 * K)
    sbuf = at("sbuf", [P, 2, ZW], fp32, 138 * K)
    CIN_W = T + PAD
    conv_in = at("conv_in", [P, CC, CIN_W], fp32, 188 * K)
    conv_sq = at("conv_sq", [P, CC, T], fp32, 188 * K)
    conv_acc = at("conv_acc", [P, CC, T], fp32, 196.5 * K)
    conv_rs = at("conv_rs", [P, 2, T], fp32, 148 * K)
    conv_t = at("conv_t", [P, T], fp32, 156 * K)
    diag = at("diag", [P, TT, P], fp32, 136 * K)
    factors = at("factors", [P, T], fp32, 134 * K)
    kx = at("kx", [P, KD, M], fp32, 172 * K)
    vx = at("vx", [P, MT, D], fp32, 180 * K)
    xq = at("xq", [P, KD, T], fp32, 148 * K)
    xp = at("xp", [P, 2, TT, M], fp32, 188 * K)
    xpt = at("xpt", [P, 2, MT, T], fp32, 164 * K)
    v_c = at("v_c", [P, TT, D], fp32, 148 * K)
    u_c = at("u_c", [P, KD, T], fp32, 188 * K)
    vg_b = at("vg_b", [P, D], fp32, 164 * K)
    vb_b = at("vb_b", [P, D], fp32, 168 * K)
    ws_in = at("ws_in", [P, GM, P], fp32, 160 * K)
    ws_t = at("ws_t", [P, GM, P], fp32, 144 * K)
    bs_b = at("bs_b", [P, GM, P], fp32, 128 * K)
    a_full = at("a_full", [P, KD, T], fp32, 96 * K)
    logits_w = at("logits_w", [NG + NE, T], fp32, 162 * K)
    xs = at("xs", [P, 2, D], fp32, 112 * K)
    gain_b = at("gain_b", [P, D], fp32, 76 * K)
    xg = at("xg", [P, 2, D], fp32, 164 * K)
    xs_hi = at("xs_hi", [P, 2, KD, P], fp32r, 164 * K)
    xs_lo = at("xs_lo", [P, 2, KD, P], fp32r, 96 * K)
    xs_full = at("xs_full", [P, KD, P], fp32, 164 * K)
    y_sb = at("y_sb", [P, 2, D], fp32, 188 * K)
    silu_g = at("silu_g", [P, 2, FE], fp32, 196 * K)
    hid = at("hid", [P, 2, FE], fp32, 198 * K)
    hid_hi = at("hid_hi", [P, 2, 2, P], fp32r, 200 * K)
    hid_lo = at("hid_lo", [P, 2, 2, P], fp32r, 160 * K)
    hid_full = at("hid_full", [P, 2, P], fp32, 200 * K)
    y_back = at("y_back", [P, 4, D], fp32, 96 * K)
    over_w = [at(f"over_w{i}", [P, GC * BANK], fp32, o * K) for i, o in enumerate((96, 104, 148))]
    slot_hot = at("slot_hot", [P, 2 * TT, P], fp32r, 188 * K)
    before_f = at("before_f", [P, P], fp32, 202 * K)
    before = at("before", [P, P], fp32r, 72 * K)
    ones_r = at("ones_r", [P, P], fp32r, 72.5 * K)
    iota_p = at("iota_p", [P, P], fp32, 73 * K)
    rt_w = at("rt_w", [P, NL, KD, NG + NE], fp32, 73.5 * K)
    rt_b = at("rt_b", [P, NL, NG + NE], fp32, 75 * K)
    rt_off = [144 * K]

    def small(name, shape, dt=fp32):
        n = 1
        for s in shape:
            n *= s
        if rt_off[0] < 148 * K < rt_off[0] + 4 * n:
            rt_off[0] = 156 * K
        assert rt_off[0] + 4 * n <= 160 * K
        t = at(name, [P] + shape, dt, rt_off[0])
        rt_off[0] += (4 * n + 31) // 32 * 32
        return t

    lg = small("lg", [TT, NG + NE])
    r4a, r4b, r4c = (small(f"r4_{c}", [TT, NG]) for c in "abc")
    oh_g, oh_1, oh_2 = (small(n, [TT, NG]) for n in ("oh_g", "oh_1", "oh_2"))
    le = small("le", [TT, EPG])
    r1a, r1b, p_top, gate1, gate2 = (small(n, [TT]) for n in ("r1a", "r1b", "p_top", "gate1", "gate2"))
    e_1, e_2, rank, slots = (small(n, [TT, NE]) for n in ("e_1", "e_2", "rank", "slots"))
    e_sum = small("e_sum", [TT, NE], fp32r)
    e_tmp = small("e_tmp", [TT, NG, EPG])
    count, b_hi = (small(n, [NE]) for n in ("count", "b_hi"))
    over_pad, over_cmp, beyond = small("over_pad", [2 * NE]), small("over_cmp", [NE, T // P - 1]), small("beyond", [TT, NE])
    scan = small("scan", [2, 2 * NE])
    slot_f = small("slot_f", [2 * TT])
    slot_i = small("slot_i", [2 * TT], i32)
    row_i, blk_i = small("row_i", [2 * TT], i32), small("blk_i", [2 * TT], i32)
    row_f, blk_f = small("row_f", [2 * TT]), small("blk_f", [2 * TT])
    blk_hot = small("blk_hot", [2 * TT, NB])
    tok_hot = small("tok_hot", [2 * TT, NB], fp32r)
    tok_f, tok_e = small("tok_f", [NB]), small("tok_e", [NB])
    tok_i = small("tok_i", [NB], i32)
    own_cmp = small("own_cmp", [OVERFLOW, NE])
    own_f = small("own_f", [OVERFLOW])
    own_i = small("own_i", [OVERFLOW], i32)
    nov_i = small("nov_i", [1], i32)
    idx_c = small("idx_c", [1], i32)

    c_pool = at("constants", [P, (229344 - BASE - 209408) // 4], fp32, 204.5 * K)
    c_off = [0]

    def const(name, shape):
        n = 1
        for s in shape:
            n *= s
        t = c_pool[:, c_off[0]:c_off[0] + n]
        c_off[0] += n
        assert c_off[0] <= c_pool.shape[1], c_off
        return t if len(shape) == 1 else t.rearrange("p (a b) -> p a b", a=shape[0])

    ident, ones, tri, causal = (const(n, [P]) for n in ("ident", "ones", "tri", "causal"))
    NV = (1 + 3 * NL) * KD + 3 * CC
    vecs = const("vecs", [NV])
    taps = const("taps", [CC, TAPS])
    iota4, iota_b, slot_lo, slot_hi, tok_no = (const(n, s) for n, s in (
        ("iota4", [NG]), ("iota_b", [NB]), ("slot_lo", [NE]), ("slot_hi", [NE]), ("tok_no", [TT])))
    n_ss, n_var, n_y, n_t = (const(n, [4]) for n in ("n_ss", "n_var", "n_y", "n_t"))
    x_max, x_sum, x_rec = (const(n, [TT]) for n in ("x_max", "x_sum", "x_rec"))
    v_st, v_mv = at("v_st", [P, TT, 2, 6], fp32, 132 * K), at("v_mv", [P, TT, 2], fp32, 132 * K + 256)
    vec_in = at("vec_in", [P, P], fp32, 188 * K)
    tap_in = at("tap_in", [P, CH], fp32, 189 * K)
    fg_b = at("fg_b", [P, D], fp32, 76 * K)

    MEM_G, MIX_G, XA_G, FFN_G = 0, KD, (1 + NL) * KD, (1 + 2 * NL) * KD
    CONV_B, CN_G, CN_B = (1 + 3 * NL) * KD, (1 + 3 * NL) * KD + CC, (1 + 3 * NL) * KD + 2 * CC

    ps = ctx.enter_context(nc.psum_tensor("ps", [P, 8, BANK], fp32))

    xn_dram = [nc.dram_tensor(f"xn_dram{l}", [T, D], fp32, kind="Internal").ap() for l in range(NL)]
    ys_dram = [nc.dram_tensor(f"ys_dram{l}", [(NB - 1) * P, D], fp32, kind="Internal").ap() for l in range(NL)]

    def slabs(w, cols):
        return [w[:, c:c + BANK] for c in cols]

    stream, ring_pos, ring_count, first, slot_total, in_ring = [], [], [], {}, {}, []

    def push(what, arrivals, slot=None):
        if slot is None:
            slot = len(in_ring) % RING
            in_ring.append(len(stream))
        place_of = slot if isinstance(slot, int) else slot[2] + RING
        slot_total[place_of] = slot_total.get(place_of, 0) + 16 * arrivals
        ring_pos.append(slot)
        ring_count.append(slot_total[place_of])
        stream.append(what)

    def plan(name, sl):
        first[name] = len(stream)
        for w in sl:
            for half in range(2):
                push((w[half * GC * P:(half + 1) * GC * P, :].rearrange("(k p) n -> p k n", p=P),), 1)

    def plan_experts(l):
        first[f"moe{l}"] = len(stream)
        for b in range(NE + 1):
            for e, part in ((b, 0), (b, 1), (b - 1, 2)):
                if 0 <= e < NE:
                    g = len(stream) - first[f"moe{l}"]
                    push((l, e, part), 2 if part < 2 else 1, ("extra", l, g) if g in EXTRA[l] else None)

    def entry(l, g, i):
        n0 = first[f"moe{l}"]
        if isinstance(i, int):
            n = n0 + 6 * i + g
            return n, ring_pos[n], ring_count[n], n % SPLIT
        n = n0 + 6 + g
        step = ring_count[n + 6] - ring_count[n]
        return 6 * i + (n0 + g), ring_pos[n], step * i + (ring_count[n] - step), n % SPLIT

    cols = lambda lo, n: range(lo, lo + n * BANK, BANK)
    plan("sb_gate", slabs(ab_w_in[0], [BANK]))
    plan("sb_a", slabs(ab_w_in[0], [0]))
    plan("sb_q", slabs(ab_w_in[0], [2 * BANK]))
    plan("sb_k", slabs(ab_w_in[0], [3 * BANK]))
    plan("sb_v", slabs(ab_w_in[0], [4 * BANK]))
    plan("kx0", slabs(xa_wk[0], cols(0, 2)))
    plan("vx0", slabs(xa_wv[0], cols(0, 2)))
    plan("mix_out0", slabs(ab_w_out[0], cols(0, 2)))
    plan("xq0", slabs(xa_wq[0], cols(0, 2)))
    plan("xo0", slabs(xa_wo[0], cols(0, 2)))
    plan("kx1", slabs(xa_wk[1], cols(0, 2)))
    plan("vx1", slabs(xa_wv[1], cols(0, 1)))
    plan_experts(0)
    plan("vx1_more", slabs(xa_wv[1], cols(BANK, 1)))
    plan("c_v", slabs(c_w_in[0], cols(D, 2)))
    plan("c_u", slabs(c_w_in[0], cols(0, 2)))
    plan("mix_out1", slabs(c_w_out[0], cols(0, 2)))
    plan("xq1", slabs(xa_wq[1], cols(0, 2)))
    plan("xo1", slabs(xa_wo[1], cols(0, 2)))
    plan_experts(1)

    def values_at(l, s):
        return first["vx1_more"] if l and s else first[f"vx{l}"] + 2 * s

    def expert_views(l, e, part):
        pick = (lambda w: w[l, bass.ds(e, 1)]) if not isinstance(e, int) else (lambda w: w[l, e:e + 1])
        if part < 2:
            rows = slice(part * GC * P, (part + 1) * GC * P)
            return [pick(w)[:, rows, :].rearrange("o (k p) n -> p (o k) n", p=P) for w in (ex_w_gate, ex_w_up)]
        return [pick(ex_w_down).rearrange("o (k p) n -> p (o k) n", p=P)]

    def load_expert(eng, l, e, part, dst, done):
        views = expert_views(l, e, part)
        if part < 2:
            d4 = dst.rearrange("p (k n) -> p k n", k=GC)
            eng.dma_start(d4[:, :, 0:FE], views[0]).then_inc(done, 16)
            eng.dma_start(d4[:, :, FE:2 * FE], views[1]).then_inc(done, 16)
        else:
            eng.dma_start(dst.rearrange("p (k n) -> p k n", k=2), views[0]).then_inc(done, 16)

    def norm_parts(tag):
        if tag.startswith("mem"):
            return MT, (lambda i: mem_tok[:, i, :]), "mem_loaded", MEM_G, mem_hi, mem_lo
        base = {"mix": MIX_G, "xa": XA_G, "ffn": FFN_G}[tag[:-1]]
        l = int(tag[-1])
        return TT, (lambda i: h[:, i, :]), f"h_{tag}", base + l * KD, a_hi, a_lo

    def xn_tile(i):
        return xn[:, i, :] if i < 2 else xn_more[:, i - 2, :]

    def source_ready(eng, tag, i):
        _, _, name, *_ = norm_parts(tag)
        if tag == "mix0":
            eng.wait_ge(*have(f"x_loaded{i}", 16))
        elif tag.startswith("mem"):
            eng.wait_ge(*have(f"mem_loaded{tag[-1]}", 16))
            if tag == "mem1":
                eng.wait_ge(*have("x_scores0", XH))
        elif tag == "mix1":
            eng.wait_ge(*have("combined0", 2 * i + 2))
        else:
            eng.wait_ge(*have(name, i + 1))

    OFF = {0: 512, 2: 512 + 384, 1: 1024}

    block = ctx.enter_context(nc.Block())

    @block.sync
    def _(sp):
        for i in range(TT):
            sp.dma_start(h[:, i, :], x[0, i * P:(i + 1) * P, :]).then_inc(sem(f"x_loaded{i}"), 16)
        sp.wait_ge(*have("vecs_loaded", 16 * 8))

        def load(n):
            slot = ring_pos[n]
            if isinstance(slot, int) and in_ring.index(n) >= RING:
                sp.wait_ge(*have("w_used", in_ring[in_ring.index(n) - RING] + 1))
            dst, done = raw_at(slot), arrivals_of(slot)
            if len(stream[n]) == 1:
                sp.dma_start(dst.rearrange("p (k n) -> p k n", k=GC), stream[n][0]).then_inc(done, 16)
            else:
                load_expert(sp, *stream[n], dst, done)

        def load_experts(l):
            m = first[f"moe{l}"]
            load(m)
            load(m + 1)
            if l:
                sp.wait_ge(*have(f"x_heads_in_psum{l}", XH))
                for g in range(44, 48):
                    load(m + g)
                for n in range(m + 2, m + 5):
                    load(n)
            x0 = min(EXTRA[l])
            sp.wait_ge(*have(f"xn_gained{l}", 2))
            load(m + x0)
            sp.wait_ge(*have(f"logits{l}", TT))
            load(m + x0 + 1)
            sp.wait_ge(*have(f"xn_gained{l}", TT))
            load(m + x0 + 2)
            if l == 0:
                for n in range(m + 2, m + 5):
                    load(n)
            with sp.Fori(1, MORE) as i:
                for g, (e, part) in enumerate(((0, 0), (0, 1), (-1, 2), (1, 0), (1, 1), (0, 2)), -1):
                    n, slot, _, _ = entry(l, g, i)
                    sp.wait_ge(*have("w_used", n - (RING - 1)))
                    load_expert(sp, l, 2 * i + e, part, raw[:, slot, :], arrivals_of(slot))
            for n in range(m + 6 * MORE - 1, m + 3 * NE):
                if n - m not in EXTRA[l]:
                    load(n)

        for n in range(first["moe0"]):
            load(n)
        load_experts(0)
        for n in range(first["vx1_more"], first["moe1"]):
            if n == first["c_v"] + 2:
                for s in range(4):
                    sp.wait_ge(*have(f"y_gathered0_{s}", 8 * TT))
            load(n)
        load_experts(1)
        for i in range(TT):
            sp.wait_ge(*(have("out_ready", i) if i else have("first_out_ready", 1)))
            sp.dma_start(out[0, i * P:(i + 1) * P, :], xn_tile(i)).then_inc(sem(f"out_stored{i % 2}"), 16)
        for i in range(2):
            sp.wait_ge(*have(f"out_stored{i}", 16 * (TT // 2)))

    @block.gpsimd
    def _(pool):
        pool_done = sem("pool_steps")
        n_own = [0]

        def own(ins):
            n_own[0] += 1
            ins.then_inc(pool_done, 1)
            pool.wait_ge(pool_done, n_own[0])

        last_row = pool.to_reg(T - 1)

        nc.gpsimd.memset(ones[:], 1.0).then_inc(sem("consts"), 1)
        own(nc.gpsimd.memset(ident[:], 1.0))
        nc.gpsimd.affine_select(out=ident[:], in_=ident[:], pattern=[[-1, P]], compare_op=ALU.is_equal,
                                fill=0.0, base=0, channel_multiplier=1).then_inc(sem("consts"), 1)
        own(nc.gpsimd.memset(tri[:], 1.0))
        nc.gpsimd.affine_select(out=tri[:], in_=tri[:], pattern=[[-1, P]], compare_op=ALU.is_ge,
                                fill=0.0, base=0, channel_multiplier=1).then_inc(sem("consts"), 1)
        own(nc.gpsimd.memset(causal[:], 0.0))
        nc.gpsimd.affine_select(out=causal[:], in_=causal[:], pattern=[[1, P]], compare_op=ALU.is_gt,
                                fill=-1e30, base=0, channel_multiplier=-1).then_inc(sem("consts"), 1)
        for t, pattern, base, ch in ((iota4, [[1, NG]], 0, 0), (iota_b, [[1, NB]], 0, 0),
                                     (slot_lo, [[P, NE]], 0, 0), (slot_hi, [[-P, NE]], P * (NE - 1), 0), (tok_no, [[P, TT]], 1, 1)):
            nc.gpsimd.iota(t[:], pattern, base=base, channel_multiplier=ch,
                           allow_small_or_imprecise_dtypes=True).then_inc(sem("consts"), 1)
        own(nc.gpsimd.memset(before_f[:], 1.0))
        nc.gpsimd.affine_select(out=before_f[:], in_=before_f[:], pattern=[[1, P]], compare_op=ALU.is_gt,
                                fill=0.0, base=0, channel_multiplier=-1).then_inc(sem("router_consts"), 1)
        nc.gpsimd.iota(iota_p[:], [[1, P]], base=0, channel_multiplier=0,
                       allow_small_or_imprecise_dtypes=True).then_inc(sem("router_consts"), 1)
        with nc.allow_non_contiguous_dma(reason="router weights are narrow"):
            for l in range(NL):
                pool.dma_start(rt_w[:, l, :, 0:NG], rt_wg[l].rearrange("(k p) n -> p k n", p=P)
                               ).then_inc(sem("router_loaded"), 16)
                pool.dma_start(rt_w[:, l, :, NG:], rt_we[l].rearrange("(k p) n -> p k n", p=P)
                               ).then_inc(sem("router_loaded"), 16)
                pool.dma_start(rt_b[:, l, 0:NG], rt_bg[l:l + 1, :].to_broadcast([P, NG])
                               ).then_inc(sem("router_loaded"), 16)
                pool.dma_start(rt_b[:, l, NG:], rt_be[l:l + 1, :].to_broadcast([P, NE])
                               ).then_inc(sem("router_loaded"), 16)
        pool.wait_ge(*have("vecs_ready", 2))
        nc.gpsimd.memset(conv_in[:, :, 0:PAD], 0.0).then_inc(sem("conv_padded"), 1)

        def gather_results(l, blocks):
            for j in range(2 * TT):
                if j >= 4:
                    pool.wait_ge(*have(f"combined{l}", j - 3))
                col = (j % 2) * TT + j // 2
                pool.indirect_dma_start(out=y_back[:, j % 4, :], out_offset=None, in_=ys_dram[l][0:blocks * P, :],
                                        in_offset=bass.IndirectOffsetOnAxis(ap=slot_i[:, col:col + 1], axis=0)
                                        ).then_inc(sem(f"y_gathered{l}_{j % 4}"), 16)

        def moe(l):
            pool.dma_start(gain_b[:], norm_ffn[l:l + 1, :].to_broadcast([P, D])).then_inc(sem(f"gain_loaded{l}"), 16)
            if l == 0:
                pool.wait_ge(*have("x_heads_in_psum0", XH))
                pool.dma_start(mem_tok[:], mem[0].rearrange("(i p) d -> p i d", p=P)
                               ).then_inc(sem("mem_loaded1"), 16)
            pool.wait_ge(*have(f"h_ffn{l}", 1))
            nc.gpsimd.memset(xs[:], 0.0).then_inc(sem(f"xs_cleared{l}"), 1)
            pool.wait_ge(*have(f"gain_loaded{l}", 16))
            for i in range(TT):
                pool.wait_ge(*have(f"xn_ffn{l}", i + 1))
                if i >= 2:
                    pool.wait_ge(*have(f"xn_stored{l}_{i % 2}", 16))
                nc.gpsimd.tensor_tensor(xg[:, i % 2, :], xn_tile(i), gain_b[:], ALU.mult
                                        ).then_inc(sem(f"xn_gained{l}"), 1)
                pool.wait_ge(*have(f"xn_gained{l}", i + 1))
                pool.dma_start(xn_dram[l][i * P:(i + 1) * P, :], xg[:, i % 2, :]
                               ).then_inc(sem(f"xn_stored{l}_{i % 2}"), 16)
            pool.wait_ge(*have(f"xs_cleared{l}", 1))
            for s in range(2):
                pool.wait_ge(*have(f"xn_stored{l}_{s}", 16 * (TT // 2)))
            pool.wait_ge(*have(f"table_ready{l}", 1))

            def gather(b):
                pool.indirect_dma_start(out=xs[:, b % 2, :], out_offset=None, in_=xn_dram[l],
                                        in_offset=bass.IndirectOffsetOnAxis(ap=tok_i[:, b:b + 1], axis=0),
                                        bounds_check=last_row, oob_is_err=False
                                        ).then_inc(sem(f"gathered{l}_{b % 2}"), 16)

            gather(0)
            gather(1)
            for b in range(NE):
                if b + 2 < NE:
                    pool.wait_ge(*have(f"xs_t_in_psum{l}", b + 1))
                    gather(b + 2)
                n = stream.index((l, b, 2))
                half = slice(GC * BANK // 2, GC * BANK)
                pool.wait_ge(*have("w_hi_ready", n + 1))
                nc.gpsimd.tensor_tensor(lo_at(ring_pos[n])[:, half], raw_at(ring_pos[n])[:, half],
                                        w_hi[:, n % SPLIT, half].bitcast(fp32), ALU.subtract
                                        ).then_inc(sem(f"down_lo_pool{l}"), 1)
            if l == NL - 1:
                pool.dma_start(fg_b[:], final_norm_g.rearrange("(o d) -> o d", o=1).to_broadcast([P, D])
                               ).then_inc(sem("final_gain_loaded"), 16)
            for s in range(2):
                pool.wait_ge(*have(f"y_stored{l}_{s}", 16 * (NE // 2)))
            pool.wait_ge(*have(f"overflow_known{l}", 1))
            n_over = pool.value_load(nov_i[0:1, 0:1])
            with pool.If(n_over > 0):
                with pool.Fori(0, OVERFLOW) as j:
                    pool.wait_ge(*have(f"over_index{l}", j + 1))
                    e = pool.value_load(own_i[0:1, bass.ds(j, 1)], min_val=0, max_val=NE - 1)
                    for part in range(3):
                        load_expert(pool, l, e, part, over_w[part][:], sem(f"over_w{l}"))
                    pool.indirect_dma_start(out=xs[:, 0, :], out_offset=None, in_=xn_dram[l],
                                            in_offset=bass.IndirectOffsetOnAxis(ap=idx_c[:, 0:1], axis=0),
                                            bounds_check=last_row, oob_is_err=False
                                            ).then_inc(sem(f"over_x{l}"), 16)
                    pool.wait_ge(*have(f"over_y{l}", 2 * j + 2))
                    pool.dma_start(ys_dram[l][bass.ds(j * P + NE * P, P), :], y_sb[:, 0, :]
                                   ).then_inc(sem(f"over_stored{l}"), 16)
                    pool.wait_ge(*have(f"over_stored{l}", 16 * j + 16))
            with pool.If(n_over > 0):
                gather_results(l, NE + OVERFLOW)
            with pool.If(n_over < 1):
                gather_results(l, NE)

        moe(0)
        pool.dma_start(ws_in[:], c_ws[0].rearrange("g t s -> t g s")).then_inc(sem("ws_loaded"), 16)
        pool.wait_ge(*have("ws_loaded", 16))
        nc.gpsimd.affine_select(out=ws_in[:], in_=ws_in[:], pattern=[[0, GM], [-1, P]], compare_op=ALU.is_ge,
                                fill=0.0, base=0, channel_multiplier=1).then_inc(sem("ws_masked"), 1)
        pool.dma_start(vg_b[:], c_vnorm_g[0:1, :].to_broadcast([P, D])).then_inc(sem("vnorm_loaded"), 16)
        pool.dma_start(vb_b[:], c_vnorm_b[0:1, :].to_broadcast([P, D])).then_inc(sem("vnorm_loaded"), 16)
        pool.wait_ge(*have("w_used", first["vx1_more"] + 2))
        pool.dma_start(bs_b[:], c_bs[0:1].to_broadcast([P, GM, P])).then_inc(sem("bs_loaded"), 16)
        for g in range(KD):
            pool.wait_ge(*have("gated_hi", g + 1))
            nc.gpsimd.tensor_tensor(a_lo[:, g, :], u_c[:, g, :], a_hi[:, g, :].bitcast(fp32), ALU.subtract
                                    ).then_inc(sem("gated_lo"), 1)
        moe(1)
        pool.wait_ge(*have("final_gain_loaded", 16))
        pool.wait_ge(*have("fin_scaled", 1))
        nc.gpsimd.tensor_tensor(xn_tile(0), xn_tile(0), fg_b[:], ALU.mult).then_inc(sem("first_out_ready"), 1)

    @block.tensor
    def _(pe):
        mm = nc.tensor.matmul

        def granule(d, j, banks, feature_major, n_m, hi, lo, part=slice(0, BANK), ready=None, tile_done=None):
            pe.wait_ge(*have("w_lo_ready", d + 1))
            w_parts = [w.rearrange("p (k n) -> p k n", k=GC) for w in (w_hi[:, d % SPLIT, :], lo_at(ring_pos[d]))]
            steps = [(kk, m) for kk in range(GC) for m in range(n_m)]
            if tile_done is not None:
                steps.sort(key=lambda step: step[1])
            for kk, m in steps:
                k = GC * j + kk
                if ready is not None and m == 0:
                    pe.wait_ge(*have(ready, k + 1))
                o = ps[:, banks + m, part]
                cut = slice(m * P, (m + 1) * P)
                for c, (wt, act) in enumerate(((w_parts[0], hi), (w_parts[0], lo), (w_parts[1], hi))):
                    if feature_major:
                        lhs, rhs = wt[:, kk, cut], act[:, k, :]
                    else:
                        lhs, rhs = act[:, k, cut], wt[:, kk, :]
                    last = mm(o, lhs, rhs, start=(k == 0 and c == 0), stop=(k == KD - 1 and c == 2))
                if tile_done is not None and kk == GC - 1 and m < n_m - 1:
                    last.then_inc(sem(tile_done), 1)
            last.then_inc(sem("w_used"), 1)

        def transposes(tag):
            n = norm_parts(tag)[0]
            per = BANK // (n * P)
            b0 = 4 if n == MT else 0
            for i in range(n):
                pe.wait_ge(*have(f"xn_{tag}", i + 1))
                for k in range(KD):
                    src = mem_tok[:, i, k * P:(k + 1) * P] if n == MT else xn_tile(i)[:, k * P:(k + 1) * P]
                    c0 = (k % per) * n * P + i * P
                    last = nc.tensor.transpose(ps[:, b0 + k // per, c0:c0 + P], src, ident[:])
                name = f"mem_t_in_psum{tag[-1]}" if n == MT else f"xn_t_in_psum_{tag}"
                last.then_inc(sem(name), 1)

        def late_transposes(tag):
            for half in range(2):
                for i in range(TT):
                    source_ready(pe, tag, i)
                    for k in range(half * CC, (half + 1) * CC):
                        last = nc.tensor.transpose(ps[:, k, i * P:(i + 1) * P], h[:, i, k * P:(k + 1) * P], ident[:])
                last.then_inc(sem(f"xn_t_in_psum_{tag}"), 1)

        def token_factors(tag):
            pe.wait_ge(*have(f"diag_ready_{tag}", 1))
            pe.wait_ge(*have(f"split_lo_{tag}", KD))
            mm(ps[:, 7, :], ones[:], diag[:].rearrange("p i t -> p (i t)"), start=True, stop=True
               ).then_inc(sem(f"factors_in_psum_{tag}"), 1)

        pe.wait_ge(*have("consts", 9))
        pe.wait_ge(*have("vecs_loaded", 16 * 8))
        nc.tensor.transpose(ps[:, 0, 0:NV], vec_in[0:NV, :], ident[0:NV, 0:NV]).then_inc(sem("vecs_in_psum"), 1)
        for m in range(CC):
            last = nc.tensor.transpose(ps[:, 1, m * TAPS:(m + 1) * TAPS], tap_in[0:TAPS, m * P:(m + 1) * P],
                                       ident[0:TAPS, 0:TAPS])
        last.then_inc(sem("vecs_in_psum"), 1)
        pe.wait_ge(*have("vecs_ready", 2))

        transposes("mix0")
        pe.wait_ge(*have("split_lo_mix0", 4))
        granule(first["sb_gate"], 0, 0, True, CC, a_hi, a_lo, ready="split_lo_mix0")
        granule(first["sb_gate"] + 1, 1, 0, True, CC, a_hi, a_lo, ready="split_lo_mix0")
        for j in range(2):
            granule(first["sb_a"] + j, j, 4, True, CC, a_hi, a_lo)
        pe.wait_ge(*have("gate_done", 1))
        for j in range(2):
            granule(first["sb_q"] + j, j, 0, True, CC, a_hi, a_lo)
        pe.wait_ge(*have("glu_done", 1))
        for j in range(2):
            granule(first["sb_k"] + j, j, 4, True, CC, a_hi, a_lo)
        pe.wait_ge(*have("q_ready", 1))
        granule(first["sb_v"], 0, 0, False, TT, a_hi, a_lo)
        pe.wait_ge(*have("k_ready", 1))
        transposes("mem0")
        granule(first["sb_v"] + 1, 1, 0, False, TT, a_hi, a_lo)

        def mem_keys(l, s, bank):
            for j in range(2):
                granule(first[f"kx{l}"] + 2 * s + j, j, bank, True, 4, mem_hi, mem_lo, part=slice(0, M),
                        ready=f"mem_split_lo{l}" if s == 0 else None)

        def mem_values(l, s, bank):
            for j in range(2):
                granule(values_at(l, s) + j, j, bank, False, MT, mem_hi, mem_lo)

        pe.wait_ge(*have("v_ready", 1))
        mem_keys(0, 0, 0)
        pe.wait_ge(*have("mem_split_lo0", KD))
        mem_keys(0, 1, 4)
        pe.wait_ge(*have("kx_ready0", 1))
        mem_values(0, 0, 0)
        mem_values(0, 1, 2)
        pe.wait_ge(*have("kx_ready0", 2))

        def head(hd):
            return slice((hd % 2) * SB_DH, (hd % 2 + 1) * SB_DH), hd // 2

        def scores(hd):
            rows, c = head(hd)
            if hd:
                pe.wait_ge(*have("z_diag", hd))
                pe.wait_ge(*have("z_off", hd))
            for j in range(TT):
                cut = slice(j * P, (j + 1) * P)
                last = mm(ps[:, 4, cut], k_t[rows, c, cut], q_t[rows, c, cut], start=True, stop=True)
                if j < TT - 1:
                    o = OFF[j]
                    bank, o = 4 + o // BANK, o % BANK
                    last = mm(ps[:, bank, o:o + T - (j + 1) * P], k_t[rows, c, cut], q_t[rows, c, (j + 1) * P:],
                              start=True, stop=True)
            last.then_inc(sem("z_in_psum"), 1)

        def sums(hd):
            pe.wait_ge(*have("softplus", hd + 1))
            if hd:
                pe.wait_ge(*have("log_w", hd))
            else:
                pe.wait_ge(*have("vx_ready0", 2))
            s = sbuf[:, hd % 2, :]
            mm(ps[:, 0, :], tri[:], s[:, 0:512], start=True, stop=True)
            mm(ps[:, 1, :], tri[:], s[:, 512:1024], start=True, stop=False, skip_group_check=True)
            mm(ps[:, 2, 0:256], tri[:], s[:, 1024:1280], start=True, stop=False, skip_group_check=True)
            mm(ps[:, 1, 0:384], ones[:], s[:, 128:512], start=False, stop=False, skip_group_check=True)
            mm(ps[:, 1, 128:384], ones[:], s[:, 1024:1280], start=False, stop=False, skip_group_check=True)
            mm(ps[:, 1, 256:384], ones[:], s[:, 896:1024], start=False, stop=False, skip_group_check=True)
            mm(ps[:, 1, 384:512], ones[:], s[:, 384:512], start=False, stop=True, skip_group_check=True)
            mm(ps[:, 2, 0:256], ones[:], s[:, 256:512], start=False, stop=False, skip_group_check=True)
            mm(ps[:, 2, 128:256], ones[:], s[:, 896:1024], start=False, stop=True, skip_group_check=True
               ).then_inc(sem("sums_in_psum"), 1)

        def values(hd):
            rows, c = head(hd)
            pe.wait_ge(*have("weights", hd + 1))
            if hd >= 2 and hd % 2 == 0:
                pe.wait_ge(*have("heads_lo", hd // 2))
            w = zbuf[:, hd % 2, :]
            o = ps[rows, 3, :]
            vcol = slice(hd * SB_DH, (hd + 1) * SB_DH)
            for j in range(TT):
                v = v_s[:, j, vcol]
                last = mm(o[:, j * P:(j + 1) * P], v, w[:, j * P:(j + 1) * P], start=(j == 0), stop=(j == TT - 1),
                          skip_group_check=True)
                if j < TT - 1:
                    n = T - (j + 1) * P
                    last = mm(o[:, (j + 1) * P:], v, w[:, OFF[j]:OFF[j] + n], start=False, stop=False,
                              skip_group_check=True)
            last.then_inc(sem("heads_in_psum"), 1)

        scores(0)
        for hd in range(SB_HEADS):
            if hd + 1 < SB_HEADS:
                scores(hd + 1)
            if hd:
                values(hd - 1)
            sums(hd)
            if hd == 3:
                pe.wait_ge(*have("conv_taps", CC * TAPS))
                for m in range(CC):
                    last = mm(ps[:, 7, :], ones[:], conv_acc[:, m, :], start=(m == 0), stop=(m == CC - 1))
                last.then_inc(sem("conv_mean"), 1)
            if hd == 5:
                pe.wait_ge(*have("conv_squared", 1))
                for m in range(CC):
                    last = mm(ps[:, 7, :], ones[:], conv_sq[:, m, :], start=(m == 0), stop=(m == CC - 1))
                last.then_inc(sem("conv_var"), 1)
        values(SB_HEADS - 1)

        def project_out(l):
            if l == 0:
                pe.wait_ge(*have("heads_lo", SB_HEADS // 2))
                pe.wait_ge(*have("log_w", SB_HEADS))
            for s in range(2):
                if l:
                    pe.wait_ge(*have("gated", GM // 2 * (s + 1)))
                for j in range(2):
                    granule(first[f"mix_out{l}"] + 2 * s + j, j, 4 * s, False, TT, a_hi, a_lo,
                            ready=None if s else "gated_lo" if l else "conv_lo" if j == 0 else None,
                            tile_done=f"tile_xa{l}" if s == j == 1 else None)

        def cross(l):
            pe.wait_ge(*have(f"h_part_xa{l}", TT))
            late_transposes(f"xa{l}")
            for s in range(2):
                pe.wait_ge(*have(f"split_lo_xa{l}", 4 * (s + 1)))
                if s:
                    pe.wait_ge(*have(f"factors_ready_xa{l}", 1))
                for j in range(2):
                    granule(first[f"xq{l}"] + 2 * s + j, j, 4 * s, True, 4, a_hi, a_lo,
                            ready=f"split_lo_xa{l}" if s == 0 else None)
                    if s == j == 0:
                        token_factors(f"xa{l}")

            def xscores(hd):
                if hd < 2:
                    pe.wait_ge(*have(f"xq_ready{l}", hd + 1))
                else:
                    pe.wait_ge(*have(f"x_exp{l}", TT * (hd - 1)))
                for i in range(TT):
                    b = 2 * (hd % 2) + i // 2
                    for c in range(2):
                        last = mm(ps[:, b, (i % 2) * M:(i % 2 + 1) * M], xq[:, 2 * hd + c, i * P:(i + 1) * P],
                                  kx[:, 2 * hd + c, :], start=(c == 0), stop=(c == 1))
                last.then_inc(sem(f"x_scores{l}"), 1)

            def xtransposes(hd):
                pe.wait_ge(*have(f"x_probs{l}", hd + 1))
                if hd:
                    pe.wait_ge(*have(f"x_probs_t{l}", hd))
                for i in range(TT):
                    for c in range(MT):
                        last = nc.tensor.transpose(ps[:, 4 + c, i * P:(i + 1) * P], xp[:, hd % 2, i, c * P:(c + 1) * P],
                                                   ident[:])
                last.then_inc(sem(f"x_probs_t_in_psum{l}"), 1)

            def xvalues(hd):
                pe.wait_ge(*have(f"x_probs_t{l}", hd + 1))
                if hd:
                    pe.wait_ge(*have(f"x_heads_lo{l}", 2 * hd))
                for c2 in range(2):
                    f0 = hd * XD + c2 * P
                    for c in range(MT):
                        last = mm(ps[:, 6 + c2, :], vx[:, c, f0:f0 + P], xpt[:, hd % 2, c, :], start=(c == 0),
                                  stop=(c == MT - 1))
                last.then_inc(sem(f"x_heads_in_psum{l}"), 1)

            xscores(0)
            pe.wait_ge(*have(f"xq_ready{l}", 2))
            xscores(1)
            for hd in range(XH):
                xtransposes(hd)
                if hd + 2 < XH:
                    xscores(hd + 2)
                xvalues(hd)
            for s in range(2):
                if s == 0:
                    pe.wait_ge(*have(f"x_exp{l}", TT * XH))
                for j in range(2):
                    if l == 0 and s == 1 and j == 0:
                        pe.wait_ge(*have("mem_split_lo1", KD))
                    granule(first[f"xo{l}"] + 2 * s + j, j, 4 * s, False, TT, a_hi, a_lo,
                            ready=f"x_heads_lo{l}" if s == 0 else None,
                            tile_done=f"tile_ffn{l}" if s == j == 1 else None)
                    if l == 0 and s == 0 and j == 0:
                        pe.wait_ge(*have(f"x_heads_lo{l}", KD))
                        transposes("mem1")

        def experts(l):
            W = NG + NE
            small_bank = 4 if l == 0 else 0
            pe.wait_ge(*have(f"h_part_ffn{l}", TT))
            if l == 0:
                mem_keys(1, 0, 0)
                pe.wait_ge(*have(f"h_ffn{l}", TT))

            def tile_transposes(i):
                b0 = (small_bank + 2 * i) % 8
                if l == 0 and i == 2:
                    pe.wait_ge(*have("kx_ready1", 1))
                pe.wait_ge(*have(f"h_ffn{l}", TT if l and i == 3 else i + 1))
                for k in range(KD):
                    last = nc.tensor.transpose(ps[:, b0 + k // 4, (k % 4) * P:(k % 4 + 1) * P],
                                               h[:, i, k * P:(k + 1) * P], ident[:])
                last.then_inc(sem(f"xn_t_in_psum_ffn{l}"), 1)

            def logits(i):
                pe.wait_ge(*have(f"a_odd{l}" if i % 2 else f"a_even{l}", i // 2 + 1))
                for k in range(KD):
                    last = mm(ps[0:W, small_bank, i * P:(i + 1) * P], rt_w[:, l, k, :], a_full[:, k, i * P:(i + 1) * P],
                              start=(k == 0), stop=(k == KD - 1))
                last.then_inc(sem(f"logits{l}"), 1)

            tile_transposes(0)
            pe.wait_ge(*have("router_scaled", NL))
            for i in range(1, TT):
                tile_transposes(i)
                logits(i - 1)
            logits(TT - 1)
            pe.wait_ge(*have(f"logits_out{l}", 1))
            for i in range(TT):
                last = nc.tensor.transpose(ps[:, small_bank + 1, i * W:(i + 1) * W], logits_w[0:W, i * P:(i + 1) * P],
                                           ident[0:W, 0:W])
            last.then_inc(sem(f"logits_t{l}"), 1)
            if l == 0:
                mem_keys(1, 1, 0)
            pe.wait_ge(*have(f"assigned{l}", 1))
            mm(ps[:, small_bank, 0:TT * NE], before[:], e_sum[:].rearrange("p i e -> p (i e)"), start=True, stop=False,
               skip_group_check=True)
            for j in range(TT - 1):
                mm(ps[:, small_bank, (j + 1) * NE:TT * NE].rearrange("p (i e) -> p i e", e=NE), ones_r[:],
                   e_sum[:, j:j + 1, :].to_broadcast([P, TT - 1 - j, NE]), start=False, stop=(j == TT - 2),
                   skip_group_check=True)
            for j in range(TT):
                last = mm(ps[:, small_bank, TT * NE:(TT + 1) * NE], ones_r[:], e_sum[:, j, :], start=(j == 0),
                          stop=(j == TT - 1))
            last.then_inc(sem(f"ranks{l}"), 1)
            if l == 0:
                pe.wait_ge(*have("kx_ready1", 2))
                mem_values(1, 0, 0)
            pe.wait_ge(*have(f"hots{l}", 2))
            for j in range(2 * TT):
                last = mm(ps[:, small_bank + 1, 0:NB], slot_hot[:, j, :], tok_hot[:, j, :], start=(j == 0),
                          stop=(j == 2 * TT - 1))
            last.then_inc(sem(f"table{l}"), 1)

            def xs_transposes(s):
                for k in range(KD):
                    last = nc.tensor.transpose(ps[:, k // 4, (k % 4) * P:(k % 4 + 1) * P],
                                               xs[:, s, k * P:(k + 1) * P], ident[:])
                last.then_inc(sem(f"xs_t_in_psum{l}"), 1)

            def gate_up(e, part, granule_at):
                n, slot, _, hs = granule_at
                pe.wait_ge(*have("w_lo_ready", n + 1))
                w = w_hi[:, hs, :], lo_at(slot)
                for kk in range(GC):
                    k = GC * part + kk
                    for c, (x_part, w_part) in enumerate(((xs_hi, w[0]), (xs_lo, w[0]), (xs_hi, w[1]))):
                        last = mm(ps[:, 2 + e, :], x_part[:, e, k, :], w_part[:, kk * BANK:(kk + 1) * BANK],
                                  start=(k == 0 and c == 0), stop=(k == KD - 1 and c == 2))
                last.then_inc(sem("w_used"), 1)

            def hidden_transposes(e, b):
                pe.wait_ge(*have(f"hidden{l}", b + 1))
                for c in range(2):
                    last = nc.tensor.transpose(ps[:, 4, c * P:(c + 1) * P], hid[:, e, c * P:(c + 1) * P], ident[:])
                last.then_inc(sem(f"hidden_t_in_psum{l}"), 1)

            def down(e, b, granule_at, first_block):
                n, slot, _, hs = granule_at
                pe.wait_ge(*have("w_lo_ready", n + 1))
                pe.wait_ge(*have(f"down_lo_pool{l}", b + 1))
                pe.wait_ge(*have(f"hidden_lo{l}", b + 1))
                if not first_block:
                    pe.wait_ge(*have(f"y_left{l}", b))
                    pe.wait_ge(*have(f"y_right{l}", b))
                w = w_hi[:, hs, :], lo_at(slot)
                for half in range(2):
                    for c in range(2):
                        cut = slice(c * D + half * BANK, c * D + (half + 1) * BANK)
                        for m, (h_part, w_part) in enumerate(((hid_hi, w[0]), (hid_lo, w[0]), (hid_hi, w[1]))):
                            last = mm(ps[:, 5 + half, :], h_part[:, e, c, :], w_part[:, cut],
                                      start=(c == 0 and m == 0), stop=(c == 1 and m == 2))
                last.then_inc(sem("w_used"), 1)

            if l == 0:
                pe.wait_ge(*have("vx_ready1", 1))
            pe.wait_ge(*have(f"table_ready{l}", 1))
            pe.wait_ge(*have(f"gathered{l}_0", 16))
            xs_transposes(0)

            def block_of(i, e, first_pair, last_pair):
                b = 2 * i + e
                pe.wait_ge(*have(f"xs_lo{l}", b + 1))
                if not first_pair:
                    pe.wait_ge(*have(f"hidden{l}", b - 1))
                gate_up(e, 0, entry(l, 0 if first_pair and e == 0 else 3 * e - 1, i))
                if not (last_pair and e == 1):
                    pe.wait_ge(*have(f"gathered{l}_{1 - e}", 16 * i + (16 if e == 0 else 32)))
                    xs_transposes(1 - e)
                if not (first_pair and e == 0):
                    hidden_transposes(1 - e, b - 1)
                gate_up(e, 1, entry(l, 1 if first_pair and e == 0 else 3 * e, i))
                if not (first_pair and e == 0):
                    down(1 - e, b - 1, entry(l, 3 * e + 1, i), first_pair)

            for e in range(2):
                block_of(0, e, True, False)
            with pe.Fori(1, NE // 2 - 1) as i:
                for e in range(2):
                    block_of(i, e, False, False)
            for e in range(2):
                block_of(NE // 2 - 1, e, False, True)
            hidden_transposes(1, NE - 1)
            down(1, NE - 1, entry(l, 3 * NE - 1, 0), False)

            if l == 0:
                mem_values(1, 1, 2)
                pe.wait_ge(*have("vx_ready1", 2))
            pe.wait_ge(*have(f"y_left{l}", NE))
            pe.wait_ge(*have(f"y_right{l}", NE))
            pe.wait_ge(*have(f"overflow_known{l}", 1))
            n_over = pe.value_load(nov_i[0:1, 0:1])
            with pe.If(n_over > 0):
                with pe.Fori(0, OVERFLOW) as j:
                    pe.wait_ge(*have(f"over_x{l}", 16 * j + 16))
                    for k in range(KD):
                        last = nc.tensor.transpose(ps[:, k // 4, (k % 4) * P:(k % 4 + 1) * P],
                                                   xs[:, 0, k * P:(k + 1) * P], ident[:])
                    last.then_inc(sem(f"over_products{l}"), 1)
                    pe.wait_ge(*have(f"over_w{l}", 80 * j + 80))
                    pe.wait_ge(*have(f"over_x_t{l}", j + 1))
                    for k in range(KD):
                        last = mm(ps[:, 2, :], xs_full[:, k, :], over_w[k // GC][:, (k % GC) * BANK:(k % GC + 1) * BANK],
                                  start=(k == 0), stop=(k == KD - 1))
                    last.then_inc(sem(f"over_products{l}"), 1)
                    pe.wait_ge(*have(f"over_hidden{l}", j + 1))
                    for c in range(2):
                        last = nc.tensor.transpose(ps[:, 4, c * P:(c + 1) * P], hid[:, 0, c * P:(c + 1) * P], ident[:])
                    last.then_inc(sem(f"over_products{l}"), 1)
                    pe.wait_ge(*have(f"over_hidden_t{l}", j + 1))
                    for half in range(2):
                        for c in range(2):
                            last = mm(ps[:, 5 + half, :], hid_full[:, c, :],
                                      over_w[2][:, c * D + half * BANK:c * D + (half + 1) * BANK],
                                      start=(c == 0), stop=(c == 1))
                    last.then_inc(sem(f"over_products{l}"), 1)
                    pe.wait_ge(*have(f"over_y{l}", 2 * j + 2))

        project_out(0)
        cross(0)
        experts(0)

        pe.wait_ge(*have("vx_ready1", 2))
        late_transposes("mix1")
        pe.wait_ge(*have("split_lo_mix1", 4))
        granule(first["c_v"], 0, 0, False, TT, a_hi, a_lo, ready="split_lo_mix1")
        token_factors("mix1")
        pe.wait_ge(*have("ws_masked", 1))
        for g in range(GM):
            last = nc.tensor.transpose(ps[:, 4 + g // 4, (g % 4) * P:(g % 4 + 1) * P], ws_in[:, g, :], ident[:])
        last.then_inc(sem("ws_t_in_psum"), 1)
        granule(first["c_v"] + 1, 1, 0, False, TT, a_hi, a_lo)
        pe.wait_ge(*have("ws_t_ready", 1))
        pe.wait_ge(*have("factors_ready_mix1", 1))
        for j in range(2):
            granule(first["c_v"] + 2 + j, j, 4, False, TT, a_hi, a_lo)
        for s in range(2):
            pe.wait_ge(*have("v_gelu", TT * (s + 1)))
            for j in range(2):
                granule(first["c_u"] + 2 * s + j, j, 4 * s, True, 4, a_hi, a_lo)
        pe.wait_ge(*have("v_normed", TT))
        for g in range(GM):
            if g in (0, 4):
                pe.wait_ge(*have("u_scaled", g // 4 + 1))
            for c in range(TT):
                last = mm(ps[:, g, c * P:(c + 1) * P], v_c[:, c, g * P:(g + 1) * P], ws_t[:, g, :], start=True, stop=True)
            last.then_inc(sem("mixed_in_psum"), 1)
        project_out(1)
        cross(1)
        experts(1)

    @block.scalar
    def _(act):
        A = nc.scalar.activation

        for t, n, src in ((0, KD, mem_norm_g.rearrange("(k p) -> k p", p=P)),
                          (MIX_G, NL * KD, norm_mix.rearrange("l (k p) -> (l k) p", p=P)),
                          (XA_G, NL * KD, norm_xa.rearrange("l (k p) -> (l k) p", p=P)),
                          (FFN_G, NL * KD, norm_ffn.rearrange("l (k p) -> (l k) p", p=P)),
                          (CONV_B, CC, ab_conv_b.rearrange("l (k p) -> (l k) p", p=P)),
                          (CN_G, CC, ab_cnorm_g.rearrange("l (k p) -> (l k) p", p=P)),
                          (CN_B, CC, ab_cnorm_b.rearrange("l (k p) -> (l k) p", p=P)),):
            act.dma_start(vec_in[t:t + n, :], src).then_inc(sem("vecs_loaded"), 16)
        act.dma_start(tap_in[0:TAPS, :], ab_conv_w[0]).then_inc(sem("vecs_loaded"), 16)
        act.dma_start(mem_tok[:], mem[0].rearrange("(i p) d -> p i d", p=P)).then_inc(sem("mem_loaded0"), 16)

        n_prep = [0]

        def hi_part(n, slot, arrivals, hs):
            act.wait_ge(arrivals_of(slot), arrivals)
            if not isinstance(n, int) or n >= SPLIT:
                act.wait_ge(*have("w_used", n - (SPLIT - 1)))
            A(w_hi[:, hs, :], raw_at(slot), ACT.Copy).then_inc(sem("w_hi_ready"), 1)

        def prep(upto):
            while n_prep[0] < upto:
                d = n_prep[0]
                n_prep[0] += 1
                hi_part(d, ring_pos[d], ring_count[d], d % SPLIT)

        def squares(tag):
            n, src, *_ = norm_parts(tag)
            for i in range(n if tag[:3] == "ffn" else n // 2):
                source_ready(act, tag, i)
                if i:
                    act.wait_ge(*have(f"squares_act_{tag}", i))
                A(xn[:, 0, :], src(i), ACT.Square, accum_out=n_ss[:, i:i + 1]).then_inc(sem(f"squares_act_{tag}"), 1)
            if tag not in LATE and tag[:3] != "ffn":
                roots(tag)

        def roots(tag):
            n = norm_parts(tag)[0]
            act.wait_ge(*have(f"norm_var_{tag}", 1))
            A(n_y[:, 0:n], n_var[:, 0:n], ACT.Sqrt).then_inc(sem(f"norm_root_{tag}"), 1)

        def split(tag, done):
            n, _, _, g0, hi, lo = norm_parts(tag)
            per = BANK // (n * P)
            b0 = 4 if n == MT else 0
            name = f"mem_t_in_psum{tag[-1]}" if n == MT else f"xn_t_in_psum_{tag}"
            if tag not in LATE:
                act.wait_ge(*have(name, n))
            for k in range(KD):
                if tag in LATE and k % CC == 0:
                    act.wait_ge(*have(name, k // CC + 1))
                c0 = (k % per) * n * P
                A(hi[:, k, :], ps[:, b0 + k // per, c0:c0 + n * P], ACT.Copy, scale=vecs[:, g0 + k:g0 + k + 1]
                  ).then_inc(sem(done), 1)

        def used(d):
            act.wait_ge(*have("w_used", d + 1))

        def copy_out(name, dst, src, scale=1.0):
            A(dst, src, ACT.Copy, scale=scale).then_inc(sem(name), 1)

        squares("mix0")
        act.wait_ge(*have("vecs_ready", 2))
        prep(2)
        split("mix0", "split_hi_mix0")
        prep(3)
        squares("mem0")
        used(1)
        A(conv_acc[:].rearrange("p k n -> p (k n)"), ps[:, 0:4, :].rearrange("p k n -> p (k n)"), ACT.Sigmoid
          ).then_inc(sem("gate_done"), 1)
        prep(7)
        used(first["sb_q"] + 1)
        copy_out("q_ready", q_t[:], ps[:, 0:4, :], SB_DH ** -0.5)
        prep(9)
        used(first["sb_k"] + 1)
        copy_out("k_ready", k_t[:], ps[:, 4:8, :])
        prep(10)
        split("mem0", "mem_split_hi0")
        prep(11)
        used(first["sb_v"] + 1)
        copy_out("v_ready", v_s[:], ps[:, 0:4, :])
        prep(13)

        def mem_keys_out(l, s, bank):
            used(first[f"kx{l}"] + 2 * s + 1)
            copy_out(f"kx_ready{l}", kx[:, 4 * s:4 * s + 4, :], ps[:, bank:bank + 4, 0:M])

        def mem_values_out(l, s, bank):
            used(values_at(l, s) + 1)
            copy_out(f"vx_ready{l}", vx[:, :, s * BANK:(s + 1) * BANK], ps[:, bank:bank + MT, :])

        prep(14)
        mem_keys_out(0, 0, 0)
        prep(15)
        prep(16)
        mem_keys_out(0, 1, 4)
        prep(18)
        mem_values_out(0, 0, 0)
        prep(19)
        nc.scalar.preload_act_table_set("natural_log_exp_and_others")
        mem_values_out(0, 1, 2)
        prep(21)

        def z_part(hd):
            s = hd % 2
            act.wait_ge(*have("z_in_psum", hd + 1))
            if hd >= 2:
                act.wait_ge(*have("heads_in_psum", hd - 1))
            else:
                act.wait_ge(*have("w_used", first["vx0"] + 4))
            A(zbuf[:, s, 512:1280], ps[:, 5:7, :].rearrange("p k n -> p (k n)")[:, 0:768], ACT.Copy
              ).then_inc(sem("z_off"), 1)
            if hd in (3, 5, 7):
                heads_hi((hd - 3) // 2)
            if hd == 7:
                act.wait_ge(*have("conv_var_ready", 1))
                A(conv_rs[:, 1, :], conv_rs[:, 0, :], ACT.Ln).then_inc(sem("conv_root"), 1)
                act.wait_ge(*have("conv_root", 1))
                A(conv_rs[:, 1, :], conv_rs[:, 1, :], ACT.Exp, scale=-0.5).then_inc(sem("conv_root"), 1)
            act.wait_ge(*have("minus_abs_z", hd + 1))
            A(sbuf[:, s, :], sbuf[:, s, :], ACT.Exp).then_inc(sem("exp_abs"), 1)
            act.wait_ge(*have("exp_abs", hd + 1))
            A(sbuf[:, s, :], sbuf[:, s, :], ACT.Ln, bias=1.0).then_inc(sem("ln_done"), 1)

        def w_part(hd):
            act.wait_ge(*have("log_w", hd + 1))
            A(zbuf[:, hd % 2, :], zbuf[:, hd % 2, :], ACT.Exp).then_inc(sem("weights"), 1)

        def heads_hi(pair):
            act.wait_ge(*have("heads_in_psum", 2 * pair + 2))
            copy_out("heads_hi", a_hi[:, CC + pair, :], ps[:, 3, :])

        z_part(0)
        for hd in range(SB_HEADS):
            if hd + 1 < SB_HEADS:
                z_part(hd + 1)
            w_part(hd)
            if hd == 4:
                act.wait_ge(*have("conv_centred", 1))
                A(conv_sq[:].rearrange("p k n -> p (k n)"), conv_acc[:].rearrange("p k n -> p (k n)"), ACT.Square
                  ).then_inc(sem("conv_squared"), 1)
        nc.scalar.preload_act_table(ACT.Silu)
        heads_hi(3)
        act.wait_ge(*have("conv_normed", 1))
        for m in range(CC):
            A(conv_sq[:, m, :], conv_acc[:, m, :], ACT.Silu, bias=vecs[:, CN_B + m:CN_B + m + 1],
              scale=vecs[:, CN_G + m:CN_G + m + 1]).then_inc(sem("conv_silu"), 1)
            act.wait_ge(*have("conv_silu", m + 1))
            copy_out("conv_hi", a_hi[:, m, :], conv_sq[:, m, :])
        prep(first["xq0"] + 2)

        def factors_out(tag, scale):
            act.wait_ge(*have(f"factors_in_psum_{tag}", 1))
            copy_out(f"factors_ready_{tag}", factors[:], ps[:, 7, :], scale)

        def cross(l):
            d = first[f"xq{l}"]
            squares(f"xa{l}")
            split(f"xa{l}", f"split_hi_xa{l}")
            prep(d + 3)
            roots(f"xa{l}")
            factors_out(f"xa{l}", XD ** -0.5)
            prep(d + 6)

            def x_exp(hd):
                act.wait_ge(*have(f"x_max{l}", hd + 1))
                if hd >= 2:
                    act.wait_ge(*have(f"x_probs_t_in_psum{l}", hd - 1))
                for i in range(TT):
                    b = 2 * (hd % 2) + i // 2
                    A(xp[:, hd % 2, i, :], ps[:, b, (i % 2) * M:(i % 2 + 1) * M], ACT.Exp, bias=x_max[:, i:i + 1],
                      accum_out=x_sum[:, i:i + 1]).then_inc(sem(f"x_exp{l}"), 1)

            x_exp(0)
            for hd in range(XH):
                act.wait_ge(*have(f"x_probs_t_in_psum{l}", hd + 1))
                if hd >= 2:
                    act.wait_ge(*have(f"x_heads_in_psum{l}", hd - 1))
                copy_out(f"x_probs_t{l}", xpt[:, hd % 2], ps[:, 4:6, :])
                if hd + 1 < XH:
                    x_exp(hd + 1)
                act.wait_ge(*have(f"x_heads_in_psum{l}", hd + 1))
                for c in range(2):
                    copy_out(f"x_heads_hi{l}", a_hi[:, 2 * hd + c, :], ps[:, 6 + c, :])
            if l == 0:
                prep(d + 7)
                squares("mem1")
                split("mem1", "mem_split_hi1")
            prep(d + 10)
            if l == 0:
                prep(d + 11)

        def experts(l):
            squares(f"ffn{l}")
            def even_tiles():
                for i in (0, 2):
                    b0 = (4 * (l == 0) + 2 * i) % 8
                    act.wait_ge(*have(f"xn_t_in_psum_ffn{l}", i + 1))
                    A(a_full[:, :, i * P:(i + 1) * P], ps[:, b0:b0 + 2, :].rearrange("p a (b n) -> p (a b) n", n=P),
                      ACT.Copy).then_inc(sem(f"a_even{l}"), 1)
                    if i == 0:
                        roots(f"ffn{l}")

            def logits_out():
                act.wait_ge(*have(f"logits{l}", TT))
                A(logits_w[:], ps[0:NG + NE, 4 * (l == 0), :], ACT.Copy).then_inc(sem(f"logits_out{l}"), 1)

            m = first[f"moe{l}"]
            if l:
                even_tiles()
                logits_out()
            if l == 0:
                k1, v1 = first["kx1"], first["vx1"]
                prep(k1 + 4)
                mem_keys_out(1, 0, 0)
                even_tiles()
                prep(v1 + 1)
                logits_out()
            act.wait_ge(*have(f"r_args{l}", 1))
            A(r4b[:], r4a[:], ACT.Exp).then_inc(sem(f"r_exp{l}"), 1)
            act.wait_ge(*have(f"r_args{l}", 2))
            A(r1b[:], r1a[:], ACT.Exp).then_inc(sem(f"r_exp{l}"), 1)
            if l == 0:
                prep(v1 + 2)
                mem_keys_out(1, 1, 0)
                prep(m + 2)
                mem_values_out(1, 0, 0)
            prep(m + 2)

            def rows_hi(e):
                A(xs_hi[:, e].rearrange("p k n -> p (k n)"), ps[:, 0:2, :].rearrange("p a n -> p (a n)"), ACT.Copy
                  ).then_inc(sem(f"xs_hi{l}"), 1)

            def hidden_hi(e, b):
                act.wait_ge(*have(f"hidden_t_in_psum{l}", b + 1))
                A(hid_hi[:, e].rearrange("p c n -> p (c n)"), ps[:, 4, 0:2 * P], ACT.Copy
                  ).then_inc(sem(f"hidden_hi{l}"), 1)

            def y_left(e, n):
                act.wait_ge(*have("w_used", n + 1))
                A(y_sb[:, e, 0:BANK], ps[:, 5, :], ACT.Copy).then_inc(sem(f"y_left{l}"), 1)

            def store(e, b):
                act.wait_ge(*have(f"y_left{l}", b + 1))
                act.wait_ge(*have(f"y_right{l}", b + 1))
                act.dma_start(ys_dram[l][b * P:(b + 1) * P, :] if isinstance(b, int) else
                              ys_dram[l][bass.ds(b * P, P), :], y_sb[:, e, :]
                              ).then_inc(sem(f"y_stored{l}_{e}"), 16)

            def block_of(i, e, first_pair, last_pair):
                b = 2 * i + e
                last_block = last_pair and e == 1
                if not last_block:
                    act.wait_ge(*have(f"xs_t_in_psum{l}", b + 2))
                    rows_hi(1 - e)
                if not (first_pair and e == 0):
                    hidden_hi(1 - e, b - 1)
                hi_part(*entry(l, 3 * e + 2, i))
                act.wait_ge(*have("w_used", entry(l, 1 if first_pair and e == 0 else 3 * e, i)[0] + 1))
                if not first_pair:
                    act.wait_ge(*have(f"hidden{l}", b - 1))
                A(silu_g[:, e, :], ps[:, 2 + e, 0:FE], ACT.Silu).then_inc(sem(f"silu{l}"), 1)
                if not last_block:
                    hi_part(*entry(l, 3 * e + 3, i))
                if not (first_pair and e == 0):
                    if not first_pair:
                        act.wait_ge(*have(f"y_stored{l}_{e}", 16 * i))
                    y_left(1 - e, entry(l, 3 * e + 1, i)[0])
                if not last_block:
                    hi_part(*entry(l, 3 * e + 4, i))
                if not (first_pair and e == 0):
                    store(1 - e, b - 1)

            nc.scalar.preload_act_table(ACT.Silu)
            act.wait_ge(*have(f"xs_t_in_psum{l}", 1))
            rows_hi(0)
            for e in range(2):
                block_of(0, e, True, False)
            with act.Fori(1, MORE) as i:
                for e in range(2):
                    block_of(i, e, False, False)
            for i in range(MORE, NE // 2):
                for e in range(2):
                    block_of(i, e, False, i == NE // 2 - 1)
            hidden_hi(1, NE - 1)
            n_prep[0] += 3 * NE - 2
            if l == 0:
                prep(first["vx1_more"] + 1)
            y_left(1, first[f"moe{l}"] + 3 * NE - 1)
            store(1, NE - 1)
            if l == 0:
                prep(first["c_v"] + 1)
                mem_values_out(1, 1, 2)

            act.wait_ge(*have(f"y_stored{l}_1", 16 * (NE // 2)))
            act.wait_ge(*have(f"y_stored{l}_0", 16 * (NE // 2)))
            act.wait_ge(*have(f"overflow_known{l}", 1))
            n_over = act.value_load(nov_i[0:1, 0:1])
            with act.If(n_over > 0):
                with act.Fori(0, OVERFLOW) as j:
                    act.wait_ge(*have(f"over_products{l}", 4 * j + 2))
                    A(silu_g[:, 0, :], ps[:, 2, 0:FE], ACT.Silu).then_inc(sem(f"over_silu{l}"), 1)
                    act.wait_ge(*have(f"over_products{l}", 4 * j + 3))
                    A(hid_full[:].rearrange("p c n -> p (c n)"), ps[:, 4, 0:2 * P], ACT.Copy
                      ).then_inc(sem(f"over_hidden_t{l}"), 1)
                    act.wait_ge(*have(f"over_products{l}", 4 * j + 4))
                    A(y_sb[:, 0, 0:BANK], ps[:, 5, :], ACT.Copy).then_inc(sem(f"over_y{l}"), 1)
                    act.wait_ge(*have(f"over_stored{l}", 16 * j + 16))

        cross(0)
        experts(0)

        prep(first["c_v"] + 2)
        squares("mix1")
        split("mix1", "split_hi_mix1")
        d = first["c_v"]
        prep(d + 3)
        roots("mix1")
        factors_out("mix1", 1.0)
        act.wait_ge(*have("ws_t_in_psum", 1))
        copy_out("ws_t_ready", ws_t[:].rearrange("p g t -> p (g t)"), ps[:, 4:6, :].rearrange("p a b -> p (a b)"))
        prep(d + 4)
        used(d + 1)
        for i in range(TT):
            A(v_c[:, i, 0:BANK], ps[:, i, :], ACT.Gelu, scale=n_y[:, i:i + 1]).then_inc(sem("v_gelu"), 1)
        prep(d + 6)
        used(d + 3)
        for i in range(TT):
            A(v_c[:, i, BANK:], ps[:, 4 + i, :], ACT.Gelu, scale=n_y[:, i:i + 1]).then_inc(sem("v_gelu"), 1)
        act.wait_ge(*have("norm_var_v", 1))
        A(n_y[:], n_var[:], ACT.Sqrt).then_inc(sem("norm_root_v"), 1)
        prep(d + 8)
        act.wait_ge(*have("u_scaled", 1))
        A(u_c[:, 0:4, :], u_c[:, 0:4, :], ACT.Gelu).then_inc(sem("u_gelu"), 1)
        prep(d + 10)
        act.wait_ge(*have("u_scaled", 2))
        A(u_c[:, 4:8, :], u_c[:, 4:8, :], ACT.Gelu).then_inc(sem("u_gelu"), 1)
        for g in range(GM):
            act.wait_ge(*have("gated", g + 1))
            copy_out("gated_hi", a_hi[:, g, :], u_c[:, g, :])
        prep(first["xq1"] + 2)
        cross(1)
        experts(1)
        for i in range(TT):
            act.wait_ge(*have("combined1", 2 * i + 2))
            if i:
                act.wait_ge(*have("squares_act_fin", i))
            A(xn_tile(TT - 1), h[:, i, :], ACT.Square, accum_out=n_ss[:, i:i + 1]).then_inc(sem("squares_act_fin"), 1)
            if i % 2:
                half = slice(i - 1, i + 1)
                act.wait_ge(*have(f"norm_var_fin{i // 2}", 1))
                A(n_y[:, half], n_var[:, half], ACT.Sqrt).then_inc(sem(f"norm_root_fin{i // 2}"), 1)
            if i == 1:
                act.wait_ge(*have("fin_factors", 1))
                A(xn_tile(0), h[:, 0, :], ACT.Copy, scale=n_y[:, 0:1]).then_inc(sem("fin_scaled"), 1)

    @block.vector
    def _(dve):
        V = nc.vector
        own_sem = sem("dve_steps")
        n_own = [0]

        def own(ins):
            n_own[0] += 1
            ins.then_inc(own_sem, 1)
            dve.wait_ge(own_sem, n_own[0])

        def go(ins):
            n_own[0] += 1
            ins.then_inc(own_sem, 1)

        def sync():
            dve.wait_ge(own_sem, n_own[0])

        n_prep = [0]

        def lo_part(n, slot, _, hs, end=GC * BANK):
            dve.wait_ge(*have("w_hi_ready", n + 1))
            V.tensor_tensor(lo_at(slot)[:, 0:end], raw_at(slot)[:, 0:end],
                            w_hi[:, hs, 0:end].bitcast(fp32), ALU.subtract).then_inc(sem("w_lo_ready"), 1)

        def prep(upto):
            while n_prep[0] < upto:
                d = n_prep[0]
                n_prep[0] += 1
                lo_part(d, ring_pos[d], ring_count[d], d % SPLIT)

        def rstd(tag, n, var):
            dve.wait_ge(*have(f"norm_root_{tag}", 1))
            y, t = n_y[:, 0:n], n_t[:, 0:n]
            own(V.reciprocal(y, y))
            own(V.tensor_tensor(t, y, y, ALU.mult))
            own(V.scalar_tensor_tensor(out=t, in0=t, scalar=-0.5, in1=var, op0=ALU.mult, op1=ALU.mult))
            own(V.scalar_tensor_tensor(out=y, in0=t, scalar=1.5, in1=y, op0=ALU.add, op1=ALU.mult))

        def norm(tag):
            n, src, *_ = norm_parts(tag)
            for i in range(n if tag[:3] == "ffn" else n // 2, n):
                source_ready(dve, tag, i)
                own(V.scalar_tensor_tensor(out=xn[:, 1, :], in0=src(i), scalar=1.0, in1=src(i), op0=ALU.mult,
                                           op1=ALU.mult, accum_out=n_ss[:, i:i + 1]))
            dve.wait_ge(*have(f"squares_act_{tag}", n if tag[:3] == "ffn" else n // 2))
            V.tensor_scalar(n_var[:, 0:n], n_ss[:, 0:n], 1.0 / D, EPS, ALU.mult, ALU.add
                            ).then_inc(sem(f"norm_var_{tag}"), 1)
            rstd(tag, n, n_var[:, 0:n])

        def late_factors(tag):
            norm(tag)
            V.tensor_tensor(diag[:], ident[:].unsqueeze(1).to_broadcast([P, TT, P]),
                            n_y[:].unsqueeze(2).to_broadcast([P, TT, P]), ALU.mult
                            ).then_inc(sem(f"diag_ready_{tag}"), 1)

        def scaled(dst, s):
            return V.tensor_tensor(dst, ps[:, 4 * s:4 * s + 4, :],
                                   factors[:].unsqueeze(1).to_broadcast([P, 4, T]), ALU.mult)

        def norm_tiles(tag, tiles=None):
            n, src, *_ = norm_parts(tag)
            for i in tiles or range(n):
                if n == MT:
                    V.tensor_scalar(src(i), src(i), n_y[:, i:i + 1], None, ALU.mult).then_inc(sem(f"xn_{tag}"), 1)
                    continue
                V.tensor_scalar(xn_tile(i), src(i), n_y[:, i:i + 1], None, ALU.mult
                                ).then_inc(sem(f"xn_{tag}"), 1)

        def split(tag, hi_done, done):
            n, _, _, g0, hi, lo = norm_parts(tag)
            per = BANK // (n * P)
            b0 = 4 if n == MT else 0
            for k in range(KD):
                c0 = (k % per) * n * P
                dve.wait_ge(*have(hi_done, (k // per + 1) * per))
                V.scalar_tensor_tensor(out=lo[:, k, :], in0=ps[:, b0 + k // per, c0:c0 + n * P],
                                       scalar=vecs[:, g0 + k:g0 + k + 1], in1=hi[:, k, :].bitcast(fp32),
                                       op0=ALU.mult, op1=ALU.subtract).then_inc(sem(done), 1)

        def low(name, dst, src, hi):
            V.tensor_tensor(dst, src, hi.bitcast(fp32), ALU.subtract).then_inc(sem(name), 1)

        def residual(name, s, i):
            cut = slice(s * BANK, (s + 1) * BANK)
            V.tensor_tensor(h[:, i, cut], ps[:, 4 * s + i, :], h[:, i, cut], ALU.add).then_inc(sem(name), 1)

        dve.wait_ge(*have("router_consts", 1))
        V.tensor_copy(before[:], before_f[:]).then_inc(sem("router_rounded"), 1)
        V.tensor_copy(ones_r[:], ones[:]).then_inc(sem("router_rounded"), 1)
        dve.wait_ge(*have("vecs_in_psum", 2))
        V.tensor_copy(vecs[:], ps[:, 0, 0:NV]).then_inc(sem("vecs_ready"), 1)
        V.tensor_copy(taps[:].rearrange("p c t -> p (c t)"), ps[:, 1, 0:CC * TAPS]).then_inc(sem("vecs_ready"), 1)
        norm("mix0")
        norm_tiles("mix0")
        prep(2)
        split("mix0", "split_hi_mix0", "split_lo_mix0")
        prep(3)
        norm("mem0")
        norm_tiles("mem0")
        prep(5)
        dve.wait_ge(*have("router_loaded", 64 * NL))
        for l in range(NL):
            V.tensor_tensor(rt_w[:, l], rt_w[:, l],
                            vecs[:, FFN_G + l * KD:FFN_G + (l + 1) * KD].unsqueeze(2).to_broadcast([P, KD, NG + NE]),
                            ALU.mult).then_inc(sem("router_scaled"), 1)

        dve.wait_ge(*have("gate_done", 1))
        dve.wait_ge(*have("conv_padded", 1))
        dve.wait_ge(*have("w_used", first["sb_a"] + 2))
        V.tensor_tensor(conv_in[:, :, PAD:], ps[:, 4:8, :], conv_acc[:], ALU.mult).then_inc(sem("glu_done"), 1)
        dve.wait_ge(*have("glu_done", 1))

        tap = [0]

        def conv(n):
            for _ in range(n):
                j = tap[0]
                if j >= TAPS:
                    return
                tap[0] += 1
                for m in range(CC):
                    if j:
                        dve.wait_ge(*have("conv_taps", CC * (j - 1) + m + 1))
                        V.scalar_tensor_tensor(out=conv_acc[:, m, :], in0=conv_in[:, m, j:j + T],
                                               scalar=taps[:, m, j:j + 1], in1=conv_acc[:, m, :], op0=ALU.mult,
                                               op1=ALU.add).then_inc(sem("conv_taps"), 1)
                    else:
                        V.tensor_scalar(conv_acc[:, m, :], conv_in[:, m, 0:T], taps[:, m, 0:1],
                                        vecs[:, CONV_B + m:CONV_B + m + 1], ALU.mult, ALU.add
                                        ).then_inc(sem("conv_taps"), 1)

        prep(6)
        conv(3)
        for d in range(7, 11):
            prep(d)
            conv(4 if d < 10 else 3)
        split("mem0", "mem_split_hi0", "mem_split_lo0")
        for d in range(11, 19):
            prep(d)
            conv(1)
        conv(3)

        def z_part(hd):
            s = hd % 2
            dve.wait_ge(*have("z_in_psum", hd + 1))
            if hd >= 2:
                dve.wait_ge(*have("heads_in_psum", hd - 1))
                dve.wait_ge(*have("sums_in_psum", hd - 1))
            else:
                dve.wait_ge(*have("w_used", first["vx0"] + 4))
            V.tensor_tensor(zbuf[:, s, 0:512].rearrange("p (j q) -> p j q", j=TT),
                            ps[:, 4, :].rearrange("p (j q) -> p j q", j=TT),
                            causal[:].unsqueeze(1).to_broadcast([P, TT, P]), ALU.add).then_inc(sem("z_diag"), 1)
            dve.wait_ge(*have("z_diag", hd + 1))
            dve.wait_ge(*have("z_off", hd + 1))
            V.scalar_tensor_tensor(out=sbuf[:, s, :], in0=zbuf[:, s, :], scalar=-1.0, in1=zbuf[:, s, :],
                                   op0=ALU.mult, op1=ALU.min).then_inc(sem("minus_abs_z"), 1)

        def softplus(hd):
            s = hd % 2
            dve.wait_ge(*have("ln_done", hd + 1))
            V.scalar_tensor_tensor(out=sbuf[:, s, :], in0=zbuf[:, s, :], scalar=0.0, in1=sbuf[:, s, :], op0=ALU.max,
                                   op1=ALU.add).then_inc(sem("softplus"), 1)

        def log_w(hd):
            s = hd % 2
            dve.wait_ge(*have("sums_in_psum", hd + 1))
            V.tensor_tensor(zbuf[:, s, :], zbuf[:, s, :], ps[:, 0:3, :].rearrange("p k n -> p (k n)")[:, 0:ZW],
                            ALU.subtract).then_inc(sem("log_w"), 1)

        def heads_lo(pair):
            dve.wait_ge(*have("heads_hi", pair + 1))
            low("heads_lo", a_lo[:, CC + pair, :], ps[:, 3, :], a_hi[:, CC + pair, :])

        z_part(0)
        softplus(0)
        for hd in range(SB_HEADS):
            if hd + 1 < SB_HEADS:
                z_part(hd + 1)
            if hd in (2, 4, 6):
                heads_lo(hd // 2 - 1)
            conv(1)
            log_w(hd)
            if hd + 1 < SB_HEADS:
                softplus(hd + 1)
            conv(1)
            if hd in (4, 5, 7):
                prep({4: 19, 5: 20, 7: 21}[hd])
            if hd == 3:
                assert tap[0] == TAPS
                dve.wait_ge(*have("conv_mean", 1))
                V.scalar_tensor_tensor(out=conv_acc[:], in0=ps[:, 7, :].unsqueeze(1).to_broadcast([P, CC, T]),
                                       scalar=-1.0 / CH, in1=conv_acc[:], op0=ALU.mult, op1=ALU.add
                                       ).then_inc(sem("conv_centred"), 1)
            if hd == 5:
                dve.wait_ge(*have("conv_var", 1))
                V.tensor_scalar(conv_rs[:, 0, :], ps[:, 7, :], 1.0 / CH, EPS, ALU.mult, ALU.add
                                ).then_inc(sem("conv_var_ready"), 1)
            if hd == 6:
                dve.wait_ge(*have("conv_root", 2))
                own(V.tensor_tensor(conv_t[:], conv_rs[:, 1, :], conv_rs[:, 1, :], ALU.mult))
                own(V.scalar_tensor_tensor(out=conv_t[:], in0=conv_t[:], scalar=-0.5, in1=conv_rs[:, 0, :],
                                           op0=ALU.mult, op1=ALU.mult))
                own(V.scalar_tensor_tensor(out=conv_rs[:, 1, :], in0=conv_t[:], scalar=1.5, in1=conv_rs[:, 1, :],
                                           op0=ALU.add, op1=ALU.mult))
                V.tensor_tensor(conv_acc[:], conv_acc[:], conv_rs[:, 1, :].unsqueeze(1).to_broadcast([P, CC, T]),
                                ALU.mult).then_inc(sem("conv_normed"), 1)
        heads_lo(3)
        for m in range(CC):
            dve.wait_ge(*have("conv_hi", m + 1))
            low("conv_lo", a_lo[:, m, :], conv_sq[:, m, :], a_hi[:, m, :])

        def residual_stage(name, part_name, d):
            if name == "h_ffn0":
                prep(d + 2)
                norm("mem1")
                norm_tiles("mem1")
                prep(d + 3)
                split("mem1", "mem_split_hi1", "mem_split_lo1")
            prep(d + 3)
            dve.wait_ge(*have("w_used", d + 2))
            for i in range(TT):
                residual(part_name, 0, i)
            prep(d + 5)
            for i in range(TT):
                dve.wait_ge(*(have(f"tile_{name[2:]}", i + 1) if i < TT - 1 else have("w_used", d + 4)))
                residual(name, 1, i)
            if name != "h_ffn1":
                prep(d + 6)

        def cross(l):
            d = first[f"xq{l}"]
            split(f"xa{l}", f"split_hi_xa{l}", f"split_lo_xa{l}")
            late_factors(f"xa{l}")
            prep(d + 4)
            for s in range(2):
                dve.wait_ge(*have("w_used", d + 2 * s + 2))
                dve.wait_ge(*have(f"factors_ready_xa{l}", 1))
                scaled(xq[:, 4 * s:4 * s + 4, :], s).then_inc(sem(f"xq_ready{l}"), 1)
                if s == 0:
                    prep(d + 6)
            def max_of(hd):
                dve.wait_ge(*have(f"x_scores{l}", hd + 1))
                b = 2 * (hd % 2)
                V.tensor_reduce(out=x_max[:], in_=ps[:, b:b + 2, :].rearrange("p a (i m) -> p (a i) m", m=M),
                                axis=AX.X, op=ALU.max, negate=True).then_inc(sem(f"x_max{l}"), 1)

            max_of(0)
            for hd in range(XH + 1):
                if hd < XH:
                    dve.wait_ge(*have(f"x_exp{l}", TT * (hd + 1)))
                    own(V.reciprocal(x_rec[:], x_sum[:]))
                    V.tensor_tensor(xp[:, hd % 2], xp[:, hd % 2], x_rec[:].unsqueeze(2).to_broadcast([P, TT, M]),
                                    ALU.mult).then_inc(sem(f"x_probs{l}"), 1)
                if hd + 1 < XH:
                    max_of(hd + 1)
                if hd:
                    for c in range(2):
                        dve.wait_ge(*have(f"x_heads_hi{l}", 2 * hd - 1 + c))
                        low(f"x_heads_lo{l}", a_lo[:, 2 * hd - 2 + c, :], ps[:, 6 + c, :], a_hi[:, 2 * hd - 2 + c, :])

        def bc(ap, shape):
            return ap.to_broadcast(shape)

        def router(l):
            dve.wait_ge(*have(f"logits_t{l}", 1))
            small_bank = 4 if l == 0 else 0
            own(V.tensor_tensor(lg[:], ps[:, small_bank + 1, 0:TT * (NG + NE)].rearrange("p (i n) -> p i n", i=TT),
                                bc(n_y[:].unsqueeze(2), [P, TT, NG + NE]), ALU.mult))
            own(V.tensor_tensor(lg[:], lg[:], bc(rt_b[:, l, :].unsqueeze(1), [P, TT, NG + NE]), ALU.add))
            S4 = [P, TT, NG]
            S44 = [P, TT, NG, EPG]
            four = bc(iota4[:].unsqueeze(1), S4)

            def argmax(src, hot, top):
                own(V.tensor_reduce(out=top[:], in_=src, axis=AX.X, op=ALU.max))
                own(V.tensor_tensor(r4c[:], src, bc(top[:].unsqueeze(2), S4), ALU.is_equal))
                own(V.scalar_tensor_tensor(out=r4c[:], in0=r4c[:], scalar=-FAR, in1=four, op0=ALU.mult, op1=ALU.add))
                own(V.tensor_reduce(out=slot_f[:, 0:TT], in_=r4c[:], axis=AX.X, op=ALU.min))
                own(V.tensor_tensor(hot[:], r4c[:], bc(slot_f[:, 0:TT].unsqueeze(2), S4), ALU.is_equal))

            argmax(lg[:, :, 0:NG], oh_g, r1a)
            V.tensor_tensor(r4a[:], lg[:, :, 0:NG], bc(r1a[:].unsqueeze(2), S4), ALU.subtract
                            ).then_inc(sem(f"r_args{l}"), 1)
            experts4 = lg[:, :, NG:].rearrange("p i (g e) -> p i g e", g=NG)
            own(V.tensor_tensor(e_tmp[:], experts4, bc(oh_g[:].unsqueeze(3), S44), ALU.mult))
            own(V.tensor_reduce(out=le[:], in_=e_tmp[:].rearrange("p i g e -> p i e g"), axis=AX.X, op=ALU.add))
            argmax(le[:], oh_1, r1a)
            own(V.scalar_tensor_tensor(out=le[:], in0=oh_1[:], scalar=-1e30, in1=le[:], op0=ALU.mult, op1=ALU.add))
            argmax(le[:], oh_2, gate1)
            V.tensor_tensor(r1a[:], gate1[:], r1a[:], ALU.subtract).then_inc(sem(f"r_args{l}"), 1)
            own(V.tensor_tensor(e_1[:].rearrange("p i (g e) -> p i g e", g=NG), bc(oh_g[:].unsqueeze(3), S44),
                                bc(oh_1[:].unsqueeze(2), S44), ALU.mult))
            own(V.tensor_tensor(e_2[:].rearrange("p i (g e) -> p i g e", g=NG), bc(oh_g[:].unsqueeze(3), S44),
                                bc(oh_2[:].unsqueeze(2), S44), ALU.mult))
            V.tensor_tensor(e_sum[:], e_1[:], e_2[:], ALU.add).then_inc(sem(f"assigned{l}"), 1)
            own(V.memset(over_pad[:, 0:NE], 0.0))
            own(V.memset(scan[:, :, 0:NE], 0.0))
            if l == 0:
                prep(first["vx1"] + 2)
            dve.wait_ge(*have(f"ranks{l}", 1))
            go(V.tensor_copy(count[:], ps[:, small_bank, TT * NE:(TT + 1) * NE]))
            go(V.tensor_copy(rank[:], ps[:, small_bank, 0:TT * NE].rearrange("p (i e) -> p i e", i=TT)))
            sync()
            FULL = T // P - 1
            SE = [P, TT, NE]
            go(V.tensor_tensor(over_cmp[:], bc(count[:].unsqueeze(2), [P, NE, FULL]),
                               bc(slot_lo[:, 1:1 + FULL].unsqueeze(1), [P, NE, FULL]), ALU.is_gt))
            go(V.tensor_scalar(beyond[:], rank[:], P - 0.5, None, ALU.is_gt))
            go(V.tensor_tensor(slots[:], rank[:], bc(slot_lo[:].unsqueeze(1), SE), ALU.add))
            sync()
            over = over_pad[:, NE:]
            own(V.tensor_reduce(out=over, in_=over_cmp[:], axis=AX.X, op=ALU.add))
            cur, step = over_pad, 1
            while step < NE:
                into = scan[:, 0 if step in (1, 4) else 1]
                own(V.tensor_tensor(into[:, NE:], cur[:, NE:], cur[:, NE - step:2 * NE - step], ALU.add))
                cur, step = into, 2 * step
            incl = cur[:, NE:]
            own(V.tensor_tensor(b_hi[:], incl, over, ALU.subtract))
            own(V.scalar_tensor_tensor(out=b_hi[:], in0=b_hi[:], scalar=float(P), in1=slot_hi[:], op0=ALU.mult,
                                       op1=ALU.add))
            own(V.tensor_tensor(beyond[:], beyond[:], bc(b_hi[:].unsqueeze(1), SE), ALU.mult))
            own(V.tensor_tensor(slots[:], slots[:], beyond[:], ALU.add))
            go(V.tensor_tensor(rank[:], slots[:], e_1[:], ALU.mult))
            go(V.tensor_tensor(beyond[:], slots[:], e_2[:], ALU.mult))
            sync()
            go(V.tensor_reduce(out=slot_f[:, 0:TT], in_=rank[:], axis=AX.X, op=ALU.add))
            go(V.tensor_reduce(out=slot_f[:, TT:2 * TT], in_=beyond[:], axis=AX.X, op=ALU.add))
            sync()
            own(V.tensor_copy(slot_i[:], slot_f[:]))
            go(V.tensor_single_scalar(row_i[:], slot_i[:], P - 1, ALU.bitwise_and))
            go(V.tensor_single_scalar(blk_i[:], slot_i[:], 7, ALU.logical_shift_right))
            sync()
            go(V.tensor_copy(blk_f[:], blk_i[:]))
            go(V.tensor_copy(row_f[:], row_i[:]))
            sync()
            J = 2 * TT
            go(V.tensor_tensor(blk_hot[:], bc(iota_b[:].unsqueeze(1), [P, J, NB]), bc(blk_f[:].unsqueeze(2), [P, J, NB]),
                               ALU.is_equal))
            V.tensor_tensor(slot_hot[:], bc(iota_p[:].unsqueeze(1), [P, J, P]), bc(row_f[:].unsqueeze(2), [P, J, P]),
                            ALU.is_equal).then_inc(sem(f"hots{l}"), 1)
            sync()
            V.tensor_tensor(tok_hot[:].rearrange("p (c i) b -> p c i b", c=2),
                            blk_hot[:].rearrange("p (c i) b -> p c i b", c=2),
                            bc(tok_no[:].unsqueeze(1).unsqueeze(3), [P, 2, TT, NB]), ALU.mult
                            ).then_inc(sem(f"hots{l}"), 1)
            own(V.tensor_tensor(own_cmp[:], bc(incl.unsqueeze(1), [P, OVERFLOW, NE]),
                                bc(iota_b[:, 0:OVERFLOW].unsqueeze(2), [P, OVERFLOW, NE]), ALU.is_le))
            own(V.tensor_reduce(out=own_f[:], in_=own_cmp[:], axis=AX.X, op=ALU.add))
            own(V.tensor_scalar(own_f[:], own_f[:], float(NE - 1), None, ALU.min))
            own(V.tensor_copy(own_i[:], own_f[:]))
            V.tensor_copy(nov_i[:], incl[:, NE - 1:NE]).then_inc(sem(f"overflow_known{l}"), 1)
            dve.wait_ge(*have(f"table{l}", 1))
            own(V.tensor_copy(tok_f[:], ps[:, small_bank + 1, 0:NB]))
            own(V.tensor_scalar(tok_e[:], tok_f[:], 0.0, FAR, ALU.is_equal, ALU.mult))
            own(V.scalar_tensor_tensor(out=tok_f[:], in0=tok_f[:], scalar=-1.0, in1=tok_e[:], op0=ALU.add,
                                       op1=ALU.add))
            V.tensor_copy(tok_i[:], tok_f[:]).then_inc(sem(f"table_ready{l}"), 1)
            dve.wait_ge(*have(f"r_exp{l}", 2))
            own(V.tensor_reduce(out=p_top[:], in_=r4b[:], axis=AX.X, op=ALU.add))
            own(V.reciprocal(p_top[:], p_top[:]))
            own(V.tensor_scalar(r1a[:], r1b[:], 1.0, None, ALU.add))
            own(V.reciprocal(r1a[:], r1a[:]))
            own(V.tensor_tensor(gate1[:], r1a[:], p_top[:], ALU.mult))
            own(V.tensor_tensor(gate2[:], gate1[:], r1b[:], ALU.mult))

        def experts(l):
            if l == 0:
                prep(first["kx1"] + 3)
            for i in (1, 3):
                b0 = (4 * (l == 0) + 2 * i) % 8
                dve.wait_ge(*have(f"xn_t_in_psum_ffn{l}", i + 1))
                V.tensor_copy(a_full[:, :, i * P:(i + 1) * P],
                              ps[:, b0:b0 + 2, :].rearrange("p a (b n) -> p (a b) n", n=P)
                              ).then_inc(sem(f"a_odd{l}"), 1)
                if i == 1:
                    norm(f"ffn{l}")
                    norm_tiles(f"ffn{l}", [0, 1])
            norm_tiles(f"ffn{l}", [2, 3])
            if l == 0:
                prep(first["kx1"] + 4)
            router(l)
            prep(first[f"moe{l}"] + 2)

            def rows_lo(e, b):
                dve.wait_ge(*have(f"xs_hi{l}", b + 1))
                V.tensor_tensor(xs_lo[:, e].rearrange("p k n -> p (k n)"), ps[:, 0:2, :].rearrange("p a n -> p (a n)"),
                                xs_hi[:, e].rearrange("p k n -> p (k n)").bitcast(fp32), ALU.subtract
                                ).then_inc(sem(f"xs_lo{l}"), 1)

            def hidden_lo(e, b):
                dve.wait_ge(*have(f"hidden_hi{l}", b + 1))
                V.tensor_tensor(hid_lo[:, e].rearrange("p c n -> p (c n)"), ps[:, 4, 0:2 * P],
                                hid_hi[:, e].rearrange("p c n -> p (c n)").bitcast(fp32), ALU.subtract
                                ).then_inc(sem(f"hidden_lo{l}"), 1)

            def y_right(e, n):
                dve.wait_ge(*have("w_used", n + 1))
                V.tensor_copy(y_sb[:, e, BANK:], ps[:, 6, :]).then_inc(sem(f"y_right{l}"), 1)

            def block_of(i, e, first_pair, last_pair):
                b = 2 * i + e
                last_block = last_pair and e == 1
                if not last_block:
                    rows_lo(1 - e, b + 1)
                if not (first_pair and e == 0):
                    hidden_lo(1 - e, b - 1)
                lo_part(*entry(l, 3 * e + 2, i), end=GC * BANK // 2 if last_block else GC * BANK)
                dve.wait_ge(*have(f"silu{l}", b + 1))
                V.tensor_tensor(hid[:, e, :], ps[:, 2 + e, FE:2 * FE], silu_g[:, e, :], ALU.mult
                                ).then_inc(sem(f"hidden{l}"), 1)
                if not last_block:
                    lo_part(*entry(l, 3 * e + 3, i))
                if not (first_pair and e == 0):
                    if not first_pair:
                        dve.wait_ge(*have(f"y_stored{l}_{e}", 16 * i))
                    y_right(1 - e, entry(l, 3 * e + 1, i)[0])
                if not last_block:
                    lo_part(*entry(l, 3 * e + 4, i), end=GC * BANK // 2)

            rows_lo(0, 0)
            for e in range(2):
                block_of(0, e, True, False)
            with dve.Fori(1, MORE) as i:
                for e in range(2):
                    block_of(i, e, False, False)
            for i in range(MORE, NE // 2):
                for e in range(2):
                    block_of(i, e, False, i == NE // 2 - 1)
            hidden_lo(1, NE - 1)
            n_prep[0] += 3 * NE - 2
            if l == 0:
                prep(first["vx1_more"] + 1)
            y_right(1, first[f"moe{l}"] + 3 * NE - 1)
            if l == 0:
                prep(first["vx1_more"] + 2)

            dve.wait_ge(*have(f"y_stored{l}_1", 16 * (NE // 2)))
            n_over = dve.value_load(nov_i[0:1, 0:1])
            with dve.If(n_over > 0):
                with dve.Fori(0, OVERFLOW) as j:
                    V.tensor_copy(idx_c[:], tok_i[:, bass.ds(j + NE, 1)]).then_inc(sem(f"over_index{l}"), 1)
                    dve.wait_ge(*have(f"over_products{l}", 4 * j + 1))
                    V.tensor_copy(xs_full[:].rearrange("p k n -> p (k n)"), ps[:, 0:2, :].rearrange("p a n -> p (a n)")
                                  ).then_inc(sem(f"over_x_t{l}"), 1)
                    dve.wait_ge(*have(f"over_silu{l}", j + 1))
                    V.tensor_tensor(hid[:, 0, :], ps[:, 2, FE:2 * FE], silu_g[:, 0, :], ALU.mult
                                    ).then_inc(sem(f"over_hidden{l}"), 1)
                    dve.wait_ge(*have(f"over_products{l}", 4 * j + 4))
                    V.tensor_copy(y_sb[:, 0, BANK:], ps[:, 6, :]).then_inc(sem(f"over_y{l}"), 1)
                    dve.wait_ge(*have(f"over_stored{l}", 16 * j + 16))

            for j in range(2 * TT):
                i, c = j // 2, j % 2
                if l == 0 and j == 0:
                    prep(first["c_v"] + 1)
                dve.wait_ge(*have(f"y_gathered{l}_{j % 4}", 16 * (j // 4 + 1)))
                if c:
                    dve.wait_ge(*have(f"combined{l}", j))
                V.scalar_tensor_tensor(out=h[:, i, :], in0=y_back[:, j % 4, :],
                                       scalar=(gate2 if c else gate1)[:, i:i + 1], in1=h[:, i, :],
                                       op0=ALU.mult, op1=ALU.add).then_inc(sem(f"combined{l}"), 1)
                if l == NL - 1 and j == 4:
                    final_var(0)
                if l == NL - 1 and j == 5:
                    final_factors(0)

        def final_var(part):
            half = slice(2 * part, 2 * part + 2)
            dve.wait_ge(*have("squares_act_fin", 2 * part + 2))
            V.tensor_scalar(n_var[:, half], n_ss[:, half], 1.0 / D, EPS, ALU.mult, ALU.add
                            ).then_inc(sem(f"norm_var_fin{part}"), 1)

        def final_factors(part):
            half = slice(2 * part, 2 * part + 2)
            dve.wait_ge(*have(f"norm_root_fin{part}", 1))
            y, t = n_y[:, half], n_t[:, half]
            own(V.reciprocal(y, y))
            own(V.tensor_tensor(t, y, y, ALU.mult))
            own(V.scalar_tensor_tensor(out=t, in0=t, scalar=-0.5, in1=n_var[:, half], op0=ALU.mult, op1=ALU.mult))
            last = V.scalar_tensor_tensor(out=y, in0=t, scalar=1.5, in1=y, op0=ALU.add, op1=ALU.mult)
            if part == 0:
                last.then_inc(sem("fin_factors"), 1)
            else:
                own(last)

        def final_out(tiles):
            for i in tiles:
                V.scalar_tensor_tensor(out=xn_tile(i), in0=h[:, i, :], scalar=n_y[:, i:i + 1], in1=fg_b[:],
                                       op0=ALU.mult, op1=ALU.mult).then_inc(sem("out_ready"), 1)

        residual_stage("h_xa0", "h_part_xa0", first["mix_out0"])
        cross(0)
        residual_stage("h_ffn0", "h_part_ffn0", first["xo0"])
        experts(0)

        split("mix1", "split_hi_mix1", "split_lo_mix1")
        prep(first["c_v"] + 2)
        late_factors("mix1")
        d = first["c_v"]
        prep(d + 6)
        for s in range(2):
            for i in range(TT):
                dve.wait_ge(*have("v_gelu", TT * s + i + 1))
                V.bn_stats(v_st[:, i, s, :], v_c[:, i, s * BANK:(s + 1) * BANK]).then_inc(sem("v_stats"), 1)
        for i in range(TT):
            dve.wait_ge(*have("v_stats", TT + i + 1))
            own(V.bn_aggr(v_mv[:, i, :], v_st[:, i].rearrange("p a b -> p (a b)")))
        V.tensor_scalar(n_var[:], v_mv[:, :, 1], EPS, None, ALU.add).then_inc(sem("norm_var_v"), 1)
        dve.wait_ge(*have("norm_var_v", 1))
        rstd("v", TT, n_var[:])
        prep(d + 7)
        dve.wait_ge(*have("vnorm_loaded", 32))
        for i in range(TT):
            V.tensor_scalar(v_c[:, i, :], v_c[:, i, :], v_mv[:, i, 0:1], n_y[:, i:i + 1], ALU.subtract, ALU.mult
                            ).then_inc(sem("v_centred"), 1)
        for i in range(TT):
            dve.wait_ge(*have("v_centred", i + 1))
            V.tensor_tensor(v_c[:, i, :], v_c[:, i, :], vg_b[:], ALU.mult).then_inc(sem("v_gained"), 1)
        prep(d + 8)
        for i in range(TT):
            dve.wait_ge(*have("v_gained", i + 1))
            V.tensor_tensor(v_c[:, i, :], v_c[:, i, :], vb_b[:], ALU.add).then_inc(sem("v_normed"), 1)
        for s in range(2):
            dve.wait_ge(*have("w_used", d + 6 + 2 * s))
            scaled(u_c[:, 4 * s:4 * s + 4, :], s).then_inc(sem("u_scaled"), 1)
            prep(d + 9 + s)
        dve.wait_ge(*have("bs_loaded", 16))
        for g in range(GM):
            dve.wait_ge(*have("mixed_in_psum", g + 1))
            dve.wait_ge(*have("u_gelu", g // 4 + 1))
            m3 = ps[:, g, :].rearrange("p (c t) -> p c t", c=TT)
            own(V.tensor_tensor(m3, m3, bs_b[:, g, :].unsqueeze(1).to_broadcast([P, TT, P]), ALU.add))
            V.tensor_tensor(u_c[:, g, :], ps[:, g, :], u_c[:, g, :], ALU.mult).then_inc(sem("gated"), 1)
        residual_stage("h_xa1", "h_part_xa1", first["mix_out1"])
        cross(1)
        residual_stage("h_ffn1", "h_part_ffn1", first["xo1"])
        experts(1)
        dve.wait_ge(*have("final_gain_loaded", 16))
        dve.wait_ge(*have("fin_factors", 1))
        final_out([1])
        final_var(1)
        final_factors(1)
        final_out([2, 3])

    ctx.close()


_INS = ["x", "mem", "mem_norm_g", "norm_mix", "norm_xa", "norm_ffn", "final_norm_g",
        "ab_w_in", "ab_conv_w", "ab_conv_b", "ab_cnorm_g", "ab_cnorm_b", "ab_w_out",
        "c_w_in", "c_vnorm_g", "c_vnorm_b", "c_ws", "c_bs", "c_w_out",
        "xa_wq", "xa_wk", "xa_wv", "xa_wo", "rt_wg", "rt_bg", "rt_we", "rt_be",
        "ex_w_gate", "ex_w_up", "ex_w_down"]


def kernel(**inputs):
    import numpy as _np
    import concourse.bacc as _bacc
    from concourse import mybir as _mybir
    from concourse.bass_utils import run_bass_kernel_spmd as _run

    nc = _bacc.Bacc("TRN2", target_bir_lowering=False, num_devices=1)
    arrays, args = {}, []
    for name in _INS:
        a = _np.ascontiguousarray(inputs[name])
        arrays[f"in_{name}"] = a
        args.append(nc.dram_tensor(f"in_{name}", a.shape, _mybir.dt.from_np(a.dtype), kind="ExternalInput").ap())
    shape = tuple(inputs["x"].shape)
    args.append(nc.dram_tensor("out_0", shape, _mybir.dt.float32, kind="ExternalOutput").ap())
    trunk_program(nc, *args)
    return _run(nc, [arrays], core_ids=[0]).results[0]["out_0"]
```
